# Optimizing a Trainium2 kernel written in Bass

```python
import math
import jax, jax.numpy as jnp
from jax import lax
import numpy as np

D_MODEL = 1024
BATCH = 1
SEQ = 1024
DEPTH = 2

GRID_W = 64
CTX_LEN = 256
N_EVEN = (DEPTH + 1) // 2
N_ODD = DEPTH // 2
EPS = 1e-6

CHUNK = 128
A_WIDTH = D_MODEL // 2
A_GROUPS = 4
A_GROUP_W = A_WIDTH // A_GROUPS
B_WIDTH = D_MODEL // 2
B_CH = 16
B_GROUPS = B_WIDTH // B_CH
B_STATE = 64
EVEN_IN = 3 * A_WIDTH + 2 * B_WIDTH
EVEN_MIX = A_WIDTH + B_WIDTH
HEAD_DIM = 128
N_Q = D_MODEL // HEAD_DIM
N_KV = 2
Q_PER_KV = N_Q // N_KV
C_WIDTH = N_Q * HEAD_DIM
KV_WIDTH = N_KV * HEAD_DIM
ODD_IN = 2 * C_WIDTH + 2 * KV_WIDTH
Q_BLOCK = 128
ROPE_THETA = 10000.0
ROPE_PAIRS = HEAD_DIM // 4

kernel_name = "hybrid_gmlp_s5_gqa_prefix_trunk"

def _rms_norm(x, g):
    xf = x.astype(jnp.float32)
    y = xf * lax.rsqrt(jnp.mean(xf * xf, axis=-1, keepdims=True) + EPS)
    return (y * g.astype(jnp.float32)).astype(x.dtype)

def _layer_norm(x, g):
    xf = x.astype(jnp.float32)
    mu = jnp.mean(xf, axis=-1, keepdims=True)
    xc = xf - mu
    var = jnp.mean(xc * xc, axis=-1, keepdims=True)
    return (xc * lax.rsqrt(var + EPS) * g.astype(jnp.float32)).astype(x.dtype)

def _ada(cond, w, b):
    m = jax.nn.silu(cond) @ w + b
    return jnp.split(m, 3, axis=-1)

def _prologue(x, ctx, c, c_ctx, g, w_mod, b_mod):
    sh, sc, gt = _ada(c, w_mod, b_mod)
    shc, scc, gtc = _ada(c_ctx, w_mod, b_mod)
    hx = _rms_norm(x, g) * (1 + sc[:, None]) + sh[:, None]
    hc = _rms_norm(ctx, g) * (1 + scc) + shc
    h = jnp.concatenate([hc, hx], axis=1)
    return h, gt[:, None], gtc

def _chunk_gmlp(u, v, v_g, w_s, b_s):
    Bn, L, _ = v.shape
    v = _layer_norm(v, v_g)
    vc = v.reshape(Bn, L // CHUNK, CHUNK, A_GROUPS, A_GROUP_W)
    mixed = jnp.einsum('gpq,bnqgc->bnpgc', w_s, vc) + b_s.T[None, None, :, :, None]
    return u * mixed.reshape(Bn, L, A_WIDTH)

def _s5_discretize(lam_re, lam_im, log_dt, b_re, b_im):
    lam_re = lam_re.astype(jnp.float32)
    lam_im = lam_im.astype(jnp.float32)
    dt = jnp.exp(log_dt.astype(jnp.float32))[:, None]
    mag = jnp.exp(lam_re * dt)
    lb_re = mag * jnp.cos(lam_im * dt)
    lb_im = mag * jnp.sin(lam_im * dt)
    den = lam_re * lam_re + lam_im * lam_im
    n_re, n_im = lb_re - 1.0, lb_im
    f_re = (n_re * lam_re + n_im * lam_im) / den
    f_im = (n_im * lam_re - n_re * lam_im) / den
    b_re = b_re.astype(jnp.float32)
    b_im = b_im.astype(jnp.float32)
    bb_re = f_re[..., None] * b_re - f_im[..., None] * b_im
    bb_im = f_re[..., None] * b_im + f_im[..., None] * b_re
    return lb_re, lb_im, bb_re, bb_im

def _ssm_combine(e1, e2):
    a1r, a1i, b1r, b1i = e1
    a2r, a2i, b2r, b2i = e2
    return (a1r * a2r - a1i * a2i,
            a1r * a2i + a1i * a2r,
            a2r * b1r - a2i * b1i + b2r,
            a2r * b1i + a2i * b1r + b2i)

def _s5_direction(seq, lam_re, lam_im, log_dt, b_re, b_im, c_re, c_im):
    Bn, L, W = seq.shape
    lb_re, lb_im, bb_re, bb_im = _s5_discretize(lam_re, lam_im, log_dt, b_re, b_im)
    u = seq.reshape(Bn, L, B_GROUPS, B_CH)
    bu_re = jnp.einsum('blgh,gph->blgp', u, bb_re)
    bu_im = jnp.einsum('blgh,gph->blgp', u, bb_im)
    a_re = jnp.broadcast_to(lb_re, (1, L, B_GROUPS, B_STATE))
    a_im = jnp.broadcast_to(lb_im, (1, L, B_GROUPS, B_STATE))
    _, _, h_re, h_im = lax.associative_scan(_ssm_combine, (a_re, a_im, bu_re, bu_im), axis=1)
    y = (jnp.einsum('blgp,ghp->blgh', h_re, c_re.astype(jnp.float32))
         - jnp.einsum('blgp,ghp->blgh', h_im, c_im.astype(jnp.float32)))
    return y.reshape(Bn, L, W)

def _s5_bidir(xs, n_ctx, lam_re, lam_im, log_dt, b_re, b_im, c_re, c_im, d_skip, w_glu, b_glu):
    dtype = xs.dtype
    xf = xs.astype(jnp.float32)
    x_ctx, x_lat = xf[:, :n_ctx], xf[:, n_ctx:]
    fwd = _s5_direction(xf, lam_re[0], lam_im[0], log_dt[0], b_re[0], b_im[0], c_re[0], c_im[0])
    bwd_seq = jnp.concatenate([x_ctx[:, ::-1], x_lat[:, ::-1]], axis=1)
    bwd = _s5_direction(bwd_seq, lam_re[1], lam_im[1], log_dt[1], b_re[1], b_im[1], c_re[1], c_im[1])
    bwd = jnp.concatenate([bwd[:, :n_ctx][:, ::-1], bwd[:, n_ctx:][:, ::-1]], axis=1)
    y = fwd + bwd + d_skip.astype(jnp.float32) * xf
    y = jax.nn.gelu(y)
    y = y * jax.nn.sigmoid(y @ w_glu.astype(jnp.float32) + b_glu.astype(jnp.float32))
    return y.astype(dtype)

def _axial_rope(n_lat):
    rows = n_lat // GRID_W
    row = jnp.repeat(jnp.arange(rows), GRID_W)
    col = jnp.tile(jnp.arange(GRID_W), rows)
    freqs = ROPE_THETA ** (-jnp.arange(ROPE_PAIRS, dtype=jnp.float32) / ROPE_PAIRS)
    ang = jnp.stack([row[:, None] * freqs, col[:, None] * freqs], axis=1)
    return jnp.cos(ang), jnp.sin(ang)

def _apply_rope(x, cos, sin):
    lead = x.shape[:-1]
    xs = x.reshape(lead + (2, 2, ROPE_PAIRS)).astype(jnp.float32)
    bshape = (1, x.shape[1]) + (1,) * (x.ndim - 3) + (2, ROPE_PAIRS)
    cos = cos.reshape(bshape)
    sin = sin.reshape(bshape)
    x1, x2 = xs[..., 0, :], xs[..., 1, :]
    out = jnp.stack([x1 * cos - x2 * sin, x1 * sin + x2 * cos], axis=-2)
    return out.reshape(x.shape).astype(x.dtype)

def _attend(q, k, v):
    s = jnp.einsum('btkgd,bskd->bkgts', q, k).astype(jnp.float32) * (HEAD_DIM ** -0.5)
    p = jax.nn.softmax(s, axis=-1).astype(v.dtype)
    return jnp.einsum('bkgts,bskd->btkgd', p, v)

def _even_layer(x, ctx, c, c_ctx, norm_g, w_mod, b_mod, w_in, w_out, gm_v_g, gm_w_s, gm_b_s,
                lam_re, lam_im, log_dt, b_re, b_im, c_re, c_im, d_skip, w_glu, b_glu, update_ctx):
    n_ctx = ctx.shape[1]
    h, gt, gtc = _prologue(x, ctx, c, c_ctx, norm_g, w_mod, b_mod)
    u, v, g_a, xs, g_b = jnp.split(
        h @ w_in, [A_WIDTH, 2 * A_WIDTH, 3 * A_WIDTH, 3 * A_WIDTH + B_WIDTH], axis=-1)
    y_a = jnp.concatenate([
        _chunk_gmlp(u[:, :n_ctx], v[:, :n_ctx], gm_v_g, gm_w_s, gm_b_s),
        _chunk_gmlp(u[:, n_ctx:], v[:, n_ctx:], gm_v_g, gm_w_s, gm_b_s)], axis=1)
    y_a = y_a * jax.nn.silu(g_a)
    y_b = _s5_bidir(xs, n_ctx, lam_re, lam_im, log_dt, b_re, b_im, c_re, c_im, d_skip, w_glu, b_glu)
    y_b = y_b * jax.nn.silu(g_b)
    mix = jnp.concatenate([y_a, y_b], axis=-1)
    x = x + gt * (mix[:, n_ctx:] @ w_out)
    if update_ctx:
        ctx = ctx + gtc * (mix[:, :n_ctx] @ w_out)
    return x, ctx

def _odd_layer(x, ctx, c, c_ctx, norm_g, w_mod, b_mod, w_in, w_out, q_g, k_g, update_ctx):
    n_ctx = ctx.shape[1]
    Bn, L, _ = x.shape
    n_tot = n_ctx + L
    h, gt, gtc = _prologue(x, ctx, c, c_ctx, norm_g, w_mod, b_mod)
    q, k, v, gate = jnp.split(h @ w_in, [C_WIDTH, C_WIDTH + KV_WIDTH, C_WIDTH + 2 * KV_WIDTH], axis=-1)
    q = _rms_norm(q.reshape(Bn, n_tot, N_KV, Q_PER_KV, HEAD_DIM), q_g)
    k = _rms_norm(k.reshape(Bn, n_tot, N_KV, HEAD_DIM), k_g)
    v = v.reshape(Bn, n_tot, N_KV, HEAD_DIM)
    cos, sin = _axial_rope(L)
    q_lat = _apply_rope(q[:, n_ctx:], cos, sin)
    k_all = jnp.concatenate([k[:, :n_ctx], _apply_rope(k[:, n_ctx:], cos, sin)], axis=1)
    nb = L // Q_BLOCK
    qb = jnp.moveaxis(q_lat.reshape(Bn, nb, Q_BLOCK, N_KV, Q_PER_KV, HEAD_DIM), 1, 0)
    o = lax.map(lambda qi: _attend(qi, k_all, v), qb)
    o_lat = jnp.moveaxis(o, 0, 1).reshape(Bn, L, C_WIDTH)
    x = x + gt * ((o_lat * jax.nn.silu(gate[:, n_ctx:])) @ w_out)
    if update_ctx:
        o_ctx = _attend(q[:, :n_ctx], k[:, :n_ctx], v[:, :n_ctx]).reshape(Bn, n_ctx, C_WIDTH)
        ctx = ctx + gtc * ((o_ctx * jax.nn.silu(gate[:, :n_ctx])) @ w_out)
    return x, ctx

def setup_inputs(seed: int = 0) -> dict:
    key = jax.random.key(seed)
    ks = iter(jax.random.split(key, 40))
    f32 = jnp.float32
    nrm = lambda shape, s=1.0: jax.random.normal(next(ks), shape, f32) * s
    lam_re = -0.5 + nrm((N_EVEN, 2, B_GROUPS, B_STATE), 0.01)
    lam_im = (jnp.pi * jnp.arange(B_STATE, dtype=f32)) + nrm((N_EVEN, 2, B_GROUPS, B_STATE), 0.01)
    return {
        "x": nrm((BATCH, SEQ, D_MODEL)),
        "c": nrm((BATCH, D_MODEL)),
        "ctx": nrm((BATCH, CTX_LEN, D_MODEL)),
        "c_ctx": nrm((D_MODEL,)),
        "norm_g": 1.0 + nrm((DEPTH, D_MODEL), 0.02),
        "w_mod": nrm((DEPTH, D_MODEL, 3 * D_MODEL), 0.5 * D_MODEL ** -0.5),
        "b_mod": nrm((DEPTH, 3 * D_MODEL), 0.02),
        "we_in": nrm((N_EVEN, D_MODEL, EVEN_IN), D_MODEL ** -0.5),
        "we_out": nrm((N_EVEN, EVEN_MIX, D_MODEL), EVEN_MIX ** -0.5),
        "gm_v_g": 1.0 + nrm((N_EVEN, A_WIDTH), 0.02),
        "gm_w_s": nrm((N_EVEN, A_GROUPS, CHUNK, CHUNK), CHUNK ** -0.5),
        "gm_b_s": 1.0 + nrm((N_EVEN, A_GROUPS, CHUNK), 0.1),
        "s5_lam_re": lam_re,
        "s5_lam_im": lam_im,
        "s5_log_dt": jax.random.uniform(next(ks), (N_EVEN, 2, B_GROUPS), f32,
                                        minval=math.log(1e-3), maxval=math.log(1e-1)),
        "s5_b_re": nrm((N_EVEN, 2, B_GROUPS, B_STATE, B_CH), (2 * B_CH) ** -0.5),
        "s5_b_im": nrm((N_EVEN, 2, B_GROUPS, B_STATE, B_CH), (2 * B_CH) ** -0.5),
        "s5_c_re": nrm((N_EVEN, 2, B_GROUPS, B_CH, B_STATE), B_STATE ** -0.5),
        "s5_c_im": nrm((N_EVEN, 2, B_GROUPS, B_CH, B_STATE), B_STATE ** -0.5),
        "s5_d": nrm((N_EVEN, B_WIDTH)),
        "s5_w_glu": nrm((N_EVEN, B_WIDTH, B_WIDTH), B_WIDTH ** -0.5),
        "s5_b_glu": nrm((N_EVEN, B_WIDTH), 0.02),
        "wo_in": nrm((N_ODD, D_MODEL, ODD_IN), D_MODEL ** -0.5),
        "wo_out": nrm((N_ODD, C_WIDTH, D_MODEL), C_WIDTH ** -0.5),
        "q_norm_g": 1.0 + nrm((N_ODD, HEAD_DIM), 0.02),
        "k_norm_g": 1.0 + nrm((N_ODD, HEAD_DIM), 0.02),
        "final_g": 1.0 + nrm((D_MODEL,), 0.02),
    }

def reference(x, c, ctx, c_ctx, norm_g, w_mod, b_mod, we_in, we_out, gm_v_g, gm_w_s, gm_b_s,
              s5_lam_re, s5_lam_im, s5_log_dt, s5_b_re, s5_b_im, s5_c_re, s5_c_im, s5_d,
              s5_w_glu, s5_b_glu, wo_in, wo_out, q_norm_g, k_norm_g, final_g):
    for layer in range(DEPTH):
        update_ctx = layer < DEPTH - 1
        i = layer // 2
        if layer % 2 == 0:
            x, ctx = _even_layer(x, ctx, c, c_ctx, norm_g[layer], w_mod[layer], b_mod[layer],
                                 we_in[i], we_out[i], gm_v_g[i], gm_w_s[i], gm_b_s[i],
                                 s5_lam_re[i], s5_lam_im[i], s5_log_dt[i], s5_b_re[i], s5_b_im[i],
                                 s5_c_re[i], s5_c_im[i], s5_d[i], s5_w_glu[i], s5_b_glu[i], update_ctx)
        else:
            x, ctx = _odd_layer(x, ctx, c, c_ctx, norm_g[layer], w_mod[layer], b_mod[layer],
                                wo_in[i], wo_out[i], q_norm_g[i], k_norm_g[i], update_ctx)
    return _rms_norm(x, final_g)


_drawn_inputs = setup_inputs


def setup_inputs(seed=0):
    import zlib

    import numpy as np

    out = dict(_drawn_inputs(seed))
    spreads = {}
    factors = {'ctx': 8.0,
     'c_ctx': 4.807,
     'norm_g': 8.0,
     'b_mod': 3.357,
     'gm_v_g': 8.0,
     'gm_b_s': 4.238,
     's5_lam_re': 64.0,
     's5_lam_im': 61.904,
     's5_log_dt': 64.0,
     's5_b_re': 64.0,
     's5_b_im': 64.0,
     's5_c_re': 64.0,
     's5_c_im': 64.0,
     's5_w_glu': 3.837,
     's5_b_glu': 200.0,
     'q_norm_g': 8.0,
     'k_norm_g': 8.0,
     'final_g': 23.201}
    for name, (base, spread) in spreads.items():
        noise = np.random.default_rng([zlib.crc32(name.encode()), seed]).standard_normal(out[name].shape)
        drawn = base * np.exp(spread * noise) if base else spread * noise
        out[name] = __import__('jax').numpy.asarray(drawn.astype(out[name].dtype))
    for name, factor in factors.items():
        out[name] = (out[name] * factor).astype(out[name].dtype)
    return out
```

```python
import math
from contextlib import ExitStack

import numpy as np

from concourse import mybir

F32 = mybir.dt.float32
I32 = mybir.dt.int32
ACT = mybir.ActivationFunctionType
ALU = mybir.AluOpType
AX = mybir.AxisListType

P = 128
D = 1024
KT = D // P
NCTX, SEQ = 256, 1024
TOK = NCTX + SEQ
CT, LT = NCTX // P, SEQ // P
TT = CT + LT
EPS = 1e-6
W = 512
FB = W // P
CH = 8
G = 32
HC = 16
NS = 64
NCH = TOK // CH
CCH = NCTX // CH
HD = 128
NH = 8
NKV = 2
HPK = NH // NKV
SLOT = 4096
NSLOT = 3
CHUNKS = [(0, 256), (256, 512), (768, 512)]
LN2_HI, LN2_LO = 0.693359375, -2.12194440e-4
PIO2 = (1.5703125, 4.83751296997e-4, 7.54978995489e-8)


def build(nc, x, c, ctx_in, c_ctx, norm_g, w_mod, b_mod, we_in, we_out, gm_v_g, gm_w_s, gm_b_s,
          s5_lam_re, s5_lam_im, s5_log_dt, s5_b_re, s5_b_im, s5_c_re, s5_c_im, s5_d,
          s5_w_glu, s5_b_glu, wo_in, wo_out, q_norm_g, k_norm_g, final_g,
          ident_in, cos_in, sin_in, out):
    with ExitStack() as es:
        def sb(name, n, dt=F32):
            return es.enter_context(nc.sbuf_tensor(name, [P, n], dt))

        def sem(name):
            return es.enter_context(nc.semaphore(name))

        bop_d = nc.dram_tensor("bop_scratch", (2, P, 2, 16, P), F32, kind="Internal").ap()
        ct_d = nc.dram_tensor("cop_t_scratch", (4, P, 3, 8, P), F32, kind="Internal").ap()
        x1_d = nc.dram_tensor("x1_scratch", (SEQ, D), F32, kind="Internal").ap()

        RA = sb("region_a", 10240)
        RB = sb("region_b", 10240)
        RC = sb("region_c", 10240)
        RD = sb("region_d", (NCH + 1) * 2 * G)
        ring = sb("weight_ring", NSLOT * SLOT)
        shared = sb("shared", 3072)
        ident = sb("ident", P)
        small = sb("small", 336)
        L8 = sb("lam8", P)
        rt = sb("rec_tmp", P)
        ps = es.enter_context(nc.psum_tensor("ps", [P, 8, 512], F32))

        def cutter(region, end):
            at = [0]

            def cut(n):
                a = region[:, at[0]:at[0] + n]
                at[0] += n
                assert at[0] <= end
                return a
            return cut

        sm = cutter(small, 336)
        NCOL = 84
        colv = sm(NCOL)
        cond = colv[:, 0:16].rearrange("p (c k) -> p k c", c=2)
        bmod = [colv[:, 16 + 24 * l:40 + 24 * l] for l in range(2)]
        ng = [colv[:, 64 + 8 * l:72 + 8 * l] for l in range(2)]
        bglu = colv[:, 80:84]
        modc = [sm(48).rearrange("p (b c) -> p b c", c=2) for _ in range(2)]
        hA = [sm(16).rearrange("p (k c) -> p k c", c=2) for _ in range(2)]
        ssq, msq, rstd = sm(10), sm(10), sm(10)
        smax, nmax, rsum, rinv = sm(1), sm(1), sm(4), sm(4)
        bnst = sm(6)
        mv = sm(20).rearrange("p (t a) -> p t a", a=2)

        X = RA[:, :].rearrange("p (t f) -> p t f", f=D)
        vt = RA[:, 0:5120].rearrange("p (t f) -> p t f", f=W)
        Tsb = RA[:, 5120:9216].rearrange("p (g m) -> p g m", m=P)
        dskip = RA[:, 9216:9728].rearrange("p (g h) -> p g h", h=HC)
        wsraw = RA[:, 9728:10240].rearrange("p (g q) -> p g q", g=4)
        U = RA[:, 5120:10240].rearrange("p (g n) -> p g n", n=NCH)
        hT1 = RA[:, :].rearrange("p (k t) -> p k t", t=TOK)
        OT = RA[:, 0:8192].rearrange("p (h t) -> p h t", t=SEQ)
        GR = RA[:, 8192:8704]

        hT0 = RB[:, :].rearrange("p (k t) -> p k t", t=TOK)
        Hn = RB[:, :].rearrange("p (r g n) -> p r g n", r=2, n=NCH)
        Yt = RB[:, 0:4096].rearrange("p (s f) -> p s f", f=W)
        Ytc = RB[:, 4096:8192].rearrange("p (s f) -> p s f", f=W)
        x1 = RB[:, :].rearrange("p (t f) -> p t f", f=D)
        Kraw = RB[:, 0:2560].rearrange("p (t f) -> p t f", f=256)
        PT = RB[:, 0:5120].rearrange("p (s q) -> p s q", q=512)
        Vt = RB[:, 5120:7680].rearrange("p (t f) -> p t f", f=256)
        KTt = RB[:, 7680:10240].rearrange("p (j t) -> p j t", t=TOK)

        lraw = RC[:, 0:384].rearrange("p (a m) -> p a m", a=3)
        ldraw = RC[:, 384:386]
        colrow = RC[:, 1536:1664]
        craw = RC[:, 512:1536].rearrange("p (r q m) -> p r q m", r=2, m=P)
        BL = RC[:, 0:8192].rearrange("p (r g s h) -> p r g s h", r=2, g=G, h=HC)
        btmp = RC[:, 8192:9216].rearrange("p (g s h) -> p g s h", g=8, h=HC)
        bstage = RC[:, 9216:10240].rearrange("p (a m) -> p a m", a=2)
        Yl = RC[:, 0:4096].rearrange("p (g s c) -> p g s c", s=CH, c=HC)
        Yc = RC[:, 4096:8192].rearrange("p (g s c) -> p g s c", s=CH, c=HC)
        hperm = RC[:, 8192:10240].rearrange("p (k t) -> p k t", t=NCTX)
        mixT = RC[:, :].rearrange("p (k t) -> p k t", t=TOK)
        Qt = RC[:, 0:8192].rearrange("p (t f) -> p t f", f=D)
        rope_t = [RC[:, 8192 + 512 * i:8704 + 512 * i] for i in range(2)]
        cs = RC[:, 9216:10240].rearrange("p (a t m) -> p a t m", a=2, m=64)
        qT = RC[:, 8192:8704].rearrange("p (h q) -> p h q", h=HPK)
        xr = RC[:, 0:8192].rearrange("p (t f) -> p t f", f=D)

        braw = RD[:, 0:1024].rearrange("p (r g h) -> p r g h", r=2, h=HC)
        cltmp = RD[:, 0:576].rearrange("p (g k o) -> p g k o", g=4, o=HC)
        BB = RD[:, 1024:2048].rearrange("p (r g h) -> p r g h", r=2, h=HC)
        Cx = RD[:, 2048:3072].rearrange("p (r g h) -> p r g h", r=2, h=HC)
        Kt = RD[:, 3072:5120].rearrange("p (g k o) -> p g k o", k=CH, o=HC)
        CL = RD[:, 5120:9728].rearrange("p (r g k o) -> p r g k o", r=2, g=16, o=HC)
        ctmp = RD[:, 9728:10240]
        vgb = RD[:, 9728:10240]
        ddtmp = RD[:, 10240:10304].rearrange("p (g o) -> p g o", o=HC)
        H = RD[:, :].rearrange("p (i r g) -> p i r g", r=2, g=G)
        ys = RD[:, 0:5120].rearrange("p (g n) -> p g n", n=NCH)
        yT = RD[:, 5120:10240].rearrange("p (k t) -> p k t", t=TOK)
        otmp = RD[:, 0:1024].rearrange("p (a n) -> p a n", a=2)
        gateT = RD[:, 0:8192].rearrange("p (h t) -> p h t", t=SEQ)
        qs = RD[:, 8192:8704]
        Pr = RD[:, 8704:9984]

        shc = cutter(shared, 3072)
        lamr, lami, ldt = shc(G), shc(G), shc(G)
        s5t = [shc(G) for _ in range(24)]
        ki, kj = shc(G).bitcast(I32), shc(G).bitcast(I32)
        LP = shc(9 * 64).rearrange("p (k r g) -> p k r g", r=2, g=G)
        LPc = shc(9 * 64).rearrange("p (k r g) -> p k r g", r=2, g=G)
        LPb = shc(8 * 64).rearrange("p (k r g) -> p k r g", r=2, g=G)
        gtb = shared[:, 0:2048].rearrange("p (c f) -> p c f", c=2)
        wsT = shared[:, 2048:2560].rearrange("p (g q) -> p g q", g=4)
        bsb = shared[:, 2560:3072]
        fgb = shared[:, 1024:2048]
        qss, qms, qrs = (shared[:, 2048 + 84 * i:2132 + 84 * i] for i in range(3))

        s_ld_const, s_ld_par, s_ld_b, s_ld_v, s_ld_ws, s_ld_bs = (
            sem("ld_const"), sem("ld_par"), sem("ld_b"), sem("ld_v"), sem("ld_ws"), sem("ld_bs"))
        s_ld_tab, s_ld_gain, s_ld_fin, s_x1_out, s_x1_back, s_stored = (
            sem("ld_tab"), sem("ld_gain"), sem("ld_fin"), sem("x1_out"), sem("x1_back"), sem("stored"))
        s_chain, s_pchain, s_lraw_ok, s_par_tr, s_par_ok, s_cond_ok = (
            sem("chain"), sem("pchain"), sem("lraw_ok"), sem("par_tr"), sem("par_ok"), sem("cond_ok"))
        s_col_ok, s_mod_mm, s_mod_ok, s_sq, s_rt_req, s_rt_ok = (
            sem("col_ok"), sem("mod_mm"), sem("mod_ok"), sem("sq"), sem("rt_req"), sem("rt_ok"))
        s_xn, s_h_tr, s_h_eva, s_h_evd, s_v_mm, s_v_ev = (
            sem("xn"), sem("h_tr"), sem("h_eva"), sem("h_evd"), sem("v_mm"), sem("v_ev"))
        s_vn_ok, s_vg_ok, s_bl_ok, s_bl_tr, s_bl_ev, s_cl_ok = (
            sem("vn_ok"), sem("vg_ok"), sem("bl_ok"), sem("bl_tr"), sem("bl_ev"), sem("cl_ok"))
        s_cop_out, s_k_mm, s_k_ev, s_t_in, s_t_out, s_par_dead = (
            sem("cop_out"), sem("k_mm"), sem("k_ev"), sem("t_in"), sem("t_out"), sem("par_dead"))
        s_hperm_ok, s_xs_mm, s_xs_eva, s_xs_evd, s_ws_tr, s_ws_ev = (
            sem("hperm_ok"), sem("xs_mm"), sem("xs_eva"), sem("xs_evd"), sem("ws_tr"), sem("ws_ev"))
        s_u_tr, s_u_ev, s_b_mm, s_b_evf, s_b_evb, s_gt_tr = (
            sem("u_tr"), sem("u_ev"), sem("b_mm"), sem("b_evf"), sem("b_evb"), sem("gt_tr"))
        s_gt_ev, s_rec, s_rec_ok, s_f_mm, s_f_ev, s_ga_ok = (
            sem("gt_ev"), sem("rec"), sem("rec_ok"), sem("f_mm"), sem("f_ev"), sem("ga_ok"))
        s_gm_mm, s_gm_ok, s_hn_f, s_hn_b, s_c_mm, s_c_ev = (
            sem("gm_mm"), sem("gm_ok"), sem("hn_f"), sem("hn_b"), sem("c_mm"), sem("c_ev"))
        s_y1_tr, s_y1_eva, s_y1_evd, s_y2_tr, s_y2_eva, s_y2_evd = (
            sem("y1_tr"), sem("y1_eva"), sem("y1_evd"), sem("y2_tr"), sem("y2_eva"), sem("y2_evd"))
        s_glu_mm, s_glu_sg, s_glu_y, s_glu_ok, s_o_mm, s_o_t = (
            sem("glu_mm"), sem("glu_sg"), sem("glu_y"), sem("glu_ok"), sem("o_mm"), sem("o_t"))
        s_o_ok, s_kv_mm, s_kv_ev, s_q_mm, s_q_ev, s_g_mm = (
            sem("o_ok"), sem("kv_mm"), sem("kv_ev"), sem("q_mm"), sem("q_ev"), sem("g_mm"))
        s_g_ev, s_k_ok, s_q_ok, s_kt_tr, s_kt_ev, s_a_qs = (
            sem("g_ev"), sem("k_ok"), sem("q_ok"), sem("kt_tr"), sem("kt_ev"), sem("a_qs"))
        s_a_q, s_a_qT, s_a_s, s_a_max, s_a_p, s_a_t = (
            sem("a_q"), sem("a_qT"), sem("a_s"), sem("a_max"), sem("a_p"), sem("a_t"))
        s_a_tea, s_a_ted, s_a_ri, s_a_rt, s_a_pv, s_a_gr = (
            sem("a_tea"), sem("a_ted"), sem("a_ri"), sem("a_rt"), sem("a_pv"), sem("a_gr"))
        s_a_o, s_z_mm, s_z_t, s_z_ok, s_fin_sq, s_fin_g = (
            sem("a_o"), sem("z_mm"), sem("z_t"), sem("z_ok"), sem("fin_sq"), sem("fin_g"))
        s_bop_out = [sem(f"bop_out{i}") for i in range(2)]
        ld_x, ld_x2 = ([sem(f"{n}_{i}") for i in range(5)] for n in ("ld_x", "ld_x2"))
        w_in = [sem(f"w_in{i}") for i in range(NSLOT)]

        uses = [("mod0", b) for b in range(4)]
        uses += [("v", 0), ("xs", 0), ("mod0", 4), ("mod0", 5), ("bop", 0), ("bop", 1), ("u", 0), ("ga", 0), ("gb", 0)]
        uses += [("mod1", b) for b in range(6)] + [("ct", q) for q in range(4)]
        uses += [("glu", 0), ("out0", 0), ("out0", 1), ("kv", 0), ("q", 0), ("q", 1), ("gate", 0), ("gate", 1),
                 ("out1", 0), ("out1", 1)]
        place = {u: i for i, u in enumerate(uses)}
        done_when = {("mod0", b): (s_mod_mm, b + 1) for b in range(6)} | {("mod1", b): (s_mod_mm, b + 7) for b in range(6)}
        done_when |= {("v", 0): (s_v_mm, TT), ("xs", 0): (s_xs_mm, CH + 2), ("u", 0): (s_f_mm, 12), ("ga", 0): (s_f_mm, 24),
                      ("gb", 0): (s_f_mm, 36), ("glu", 0): (s_glu_mm, 12), ("kv", 0): (s_kv_mm, TT)}
        for b in range(2):
            done_when |= {("bop", b): (s_b_mm, 16 * (b + 1)), ("out0", b): (s_o_mm, TT * (b + 1)),
                          ("q", b): (s_q_mm, LT * (b + 1)), ("gate", b): (s_g_mm, LT * (b + 1))}
        done_when |= {("ct", q): (s_c_mm, 4 * (q + 1)) for q in range(4)}
        source = {"v": (we_in, W), "xs": (we_in, 3 * W), "u": (we_in, 0), "ga": (we_in, 2 * W), "gb": (we_in, 4 * W),
                  "mod0": (w_mod[0:1], 0), "mod1": (w_mod[1:2], 0), "out0": (we_out, 0), "out1": (wo_out, 0),
                  "kv": (wo_in, D), "q": (wo_in, 0), "gate": (wo_in, D + 512)}

        def slot(u):
            i = place[u] % NSLOT
            return ring[:, i * SLOT:(i + 1) * SLOT]

        def slot_kn(u):
            return slot(u).rearrange("p (k n) -> p k n", n=512)

        block = es.enter_context(nc.Block())

        @block.sync
        def _(sp):
            def ring_load(kind, b):
                u = (kind, b)
                i = place[u]
                if i >= NSLOT:
                    sp.wait_ge(*done_when[uses[i - NSLOT]])
                dst = slot(u)
                if kind == "bop":
                    if b == 0:
                        sp.wait_ge(s_bop_out[0], 16 * 8)
                        sp.wait_ge(s_bop_out[1], 16 * 8)
                    src = bop_d[b].rearrange("p r g m -> p (r g m)")
                elif kind == "ct":
                    if b == 0:
                        sp.wait_ge(s_cop_out, 16 * 16)
                        sp.wait_ge(s_t_out, 16 * 4)
                    dst, src = dst[:, 0:3072], ct_d[b].rearrange("p r g m -> p (r g m)")
                elif kind == "glu":
                    dst = dst[:, 0:2048].rearrange("p (k n) -> p k n", n=512)
                    src = s5_w_glu[0].rearrange("(k p) n -> p k n", p=P)
                else:
                    wt, a = source[kind]
                    dst = dst.rearrange("p (k n) -> p k n", n=512)
                    src = wt[0][:, a + 512 * b:a + 512 * b + 512].rearrange("(k p) n -> p k n", p=P)
                sp.dma_start(dst, src).then_inc(w_in[i % NSLOT], 16)

            def token_loads(dst, name):
                sp.dma_start(dst[:, 0:CT, :], ctx_in[0].rearrange("(t p) f -> p t f", p=P)).then_inc(name[0], 16)
                for t in range(0, LT, 2):
                    sp.dma_start(dst[:, CT + t:CT + t + 2, :],
                                 x[0, t * P:(t + 2) * P, :].rearrange("(t p) f -> p t f", p=P)).then_inc(name[1 + t // 2], 16)

            sp.dma_start(ident[:], ident_in).then_inc(s_ld_const, 16)
            r0 = 0
            for rows in (c[0], c_ctx, b_mod[0], b_mod[1], norm_g[0], norm_g[1], s5_b_glu[0]):
                rows = rows.rearrange("(k p) -> k p", p=P)
                sp.dma_start(colrow[r0:r0 + rows.shape[0]], rows).then_inc(s_ld_const, 16)
                r0 += rows.shape[0]
            ring_load("mod0", 0)
            ring_load("mod0", 1)
            ring_load("mod0", 2)
            token_loads(X, ld_x)
            ring_load("mod0", 3)
            ring_load("v", 0)
            ring_load("xs", 0)
            ring_load("mod0", 4)
            sp.wait_ge(s_par_ok, 1)
            sp.dma_start(vgb, gm_v_g.broadcast_to([P, W])).then_inc(s_ld_v, 16)
            sp.wait_ge(s_h_tr, 24)
            sp.dma_start(dskip[0:HC].rearrange("p g h -> p (g h)"), s5_d.broadcast_to([HC, W])).then_inc(s_ld_ws, 16)
            sp.dma_start(wsraw, gm_w_s[0].rearrange("g p q -> p g q")).then_inc(s_ld_ws, 16)
            ring_load("mod0", 5)
            for j in range(16):
                r, q = divmod(j, 8)
                sp.wait_ge(s_bl_ev, j + 1)
                sp.dma_start(bop_d[q // 4, :, r, 4 * (q % 4):4 * (q % 4) + 4, :],
                             bstage[:, j % 2].rearrange("p (g m) -> p g m", m=P)).then_inc(s_bop_out[j % 2], 16)
            for half in range(2):
                sp.wait_ge(s_cl_ok, half + 1)
                for q in range(2):
                    for r in range(2):
                        for d in range(2):
                            rows, k0 = slice(d * NS, (d + 1) * NS), 1 - d
                            sp.dma_start(ct_d[2 * half + q, rows, r].rearrange("p g (s o) -> p g s o", o=HC),
                                         CL[rows, r, 8 * q:8 * q + 8, k0:k0 + CH, :]).then_inc(s_cop_out, 16)
                sp.wait_ge(s_k_ev, 4 * (half + 1))
                gs = slice(16 * half, 16 * half + 16)
                for s in range(CH):
                    rows = slice(HC * s, HC * s + HC)
                    sp.dma_start(Tsb[rows, gs, HC * s:P].rearrange("p g (k o) -> p g k o", o=HC),
                                 Kt[0:HC, :, 0:CH - s, :]).then_inc(s_t_in, 16)
                    if s:
                        sp.dma_start(Tsb[rows, gs, 0:HC * s].rearrange("p g (k o) -> p g k o", o=HC),
                                     Kt[32:32 + HC, :, 7 - s:7, :]).then_inc(s_t_in, 16)
                if half:
                    ring_load("bop", 0)
                sp.wait_ge(s_t_in, 16 * 15 * (half + 1))
                for q in range(2):
                    a = 16 * half + 8 * q
                    sp.dma_start(ct_d[2 * half + q, :, 2], Tsb[:, a:a + 8, :]).then_inc(s_t_out, 16)
            ring_load("bop", 1)
            sp.wait_ge(s_par_dead, 1)
            sp.dma_start(bsb, gm_b_s[0].rearrange("g (o q) -> o (g q)", o=1).broadcast_to([P, 512])).then_inc(s_ld_bs, 16)
            for u in uses[place[("u", 0)]:place[("out0", 0)] + 2]:
                ring_load(*u)
            sp.wait_ge(s_y2_tr, 12)
            token_loads(x1, ld_x2)
            ring_load("kv", 0)
            sp.wait_ge(s_o_mm, 2 * TT)
            sp.dma_start(cs[:, 0], cos_in.rearrange("(t p) m -> p t m", p=P)).then_inc(s_ld_tab, 16)
            sp.dma_start(cs[:, 1], sin_in.rearrange("(t p) m -> p t m", p=P)).then_inc(s_ld_tab, 16)
            sp.dma_start(L8[:], q_norm_g.broadcast_to([P, HD])).then_inc(s_ld_gain, 16)
            sp.dma_start(rt[:], k_norm_g.broadcast_to([P, HD])).then_inc(s_ld_gain, 16)
            sp.wait_ge(s_o_ok, 2 * TT)
            sp.dma_start(x1_d.rearrange("(t p) f -> p t f", p=P), x1[:, CT:TT, :]).then_inc(s_x1_out, 16)
            sp.dma_start(fgb, final_g.rearrange("(o f) -> o f", o=1).broadcast_to([P, D])).then_inc(s_ld_fin, 16)
            for u in uses[place[("q", 0)]:]:
                ring_load(*u)
            sp.wait_ge(s_a_qs, 2 * LT)
            sp.wait_ge(s_x1_out, 16)
            sp.dma_start(xr, x1_d.rearrange("(t p) f -> p t f", p=P)).then_inc(s_x1_back, 16)
            for t in range(LT):
                sp.wait_ge(s_fin_g, t + 1)
                sp.dma_start(out[0, t * P:(t + 1) * P, :], xr[:, t, :]).then_inc(s_stored, 16)
            sp.wait_ge(s_stored, 16 * LT)

        @block.gpsimd
        def _(pool):
            g = nc.gpsimd
            n = [0]

            def step(ins):
                n[0] += 1
                ins.then_inc(s_pchain, 1)
                pool.wait_ge(s_pchain, n[0])

            pool.wait_ge(s_par_ok, 1)
            for q in range(4):
                gs = slice(8 * q, 8 * q + 8)
                L = [LPb[:, :, r, gs].rearrange("p s g -> p g s").unsqueeze(3).broadcast_to([P, 8, CH, HC])
                     for r in range(2)]
                B = [BB[:, r, gs, :].unsqueeze(2).broadcast_to([P, 8, CH, HC]) for r in range(2)]
                step(g.tensor_tensor(BL[:, 0, gs], B[0], L[0], ALU.mult))
                step(g.tensor_tensor(btmp, B[1], L[1], ALU.mult))
                step(g.tensor_tensor(BL[:, 0, gs], BL[:, 0, gs], btmp, ALU.subtract))
                step(g.tensor_tensor(BL[:, 1, gs], B[0], L[1], ALU.mult))
                step(g.tensor_tensor(btmp, B[1], L[0], ALU.mult))
                g.tensor_tensor(BL[:, 1, gs], BL[:, 1, gs], btmp, ALU.add).then_inc(s_bl_ok, 1)
                pool.wait_ge(s_bl_ok, q + 1)
            pool.wait_ge(s_ld_v, 16)
            for t in range(TT):
                pool.wait_ge(s_vn_ok, t + 1)
                g.tensor_tensor(vt[:, t], vt[:, t], vgb, ALU.mult).then_inc(s_vg_ok, 1)
            j = 0
            for fb in range(FB):
                for t0, nt in CHUNKS:
                    pool.wait_ge(s_f_ev, 12 + j + 1)
                    g.tensor_tensor(mixT[:, fb, t0:t0 + nt], mixT[:, fb, t0:t0 + nt], mixT[:, FB + fb, t0:t0 + nt],
                                    ALU.mult).then_inc(s_ga_ok, 1)
                    j += 1
            j = 0
            for half in range(2):
                for t in range(TT):
                    pool.wait_ge(s_o_t, j + 1)
                    if half == 0:
                        pool.wait_ge(ld_x2[t // 2], 16)
                    xs_ = x1[:, t, half * 512:half * 512 + 512]
                    g.tensor_tensor(xs_, xs_, otmp[:, j % 2], ALU.add).then_inc(s_o_ok, 1)
                    j += 1
            pool.wait_ge(s_x1_back, 16)
            for j in range(2 * LT):
                half, t = divmod(j, LT)
                pool.wait_ge(s_z_t, j + 1)
                xs_ = xr[:, t, half * 512:half * 512 + 512]
                g.tensor_tensor(xs_, xs_, otmp[:, j % 2], ALU.add).then_inc(s_z_ok, 1)

        @block.scalar
        def _(act):
            a = nc.scalar

            def copy(o, i):
                return a.activation(o, i, ACT.Copy)

            for k, tensor in enumerate((s5_lam_re, s5_lam_im)):
                act.dma_start(lraw[0:G, k].rearrange("g (d p) -> g d p", d=2),
                              tensor[0].rearrange("d g p -> g d p")).then_inc(s_ld_par, 16)
            act.dma_start(ldraw[0:G], s5_log_dt[0].rearrange("d g -> g d"), allow_slow_non_contiguous=True).then_inc(s_ld_par, 16)
            for r, tensor in enumerate((s5_c_re, s5_c_im)):
                for d in range(2):
                    act.dma_start(craw[:, r, :, d * NS:(d + 1) * NS],
                                  tensor[0, d].rearrange("(q g) h p -> (g h) q p", q=4)).then_inc(s_ld_par, 16)
            for r, tensor in enumerate((s5_b_re, s5_b_im)):
                for d in range(2):
                    act.dma_start(braw[d * NS:(d + 1) * NS, r],
                                  tensor[0, d].rearrange("g p h -> p g h")).then_inc(s_ld_b, 16)

            def root(i):
                act.wait_ge(s_rt_req, i)
                if i == 4:
                    a.activation(qrs, qms, ACT.Sqrt).then_inc(s_rt_ok, 1)
                else:
                    a.activation(rstd, msq, ACT.Sqrt).then_inc(s_rt_ok, 1)

            def squares(l, Xr, junk, ready):
                for t in range(TT):
                    ready(t)
                    a.activation(junk, Xr[:, t], ACT.Square, accum_out=ssq[:, t:t + 1]).then_inc(s_sq, 1)
                    act.wait_ge(s_sq, TT * l + t + 1)

            def h_evac(l, hT):
                for q, (t0, nt) in enumerate(CHUNKS):
                    ci = 1 if q == 0 else 0
                    for k in range(0, KT, 2):
                        j = KT * q + k
                        act.wait_ge(s_h_tr, 24 * l + j + 1)
                        a.activation(hT[:, k, t0:t0 + nt], ps[:, j % 4, 0:nt], ACT.Identity,
                                     bias=modc[l][:, k, ci:ci + 1], scale=hA[l][:, k, ci:ci + 1]).then_inc(s_h_eva, 1)

            act.wait_ge(s_col_ok, 1)
            a.activation(cond, cond, ACT.Silu).then_inc(s_cond_ok, 1)
            squares(0, X, RB[:, 0:D], lambda t: act.wait_ge(ld_x[t // 2], 16))
            root(1)
            act.wait_ge(s_mod_ok, 1)
            h_evac(0, hT0)
            for t in range(TT):
                act.wait_ge(s_v_mm, t + 1)
                copy(vt[:, t], ps[:, 4 + t % 4, :]).then_inc(s_v_ev, 1)
            for j in range(16):
                act.wait_ge(s_bl_tr, j + 1)
                if j >= 2:
                    act.wait_ge(s_bop_out[j % 2], 16 * (j // 2))
                copy(bstage[:, j % 2], ps[:, j % 4, :]).then_inc(s_bl_ev, 1)
            root(2)
            act.wait_ge(s_h_evd, 12)
            act.wait_ge(s_bop_out[0], 16 * 8)
            act.wait_ge(s_bop_out[1], 16 * 8)
            copy(hperm.rearrange("p k (s n) -> p k s n", s=CH),
                 hT0[:, :, 0:NCTX].rearrange("p k (n s) -> p k s n", s=CH)).then_inc(s_hperm_ok, 1)
            for s in range(CH):
                act.wait_ge(s_xs_mm, s + 1)
                copy(Yl[:, :, s, :], ps[:, 4 + s % 4, :].rearrange("p (g c) -> p g c", c=HC)).then_inc(s_xs_eva, 1)
            act.wait_ge(s_t_out, 16 * 4)
            act.wait_ge(s_ws_ev, 1)
            for j in range(11):
                m = min(3, G - 3 * j)
                act.wait_ge(s_u_tr, j + 1)
                copy(U[:, 3 * j:3 * j + m, :].rearrange("p g n -> p (g n)"), ps[:, j % 4, 0:m * NCH]).then_inc(s_u_ev, 1)
            act.wait_ge(s_cop_out, 16 * 16)
            act.wait_ge(s_t_in, 16 * 30)
            act.wait_ge(s_vg_ok, TT)
            for j in range(32):
                q, r = divmod(j, 2)
                act.wait_ge(s_b_mm, j + 1)
                copy(H[0:NS, 1:NCH + 1, r, 2 * q:2 * q + 2].rearrange("p n g -> p g n"),
                     ps[0:NS, j % 4, 0:2 * NCH].rearrange("p (g n) -> p g n", n=NCH)).then_inc(s_b_evf, 1)
            act.wait_ge(s_par_dead, 1)
            for j in range(4):
                act.wait_ge(s_gt_tr, j + 1)
                copy(gtb[:, j // 2, (j % 2) * 512:(j % 2) * 512 + 512], ps[:, 4 + j, :]).then_inc(s_gt_ev, 1)
            for part in range(3):
                for fb in range(FB):
                    for q, (t0, nt) in enumerate(CHUNKS):
                        j = 12 * part + 3 * fb + q
                        act.wait_ge(s_f_mm, j + 1)
                        if part == 2:
                            act.wait_ge(s_ga_ok, 3 * fb + q + 1)
                        a.activation(mixT[:, (FB if part else 0) + fb, t0:t0 + nt], ps[:, j % 4, 0:nt],
                                     ACT.Silu if part else ACT.Copy).then_inc(s_f_ev, 1)
            act.wait_ge(s_rec_ok, 1)
            for r in range(2):
                copy(Hn[0:NS, r], H[0:NS, 0:NCH, r, :].rearrange("p n g -> p g n")).then_inc(s_hn_f, 1)
            act.wait_ge(s_hn_f, 2)
            act.wait_ge(s_hn_b, 4)
            for j in range(16):
                act.wait_ge(s_c_mm, j + 1)
                a.activation(ys[:, 2 * j:2 * j + 2, :], ps[:, 4 + j % 4, 0:2 * NCH].rearrange("p (g n) -> p g n", n=NCH),
                             ACT.Gelu_apprx_tanh).then_inc(s_c_ev, 1)
            for j in range(8):
                act.wait_ge(s_y1_tr, 2 * j + 1)
                copy(Yt[:, :, 64 * j:64 * j + 64].rearrange("p s (g o) -> p g s o", o=HC),
                     ps[:, 2 * (j % 2), :].rearrange("p (g s o) -> p g s o", g=4, o=HC)).then_inc(s_y1_eva, 1)
            for j in range(8):
                fb, q = divmod(j, 2)
                act.wait_ge(s_y2_tr, j + 1)
                copy(yT[:, fb, NCTX:TOK].rearrange("p (n s) -> p s n", s=CH)[:, 4 * q:4 * q + 4, :],
                     ps[:, 4 + j % 4, :].rearrange("p (s n) -> p s n", s=4)).then_inc(s_y2_eva, 1)
            for j in range(12):
                act.wait_ge(s_glu_mm, j + 1)
                nt = CHUNKS[j % 3][1]
                a.activation(ps[:, j % 4, 0:nt], ps[:, j % 4, 0:nt], ACT.Sigmoid,
                             bias=bglu[:, j // 3:j // 3 + 1]).then_inc(s_glu_sg, 1)
            squares(1, x1, RA[:, 0:D], lambda t: act.wait_ge(s_o_ok, TT + t + 1))
            root(3)
            act.wait_ge(s_mod_ok, 2)
            h_evac(1, hT1)
            for t in range(TT):
                act.wait_ge(s_kv_mm, t + 1)
                copy(Kraw[:, t], ps[:, 4 + t % 4, 0:256]).then_inc(s_kv_ev, 1)
                copy(Vt[:, t], ps[:, 4 + t % 4, 256:512]).then_inc(s_kv_ev, 1)
            for j in range(2 * LT):
                half, t = divmod(j, LT)
                act.wait_ge(s_q_mm, j + 1)
                copy(Qt[:, t, half * 512:half * 512 + 512], ps[:, j % 4, :]).then_inc(s_q_ev, 1)
            for j in range(2 * NH):
                h, q = divmod(j, 2)
                act.wait_ge(s_g_mm, j + 1)
                a.activation(gateT[:, h, q * 512:q * 512 + 512], ps[:, j % 4, :], ACT.Silu).then_inc(s_g_ev, 1)
            root(4)
            for j in range(6):
                act.wait_ge(s_kt_tr, j + 1)
                h, q = divmod(j, 3)
                nt = 256 if q == 2 else 512
                copy(KTt[:, h, 512 * q:512 * q + nt], ps[:, 4 + j % 4, 0:nt]).then_inc(s_kt_ev, 1)
            for j in range(2):
                act.wait_ge(s_kt_tr, 7 + j)
                copy(gtb[:, 0, 512 * j:512 * j + 512], ps[:, 4 + (6 + j) % 4, :]).then_inc(s_kt_ev, 1)

            def group(i):
                act.wait_ge(s_a_qT, i + 1)
                copy(qT, ps[:, 7, :].rearrange("p (h q) -> p h q", q=P)).then_inc(s_a_q, 1)
                for h in range(HPK):
                    m = HPK * i + h
                    act.wait_ge(s_a_max, m + 1)
                    if m:
                        act.wait_ge(s_a_t, m)
                    if h == 0 and i:
                        act.wait_ge(s_a_ri, i)
                    a.activation(Pr, ps[:, 0:3, :].rearrange("p b n -> p (b n)")[:, 0:TOK], ACT.Exp,
                                 bias=nmax, accum_out=rsum[:, h:h + 1]).then_inc(s_a_p, 1)
                    act.wait_ge(s_a_t, m + 1)
                    if h == 0 and i:
                        act.wait_ge(s_a_pv, i)
                    copy(PT[:, 0:4, h * P:h * P + P], ps[:, 3, :].rearrange("p (s q) -> p s q", q=P)).then_inc(s_a_tea, 1)
            for i in range(2 * LT):
                group(i)
            act.wait_ge(s_a_pv, 2 * LT)
            for t in range(LT):
                act.wait_ge(s_z_ok, LT + t + 1)
                a.activation(RB[:, 0:D], xr[:, t], ACT.Square, accum_out=ssq[:, t:t + 1]).then_inc(s_fin_sq, 1)
                act.wait_ge(s_fin_sq, t + 1)
            root(5)

        @block.vector
        def _(dve):
            v = nc.vector
            n = [0]

            def step(ins):
                n[0] += 1
                ins.then_inc(s_chain, 1)
                dve.wait_ge(s_chain, n[0])

            def tt(o, a, b, op):
                step(v.tensor_tensor(o, a, b, op))

            def ts(o, a, s1, op1, s2=None, op2=ALU.bypass):
                step(v.tensor_scalar(o, a, s1, s2, op1, op2))

            def cp(o, a):
                step(v.tensor_copy(o, a))

            def rsqrt(i, ss, m, rr, scale):
                v.tensor_scalar(m, ss, scale, EPS, ALU.mult, ALU.add).then_inc(s_rt_req, 1)
                dve.wait_ge(s_rt_req, i)
                dve.wait_ge(s_rt_ok, i)
                step(v.reciprocal(rr, rr))
                tt(ss, rr, rr, ALU.mult)
                tt(ss, ss, m, ALU.mult)
                ts(ss, ss, -0.5, ALU.mult, 1.5, ALU.add)
                tt(rr, rr, ss, ALU.mult)

            dve.wait_ge(s_par_tr, 1)
            v.tensor_copy(colv, ps[:, 3, 0:NCOL]).then_inc(s_col_ok, 1)
            dve.wait_ge(s_ld_par, 16 * 7)
            v.tensor_copy(lraw[0:G, 2].rearrange("g (d p) -> g d p", d=2),
                          ldraw[0:G].unsqueeze(2).broadcast_to([G, 2, NS])).then_inc(s_lraw_ok, 1)
            dve.wait_ge(s_par_tr, 2)
            for k, dst in enumerate((lamr, lami, ldt)):
                cp(dst, ps[:, 0, 32 * k:32 * k + 32])
            (dt, xe, kf, rr, ex, mg, s_, c_, r2, odd, sg, sn, cn, lr, li, fr, fi, t1, t2, t3, den, msk, t4, th) = s5t

            def exp_(o, xin):
                ts(msk, xin, -87.0, ALU.is_ge)
                ts(t4, xin, -87.0, ALU.max, 88.0, ALU.min)
                ts(ki, t4, 1.0 / math.log(2.0), ALU.mult)
                cp(kf, ki)
                ts(t1, kf, -LN2_HI, ALU.mult)
                tt(rr, t4, t1, ALU.add)
                ts(t1, kf, -LN2_LO, ALU.mult)
                tt(rr, rr, t1, ALU.add)
                ts(ex, rr, 1.0 / 5040, ALU.mult, 1.0 / 720, ALU.add)
                for q in (120.0, 24.0, 6.0, 2.0, 1.0, 1.0):
                    tt(ex, ex, rr, ALU.mult)
                    ts(ex, ex, 1.0 / q, ALU.add)
                ts(kf, kf, 127.0, ALU.add)
                cp(ki, kf)
                ts(kj, ki, 23, ALU.logical_shift_left)
                tt(ex, ex, kj.bitcast(F32), ALU.mult)
                tt(o, ex, msk, ALU.mult)

            exp_(dt, ldt)
            tt(xe, lamr, dt, ALU.mult)
            exp_(mg, xe)
            tt(th, lami, dt, ALU.mult)
            ts(ki, th, 2.0 / math.pi, ALU.mult)
            cp(kf, ki)
            cp(rr, th)
            for q in PIO2:
                ts(t1, kf, -q, ALU.mult)
                tt(rr, rr, t1, ALU.add)
            tt(r2, rr, rr, ALU.mult)
            ts(s_, r2, 1.0 / 362880, ALU.mult, -1.0 / 5040, ALU.add)
            for q in (1.0 / 120, -1.0 / 6, 1.0):
                tt(s_, s_, r2, ALU.mult)
                ts(s_, s_, q, ALU.add)
            tt(s_, s_, rr, ALU.mult)
            ts(c_, r2, -1.0 / 3628800, ALU.mult, 1.0 / 40320, ALU.add)
            for q in (-1.0 / 720, 1.0 / 24, -0.5, 1.0):
                tt(c_, c_, r2, ALU.mult)
                ts(c_, c_, q, ALU.add)
            ts(kj, ki, 1, ALU.bitwise_and)
            cp(odd, kj)
            ts(sg, odd, -1.0, ALU.mult, 1.0, ALU.add)
            tt(sn, s_, sg, ALU.mult)
            tt(t1, c_, odd, ALU.mult)
            tt(sn, sn, t1, ALU.add)
            tt(cn, c_, sg, ALU.mult)
            tt(t1, s_, odd, ALU.mult)
            tt(cn, cn, t1, ALU.add)
            for o, add in ((sn, 0.0), (cn, 1.0)):
                ts(kf, kf, add, ALU.add)
                cp(ki, kf)
                ts(kj, ki, 1, ALU.logical_shift_right, 1, ALU.bitwise_and)
                cp(sg, kj)
                ts(sg, sg, -2.0, ALU.mult, 1.0, ALU.add)
                tt(o, o, sg, ALU.mult)
            tt(lr, mg, cn, ALU.mult)
            tt(li, mg, sn, ALU.mult)
            tt(den, lamr, lamr, ALU.mult)
            tt(t1, lami, lami, ALU.mult)
            tt(den, den, t1, ALU.add)
            step(v.reciprocal(den, den))
            ts(t3, lr, -1.0, ALU.add)
            tt(t1, t3, lamr, ALU.mult)
            tt(t2, li, lami, ALU.mult)
            tt(t1, t1, t2, ALU.add)
            tt(fr, t1, den, ALU.mult)
            tt(t1, li, lamr, ALU.mult)
            tt(t2, t3, lami, ALU.mult)
            tt(t1, t1, t2, ALU.subtract)
            tt(fi, t1, den, ALU.mult)
            step(v.memset(LP[:, 0, 0], 1.0))
            step(v.memset(LP[:, 0, 1], 0.0))
            cp(LP[:, 1, 0], lr)
            cp(LP[:, 1, 1], li)
            for m in (1, 2, 4):
                A = [LP[:, 1:m + 1, r] for r in range(2)]
                M = [LP[:, m, r].unsqueeze(1).broadcast_to([P, m, G]) for r in range(2)]
                O = [LP[:, m + 1:2 * m + 1, r] for r in range(2)]
                tmp = ctmp[:, 0:m * G].rearrange("p (m g) -> p m g", g=G)
                tt(O[0], A[0], M[0], ALU.mult)
                tt(tmp, A[1], M[1], ALU.mult)
                tt(O[0], O[0], tmp, ALU.subtract)
                tt(O[1], A[0], M[1], ALU.mult)
                tt(tmp, A[1], M[0], ALU.mult)
                tt(O[1], O[1], tmp, ALU.add)
            fwd, bwd = slice(0, NS), slice(NS, P)
            cp(LPc[fwd], LP[fwd])
            cp(LPc[bwd], LP[bwd, ::-1])
            cp(LPb[fwd], LP[fwd, 7::-1])
            cp(LPb[bwd], LP[bwd, 0:8])
            cp(L8[:, 0:32], LP[:, 8, 0])
            cp(L8[:, 32:64], LP[:, 8, 0])
            cp(L8[:, 64:96], LP[:, 8, 1])
            ts(L8[:, 96:128], LP[:, 8, 1], -1.0, ALU.mult)
            dve.wait_ge(s_ld_b, 16 * 4)
            F = [q.unsqueeze(2).broadcast_to([P, G, HC]) for q in (fr, fi)]
            tmp = ctmp.rearrange("p (g h) -> p g h", h=HC)
            tt(BB[:, 0], braw[:, 0], F[0], ALU.mult)
            tt(tmp, braw[:, 1], F[1], ALU.mult)
            tt(BB[:, 0], BB[:, 0], tmp, ALU.subtract)
            tt(BB[:, 1], braw[:, 1], F[0], ALU.mult)
            tt(tmp, braw[:, 0], F[1], ALU.mult)
            tt(BB[:, 1], BB[:, 1], tmp, ALU.add)
            dve.wait_ge(s_par_tr, 4)
            cp(Cx[:, 0], ps[:, 1, :].rearrange("p (g h) -> p g h", h=HC))
            v.tensor_scalar(Cx[:, 1], ps[:, 2, :].rearrange("p (g h) -> p g h", h=HC), -1.0, None,
                            ALU.mult).then_inc(s_par_ok, 1)
            dve.wait_ge(s_par_ok, 1)

            def mod_evac(l, k, b0, b1, bank):
                dve.wait_ge(s_mod_mm, k)
                tt(modc[l][:, b0:b1], ps[:, bank, 2 * b0:2 * b1].rearrange("p (b c) -> p b c", c=2),
                   bmod[l][:, b0:b1].unsqueeze(2).broadcast_to([P, b1 - b0, 2]), ALU.add)

            def make_a(l):
                ts(hA[l], modc[l][:, 8:16], 1.0, ALU.add)
                v.tensor_tensor(hA[l], hA[l], ng[l].unsqueeze(2).broadcast_to([P, KT, 2]), ALU.mult).then_inc(s_mod_ok, 1)
                dve.wait_ge(s_mod_ok, l + 1)

            def normed(l, Xr, i):
                dve.wait_ge(s_sq, TT * (l + 1))
                rsqrt(i, ssq, msq, rstd, 1.0 / D)
                for t in range(TT):
                    v.tensor_scalar(Xr[:, t], Xr[:, t], rstd[:, t:t + 1], None, ALU.mult).then_inc(s_xn, 1)

            def h_evac(l, hT):
                for q, (t0, nt) in enumerate(CHUNKS):
                    ci = 1 if q == 0 else 0
                    for k in range(1, KT, 2):
                        j = KT * q + k
                        dve.wait_ge(s_h_tr, 24 * l + j + 1)
                        v.tensor_scalar(hT[:, k, t0:t0 + nt], ps[:, j % 4, 0:nt], hA[l][:, k, ci:ci + 1],
                                        modc[l][:, k, ci:ci + 1], ALU.mult, ALU.add).then_inc(s_h_evd, 1)

            normed(0, X, 1)
            mod_evac(0, 4, 0, 16, 4)
            make_a(0)
            h_evac(0, hT0)

            def build_cl(half):
                if half:
                    dve.wait_ge(s_cop_out, 16 * 8)
                    dve.wait_ge(s_k_mm, 4)
                for q in range(4):
                    g4 = slice(4 * q, 4 * q + 4)
                    a4 = slice(16 * half + 4 * q, 16 * half + 4 * q + 4)
                    L = [LPc[:, :, r, a4].rearrange("p k g -> p g k").unsqueeze(3).broadcast_to([P, 4, 9, HC])
                         for r in range(2)]
                    C_ = [Cx[:, r, a4, :].unsqueeze(2).broadcast_to([P, 4, 9, HC]) for r in range(2)]
                    tt(CL[:, 0, g4], C_[0], L[0], ALU.mult)
                    tt(cltmp, C_[1], L[1], ALU.mult)
                    tt(CL[:, 0, g4], CL[:, 0, g4], cltmp, ALU.add)
                    tt(CL[:, 1, g4], C_[1], L[0], ALU.mult)
                    tt(cltmp, C_[0], L[1], ALU.mult)
                    tt(CL[:, 1, g4], CL[:, 1, g4], cltmp, ALU.subtract)
                v.tensor_copy(cltmp[:, 0, 0, :], cltmp[:, 0, 1, :]).then_inc(s_cl_ok, 1)
                dve.wait_ge(s_cl_ok, half + 1)

            def k_evac(half):
                dve.wait_ge(s_ld_ws, 16 * 2)
                if half:
                    dve.wait_ge(s_t_in, 16 * 15)
                for q in range(4):
                    dve.wait_ge(s_k_mm, 4 * half + q + 1)
                    g4 = slice(4 * q, 4 * q + 4)
                    a4 = slice(16 * half + 4 * q, 16 * half + 4 * q + 4)
                    bk = ps[:, q, :].rearrange("p (g k o) -> p g k o", k=CH, o=HC)
                    cp(Kt[32:32 + HC, g4, 0:7], bk[32:32 + HC, :, 0:7])
                    cp(Kt[0:HC, g4], bk[0:HC])
                    tt(ddtmp[0:HC], ident[0:HC, 0:HC].unsqueeze(1).broadcast_to([HC, 4, HC]), dskip[0:HC, a4, :], ALU.mult)
                    v.tensor_tensor(Kt[0:HC, g4, 0], Kt[0:HC, g4, 0], ddtmp[0:HC], ALU.add).then_inc(s_k_ev, 1)
                    dve.wait_ge(s_k_ev, 4 * half + q + 1)

            build_cl(0)
            for t in range(TT):
                dve.wait_ge(s_v_ev, t + 1)
                step(v.bn_stats(bnst, vt[:, t]))
                step(v.bn_aggr(mv[:, t], bnst))
            cp(ssq.unsqueeze(2), mv[:, :, 1:2])
            rsqrt(2, ssq, msq, rstd, 1.0)
            for t in range(TT):
                v.tensor_scalar(vt[:, t], vt[:, t], mv[:, t, 0:1], rstd[:, t:t + 1], ALU.subtract, ALU.mult).then_inc(s_vn_ok, 1)
            k_evac(0)
            build_cl(1)
            dve.wait_ge(s_bl_tr, 16)
            for j in range(2):
                dve.wait_ge(s_xs_mm, CH + j + 1)
                for q in range(4):
                    v.tensor_copy(Yc[0:CCH, :, 4 * j + q, :],
                                  ps[32 * q:32 * q + 32, 4 + j, :].rearrange("p (g c) -> p g c", c=HC)).then_inc(s_xs_evd, 1)
            k_evac(1)
            dve.wait_ge(s_k_mm, 8)
            dve.wait_ge(s_bl_ok, 4)
            dve.wait_ge(s_ws_tr, 1)
            v.tensor_copy(wsT, ps[:, 5, :].rearrange("p (g q) -> p g q", g=4)).then_inc(s_ws_ev, 1)
            mod_evac(0, 6, 16, 24, 4)
            v.tensor_copy(rt[:, 0:1], L8[:, 0:1]).then_inc(s_par_dead, 1)
            dve.wait_ge(s_cop_out, 16 * 16)
            dve.wait_ge(s_t_in, 16 * 30)
            dve.wait_ge(s_vg_ok, TT)
            v.memset(H[:, 0], 0.0).then_inc(s_b_evb, 1)
            for j in range(32):
                q, r = divmod(j, 2)
                dve.wait_ge(s_b_mm, j + 1)
                src = ps[NS:P, j % 4, 0:2 * NCH].rearrange("p (g n) -> p g n", n=NCH)
                v.tensor_copy(H[NS:P, CCH:0:-1, r, 2 * q:2 * q + 2].rearrange("p n g -> p g n"),
                              src[:, :, 0:CCH]).then_inc(s_b_evb, 1)
                v.tensor_copy(H[NS:P, NCH:CCH:-1, r, 2 * q:2 * q + 2].rearrange("p n g -> p g n"),
                              src[:, :, CCH:NCH]).then_inc(s_b_evb, 1)
            dve.wait_ge(s_b_evb, 65)
            dve.wait_ge(s_b_evf, 32)
            Hf = H.rearrange("p i r g -> p i (r g)")
            LR, LI = L8[:, 0:64], L8[:, 64:128].rearrange("p (r g) -> p r g", r=2)
            m0, m1 = rt[:, 0:64], rt[:, 64:128]
            UNR = 4
            with dve.Fori(0, NCH // UNR) as it:
                for k in range(UNR):
                    i = it * UNR + k
                    v.tensor_tensor(m0, Hf[:, i, :], LR, ALU.mult).then_inc(s_rec, 1)
                    v.tensor_tensor(m1.rearrange("p (r g) -> p r g", r=2)[:, ::-1, :], H[:, i, :, :], LI, ALU.mult).then_inc(s_rec, 1)
                    dve.wait_ge(s_rec, i * 4 + 1)
                    v.tensor_tensor(Hf[:, i + 1, :], Hf[:, i + 1, :], m0, ALU.add).then_inc(s_rec, 1)
                    dve.wait_ge(s_rec, i * 4 + 3)
                    v.tensor_tensor(Hf[:, i + 1, :], Hf[:, i + 1, :], m1, ALU.add).then_inc(s_rec, 1)
                    dve.wait_ge(s_rec, i * 4 + 4)
            v.tensor_copy(rt[:, 0:1], rt[:, 1:2]).then_inc(s_rec_ok, 1)
            dve.wait_ge(s_ld_bs, 16)
            dve.wait_ge(s_ga_ok, 12)
            for t in range(TT):
                dve.wait_ge(s_gm_mm, t + 1)
                pb = ps[:, 4 + t % 4, :]
                tt(pb, pb, bsb, ALU.add)
                v.tensor_tensor(mixT[:, 0:FB, t * P:(t + 1) * P], mixT[:, 0:FB, t * P:(t + 1) * P],
                                pb.rearrange("p (g q) -> p g q", g=FB), ALU.mult).then_inc(s_gm_ok, 1)
            dve.wait_ge(s_f_mm, 36)
            dve.wait_ge(s_rec_ok, 1)
            for r in range(2):
                v.tensor_copy(Hn[NS:P, r, :, 0:CCH], H[NS:P, CCH - 1::-1, r, :].rearrange("p n g -> p g n")).then_inc(s_hn_b, 1)
                v.tensor_copy(Hn[NS:P, r, :, CCH:NCH], H[NS:P, NCH - 1:CCH - 1:-1, r, :].rearrange("p n g -> p g n")).then_inc(s_hn_b, 1)
            mod_evac(1, 12, 0, 24, 0)
            make_a(1)
            for j in range(8):
                dve.wait_ge(s_y1_tr, 2 * j + 2)
                v.tensor_copy(Ytc[0:CCH, :, 64 * j:64 * j + 64].rearrange("p s (g o) -> p g s o", o=HC),
                              ps[0:CCH, 2 * (j % 2) + 1, :].rearrange("p (g s o) -> p g s o", g=4, o=HC)).then_inc(s_y1_evd, 1)
            for j in range(4):
                dve.wait_ge(s_y2_tr, 8 + j + 1)
                v.tensor_copy(yT[:, j, 0:NCTX].rearrange("p (n s) -> p s n", s=CH),
                              ps[:, 4 + j, 0:NCTX].rearrange("p (s n) -> p s n", s=CH)).then_inc(s_y2_evd, 1)
            for j in range(12):
                fb, q = divmod(j, 3)
                t0, nt = CHUNKS[q]
                dve.wait_ge(s_glu_sg, j + 1)
                pb, m = ps[:, j % 4, 0:nt], mixT[:, FB + fb, t0:t0 + nt]
                tt(pb, pb, yT[:, fb, t0:t0 + nt], ALU.mult)
                v.tensor_tensor(m, m, pb, ALU.mult).then_inc(s_glu_ok, 1)
            for j in range(2 * TT):
                half, t = divmod(j, TT)
                dve.wait_ge(s_o_mm, j + 1)
                if j >= 2:
                    dve.wait_ge(s_o_ok, j - 1)
                v.tensor_tensor(otmp[:, j % 2], ps[:, 4 + j % 4, :],
                                gtb[:, 1 if t < CT else 0, half * 512:half * 512 + 512], ALU.mult).then_inc(s_o_t, 1)
            dve.wait_ge(s_x1_out, 16)
            normed(1, x1, 3)
            h_evac(1, hT1)
            dve.wait_ge(s_ld_gain, 16 * 2)
            ts(L8[:], L8[:], HD ** -0.5, ALU.mult)

            def head_sums(src, nh, o):
                tt(rope_t[0][:, 0:nh * HD], src, src, ALU.mult)
                step(v.tensor_reduce(o, rope_t[0][:, 0:nh * HD].rearrange("p (h d) -> p h d", d=HD), AX.X, ALU.add))

            def gained(q, nh, r, gain):
                qv = q.rearrange("p (h d) -> p h d", d=HD)
                tt(qv, qv, r.unsqueeze(2).broadcast_to([P, nh, HD]), ALU.mult)
                tt(qv, qv, gain.unsqueeze(1).broadcast_to([P, nh, HD]), ALU.mult)

            def rope(q, nh, t):
                q4 = q.rearrange("p (h a b m) -> p h a b m", h=nh, a=2, b=2)
                tabs = [cs[:, k, t].rearrange("p (a m) -> p a m", a=2) for k in range(2)]
                t_ = [rope_t[k][:, 0:nh * 64].rearrange("p (h a m) -> p h a m", h=nh, a=2) for k in range(2)]
                for ax in range(2):
                    x1_, x2_ = q4[:, :, ax, 0], q4[:, :, ax, 1]
                    co, si = (tabs[k][:, ax].unsqueeze(1).broadcast_to([P, nh, 32]) for k in range(2))
                    tt(t_[0][:, :, ax], x1_, si, ALU.mult)
                    tt(t_[1][:, :, ax], x2_, si, ALU.mult)
                    tt(x1_, x1_, co, ALU.mult)
                    tt(x1_, x1_, t_[1][:, :, ax], ALU.subtract)
                    tt(x2_, x2_, co, ALU.mult)
                    tt(x2_, x2_, t_[0][:, :, ax], ALU.add)

            dve.wait_ge(s_ld_tab, 16 * 2)
            for t in range(TT):
                dve.wait_ge(s_kv_ev, 2 * t + 2)
                head_sums(Kraw[:, t], NKV, qss[:, 64 + 2 * t:66 + 2 * t])
            for j in range(2 * LT):
                half, t = divmod(j, LT)
                dve.wait_ge(s_q_ev, j + 1)
                head_sums(Qt[:, t, half * 512:half * 512 + 512], 4, qss[:, 8 * t + 4 * half:8 * t + 4 * half + 4])
            rsqrt(4, qss, qms, qrs, 1.0 / HD)
            for t in range(TT):
                gained(Kraw[:, t], NKV, qrs[:, 64 + 2 * t:66 + 2 * t], rt[:])
                if t >= CT:
                    rope(Kraw[:, t], NKV, t - CT)
            v.tensor_copy(small[:, 335:336], small[:, 0:1]).then_inc(s_k_ok, 1)
            for t in range(LT):
                for half in range(2):
                    q = Qt[:, t, half * 512:half * 512 + 512]
                    gained(q, 4, qrs[:, 8 * t + 4 * half:8 * t + 4 * half + 4], L8[:])
                    rope(q, 4, t)
            dve.wait_ge(s_g_ev, 2 * NH)
            dve.wait_ge(s_kt_ev, 8)

            def queries(i):
                if i:
                    dve.wait_ge(s_a_qT, i)
                v.tensor_copy(qs, Qt[:, i // 2, (i % 2) * 512:(i % 2) * 512 + 512]).then_inc(s_a_qs, 1)

            def row_max(m):
                dve.wait_ge(s_a_s, m + 1)
                if m:
                    dve.wait_ge(s_a_p, m)
                step(v.tensor_reduce(smax, ps[:, 0:3, :].rearrange("p b n -> p (b n)")[:, 0:TOK], AX.X, ALU.max))
                v.tensor_scalar(nmax, smax, -1.0, None, ALU.mult).then_inc(s_a_max, 1)

            def group(i):
                b, kv = divmod(i, 2)
                for h in range(HPK):
                    m = HPK * i + h
                    if h or i == 0:
                        row_max(m)
                    dve.wait_ge(s_a_t, m + 1)
                    if h == 0 and i:
                        dve.wait_ge(s_a_pv, i)
                    v.tensor_copy(PT[:, 4:10, h * P:h * P + P],
                                  ps[:, 4:6, :].rearrange("p b (s q) -> p (b s) q", q=P)[:, 0:6]).then_inc(s_a_ted, 1)
                dve.wait_ge(s_a_p, HPK * (i + 1))
                v.reciprocal(rinv, rsum).then_inc(s_a_ri, 1)
                if i + 1 < 2 * LT:
                    queries(i + 1)
                dve.wait_ge(s_a_rt, i + 1)
                gt_ = gateT[:, HPK * kv:HPK * kv + HPK, b * P:(b + 1) * P]
                gr = GR.rearrange("p (h q) -> p h q", q=P)
                step(v.tensor_tensor(gr, gt_, ps[:, 7, :].rearrange("p (h q) -> p h q", q=P), ALU.mult))
                dve.wait_ge(s_chain, n[0])
                v.tensor_copy(small[:, 335:336], small[:, 0:1]).then_inc(s_a_gr, 1)
                if i + 1 < 2 * LT:
                    row_max(HPK * (i + 1))
                dve.wait_ge(s_a_pv, i + 1)
                v.tensor_tensor(OT[:, HPK * kv:HPK * kv + HPK, b * P:(b + 1) * P], gr,
                                ps[:, 6, :].rearrange("p (h q) -> p h q", q=P), ALU.mult).then_inc(s_a_o, 1)

            queries(0)
            for i in range(2 * LT):
                group(i)
            for j in range(2 * LT):
                half, t = divmod(j, LT)
                dve.wait_ge(s_z_mm, j + 1)
                if j >= 2:
                    dve.wait_ge(s_z_ok, j - 1)
                v.tensor_tensor(otmp[:, j % 2], ps[:, j % 4, :], gtb[:, 0, half * 512:half * 512 + 512], ALU.mult).then_inc(s_z_t, 1)
            dve.wait_ge(s_ld_fin, 16)
            dve.wait_ge(s_fin_sq, LT)
            rsqrt(5, ssq, msq, rstd, 1.0 / D)
            for t in range(LT):
                v.scalar_tensor_tensor(out=xr[:, t], in0=xr[:, t], scalar=rstd[:, t:t + 1], in1=fgb,
                                       op0=ALU.mult, op1=ALU.mult).then_inc(s_fin_g, 1)

        @block.tensor
        def _(pe):
            te = nc.tensor

            def arrived(kind, b):
                u = (kind, b)
                pe.wait_ge(w_in[place[u] % NSLOT], 16 * (place[u] // NSLOT + 1))
                return u

            def tr(o, i):
                m = i.shape[0]
                return te.transpose(o, i, ident[0:m, 0:m])

            pe.wait_ge(s_ld_const, 16 * 8)
            tr(ps[:, 3, 0:NCOL], colrow[0:NCOL]).then_inc(s_par_tr, 1)
            pe.wait_ge(s_ld_par, 16 * 7)
            pe.wait_ge(s_lraw_ok, 1)
            for k in range(3):
                last = tr(ps[:, 0, 32 * k:32 * k + 32], lraw[0:G, k])
            last.then_inc(s_par_tr, 1)
            for r in range(2):
                for q in range(4):
                    last = tr(ps[:, 1 + r, P * q:P * q + P], craw[:, r, q])
                last.then_inc(s_par_tr, 1)

            def modulation(kind, b0, b1, bank):
                for b in range(b0, b1):
                    u = arrived(kind, b)
                    for f in range(4):
                        o = 2 * (4 * b + f)
                        for k in range(KT):
                            last = te.matmul(ps[:, bank, o:o + 2], slot_kn(u)[:, k, P * f:P * f + P], cond[:, k],
                                             start=k == 0, stop=k == KT - 1)
                    last.then_inc(s_mod_mm, 1)

            pe.wait_ge(s_cond_ok, 1)
            modulation("mod0", 0, 4, 4)

            def to_features(l, Xr):
                for q, (t0, nt) in enumerate(CHUNKS):
                    for k in range(KT):
                        j = KT * q + k
                        if j >= 4:
                            pe.wait_ge(s_h_evd if j % 2 else s_h_eva, 12 * l + (j - 4) // 2 + 1)
                        for t in range(nt // P):
                            if k == 0:
                                pe.wait_ge(s_xn, TT * l + t0 // P + t + 1)
                            last = tr(ps[:, j % 4, t * P:t * P + P], Xr[:, t0 // P + t, P * k:P * k + P])
                        last.then_inc(s_h_tr, 1)

            pe.wait_ge(s_par_ok, 1)
            to_features(0, X)

            def token_major(u, bank, lhs, signal):
                for k in range(KT):
                    last = te.matmul(ps[:, bank, :], lhs(k), slot_kn(u)[:, k], start=k == 0, stop=k == KT - 1)
                last.then_inc(signal, 1)

            pe.wait_ge(s_h_eva, 12)
            pe.wait_ge(s_h_evd, 12)
            pe.wait_ge(s_mod_ok, 1)
            u = arrived("v", 0)
            for t in range(TT):
                if t >= 4:
                    pe.wait_ge(s_v_ev, t - 3)
                token_major(u, 4 + t % 4, lambda k: hT0[:, k, t * P:t * P + P], s_v_mm)
            for j in range(16):
                r, q = divmod(j, 8)
                pe.wait_ge(s_bl_ok, 4)
                if j >= 4:
                    pe.wait_ge(s_bl_ev, j - 3)
                for m in range(4):
                    last = tr(ps[:, j % 4, P * m:P * m + P], BL[:, r, 4 * q + m].rearrange("p s h -> p (s h)"))
                last.then_inc(s_bl_tr, 1)

            def lags(half):
                pe.wait_ge(s_cl_ok, half + 1)
                if half:
                    pe.wait_ge(s_k_ev, 4 * half)
                else:
                    pe.wait_ge(s_bl_ev, 16)
                for q in range(4):
                    for m in range(4):
                        gl, g = 4 * q + m, 16 * half + 4 * q + m
                        base = P * m
                        for r in range(2):
                            te.matmul(ps[0:HC, q, base:base + HC], BB[:, r, g], Cx[:, r, g], start=r == 0, stop=r == 1)
                        for d in range(2):
                            rows, o = slice(d * NS, (d + 1) * NS), base + (HC if d == 0 else 0)
                            for r in range(2):
                                last = te.matmul(ps[32 * d:32 * d + HC, q, o:o + 7 * HC], BB[rows, r, g],
                                                 CL[rows, r, gl, 1:8].rearrange("p k o -> p (k o)"), start=r == 0, stop=r == 1)
                    last.then_inc(s_k_mm, 1)

            lags(0)
            u = arrived("xs", 0)
            pe.wait_ge(s_v_ev, TT)
            for s in range(CH):
                if s >= 4:
                    pe.wait_ge(s_xs_eva, s - 3)
                token_major(u, 4 + s % 4, lambda k: hT0[:, k, NCTX + s:TOK:CH], s_xs_mm)
            pe.wait_ge(s_hperm_ok, 1)
            for j in range(2):
                pe.wait_ge(s_xs_eva, 5 + j)
                token_major(u, 4 + j, lambda k: hperm[:, k, P * j:P * j + P], s_xs_mm)
            lags(1)
            pe.wait_ge(s_xs_evd, 8)
            pe.wait_ge(s_xs_eva, 8)
            modulation("mod0", 4, 6, 4)
            pe.wait_ge(s_ld_ws, 32)
            for g in range(4):
                last = tr(ps[:, 5, P * g:P * g + P], wsraw[:, g])
            last.then_inc(s_ws_tr, 1)
            pe.wait_ge(s_k_ev, 8)
            for j in range(11):
                if j >= 4:
                    pe.wait_ge(s_u_ev, j - 3)
                for m in range(min(3, G - 3 * j)):
                    g = 3 * j + m
                    tr(ps[:, j % 4, NCH * m:NCH * m + CCH], Yc[0:CCH, g].rearrange("p s c -> p (s c)"))
                    last = tr(ps[:, j % 4, NCH * m + CCH:NCH * (m + 1)], Yl[:, g].rearrange("p s c -> p (s c)"))
                last.then_inc(s_u_tr, 1)
            pe.wait_ge(s_u_ev, 11)
            for j in range(32):
                q, r = divmod(j, 2)
                u = arrived("bop", q // 8)
                op = slot(u).rearrange("p (r g m) -> p r g m", r=2, m=P)
                if j >= 4:
                    pe.wait_ge(s_b_evf, j - 3)
                    pe.wait_ge(s_b_evb, 2 * (j - 3) + 1)
                for m in range(2):
                    last = te.matmul(ps[:, j % 4, NCH * m:NCH * (m + 1)], op[:, r, (2 * q + m) % 16], U[:, 2 * q + m],
                                     start=True, stop=True)
                last.then_inc(s_b_mm, 1)

            def gt_rows(l, c, bank, signal):
                for half in range(2):
                    for m in range(4):
                        k = 16 + 4 * half + m
                        last = tr(ps[:, bank + half, P * m:P * m + P], modc[l][:, k, c:c + 1].broadcast_to([P, P]))
                    last.then_inc(signal, 1)

            pe.wait_ge(s_par_dead, 1)
            gt_rows(0, 0, 4, s_gt_tr)
            gt_rows(0, 1, 6, s_gt_tr)
            pe.wait_ge(s_b_evf, 32)
            pe.wait_ge(s_b_evb, 65)
            for part, kind in enumerate(("u", "ga", "gb")):
                u = arrived(kind, 0)
                for fb in range(FB):
                    for q, (t0, nt) in enumerate(CHUNKS):
                        j = 12 * part + 3 * fb + q
                        if j >= 4:
                            pe.wait_ge(s_f_ev, j - 3)
                        for k in range(KT):
                            last = te.matmul(ps[:, j % 4, 0:nt], slot_kn(u)[:, k, P * fb:P * fb + P], hT0[:, k, t0:t0 + nt],
                                             start=k == 0, stop=k == KT - 1)
                        last.then_inc(s_f_mm, 1)
            pe.wait_ge(s_gt_ev, 4)
            pe.wait_ge(s_vg_ok, TT)
            pe.wait_ge(s_ws_ev, 1)
            for t in range(TT):
                if t >= 4:
                    pe.wait_ge(s_gm_ok, t - 3)
                for g in range(FB):
                    last = te.matmul(ps[:, 4 + t % 4, P * g:P * g + P], vt[:, t, P * g:P * g + P], wsT[:, g], start=True, stop=True)
                last.then_inc(s_gm_mm, 1)
            pe.wait_ge(s_f_ev, 36)
            modulation("mod1", 0, 6, 0)
            pe.wait_ge(s_gm_ok, TT)
            pe.wait_ge(s_hn_f, 2)
            pe.wait_ge(s_hn_b, 4)
            for j in range(16):
                u = arrived("ct", j // 4)
                op = slot(u)[:, 0:3072].rearrange("p (r g m) -> p r g m", r=3, m=P)
                if j >= 4:
                    pe.wait_ge(s_c_ev, j - 3)
                for m in range(2):
                    g, gl = 2 * j + m, (2 * j + m) % 8
                    o = ps[:, 4 + j % 4, NCH * m:NCH * (m + 1)]
                    te.matmul(o, op[:, 2, gl], U[:, g], start=True, stop=False)
                    te.matmul(o, op[:, 0, gl], Hn[:, 0, g], start=False, stop=False)
                    last = te.matmul(o, op[:, 1, gl], Hn[:, 1, g], start=False, stop=True)
                last.then_inc(s_c_mm, 1)
            pe.wait_ge(s_mod_ok, 2)
            pe.wait_ge(s_c_ev, 16)
            for j in range(8):
                if j >= 2:
                    pe.wait_ge(s_y1_eva, j - 1)
                    pe.wait_ge(s_y1_evd, j - 1)
                bk = 2 * (j % 2)
                for m in range(4):
                    last = tr(ps[:, bk, P * m:P * m + P], ys[:, 4 * j + m, CCH:NCH])
                last.then_inc(s_y1_tr, 1)
                for m in range(4):
                    last = tr(ps[0:CCH, bk + 1, P * m:P * m + P], ys[:, 4 * j + m, 0:CCH])
                last.then_inc(s_y1_tr, 1)
            pe.wait_ge(s_y1_eva, 8)
            pe.wait_ge(s_y1_evd, 8)
            for j in range(8):
                fb, q = divmod(j, 2)
                if j >= 4:
                    pe.wait_ge(s_y2_eva, j - 3)
                for m in range(4):
                    last = tr(ps[:, 4 + j % 4, P * m:P * m + P], Yt[:, 4 * q + m, P * fb:P * fb + P])
                last.then_inc(s_y2_tr, 1)
            for j in range(4):
                pe.wait_ge(s_y2_eva, 5 + j)
                for s in range(CH):
                    last = tr(ps[:, 4 + j, CCH * s:CCH * s + CCH], Ytc[0:CCH, s, P * j:P * j + P])
                last.then_inc(s_y2_tr, 1)
            u = arrived("glu", 0)
            wg = slot(u)[:, 0:2048].rearrange("p (k n) -> p k n", n=512)
            pe.wait_ge(s_y2_eva, 8)
            pe.wait_ge(s_y2_evd, 4)
            for j in range(12):
                fb, q = divmod(j, 3)
                t0, nt = CHUNKS[q]
                if j >= 4:
                    pe.wait_ge(s_glu_ok, j - 3)
                for k in range(FB):
                    last = te.matmul(ps[:, j % 4, 0:nt], wg[:, k, P * fb:P * fb + P], yT[:, k, t0:t0 + nt],
                                     start=k == 0, stop=k == FB - 1)
                last.then_inc(s_glu_mm, 1)
            pe.wait_ge(s_gm_ok, TT)
            pe.wait_ge(s_glu_ok, 12)
            for half in range(2):
                u = arrived("out0", half)
                for t in range(TT):
                    j = TT * half + t
                    if j >= 4:
                        pe.wait_ge(s_o_t, j - 3)
                    token_major(u, 4 + j % 4, lambda k: mixT[:, k, t * P:t * P + P], s_o_mm)

            to_features(1, x1)
            pe.wait_ge(s_o_t, 2 * TT)
            pe.wait_ge(s_h_eva, 24)
            pe.wait_ge(s_h_evd, 24)
            u = arrived("kv", 0)
            for t in range(TT):
                if t >= 4:
                    pe.wait_ge(s_kv_ev, 2 * (t - 3))
                token_major(u, 4 + t % 4, lambda k: hT1[:, k, t * P:t * P + P], s_kv_mm)
            for half in range(2):
                u = arrived("q", half)
                for t in range(LT):
                    j = LT * half + t
                    if j >= 4:
                        pe.wait_ge(s_q_ev, j - 3)
                    token_major(u, j % 4, lambda k: hT1[:, k, NCTX + t * P:NCTX + t * P + P], s_q_mm)
            pe.wait_ge(s_q_ev, 2 * LT)
            for j in range(2 * NH):
                h, q = divmod(j, 2)
                u = arrived("gate", h // 4)
                if j >= 4:
                    pe.wait_ge(s_g_ev, j - 3)
                for k in range(KT):
                    last = te.matmul(ps[:, j % 4, :], slot_kn(u)[:, k, P * (h % 4):P * (h % 4) + P],
                                     hT1[:, k, NCTX + 512 * q:NCTX + 512 * q + 512], start=k == 0, stop=k == KT - 1)
                last.then_inc(s_g_mm, 1)
            pe.wait_ge(s_k_ok, 1)
            pe.wait_ge(s_kv_ev, 2 * TT)
            for j in range(6):
                h, q = divmod(j, 3)
                if j >= 4:
                    pe.wait_ge(s_kt_ev, j - 3)
                for t in range(4 * q, min(4 * q + 4, TT)):
                    last = tr(ps[:, 4 + j % 4, P * (t - 4 * q):P * (t - 4 * q) + P], Kraw[:, t, HD * h:HD * h + HD])
                last.then_inc(s_kt_tr, 1)
            pe.wait_ge(s_kt_ev, 4)
            gt_rows(1, 0, 6, s_kt_tr)
            pe.wait_ge(s_kt_ev, 8)
            pe.wait_ge(s_g_ev, 2 * NH)

            def q_transposes(i):
                pe.wait_ge(s_a_qs, i + 1)
                if i:
                    pe.wait_ge(s_a_gr, i)
                for h in range(HPK):
                    last = tr(ps[:, 7, P * h:P * h + P], qs[:, HD * h:HD * h + HD])
                last.then_inc(s_a_qT, 1)

            def scores(m):
                i, h = divmod(m, HPK)
                if h == 0:
                    pe.wait_ge(s_a_q, i + 1)
                if m:
                    pe.wait_ge(s_a_p, m)
                for b, (t0, nt) in enumerate(((0, 512), (512, 512), (1024, 256))):
                    last = te.matmul(ps[:, b, 0:nt], qT[:, h], KTt[:, i % 2, t0:t0 + nt], start=True, stop=True)
                last.then_inc(s_a_s, 1)

            def p_transposes(m):
                pe.wait_ge(s_a_p, m + 1)
                if m:
                    pe.wait_ge(s_a_tea, m)
                    pe.wait_ge(s_a_ted, m)
                for t in range(TT):
                    last = tr(ps[:, 3 + t // 4, P * (t % 4):P * (t % 4) + P], Pr[:, P * t:P * t + P])
                last.then_inc(s_a_t, 1)

            def sums(i):
                pe.wait_ge(s_a_ri, i + 1)
                for h in range(HPK):
                    last = tr(ps[:, 7, P * h:P * h + P], rinv[:, h:h + 1].broadcast_to([P, P]))
                last.then_inc(s_a_rt, 1)

            def values(i):
                pe.wait_ge(s_a_tea, HPK * (i + 1))
                pe.wait_ge(s_a_ted, HPK * (i + 1))
                if i:
                    pe.wait_ge(s_a_o, i)
                for t in range(TT):
                    last = te.matmul(ps[:, 6, :], Vt[:, t, HD * (i % 2):HD * (i % 2) + HD], PT[:, t],
                                     start=t == 0, stop=t == TT - 1)
                last.then_inc(s_a_pv, 1)

            q_transposes(0)
            scores(0)
            for i in range(2 * LT):
                for h in range(HPK):
                    m = HPK * i + h
                    if h < HPK - 1:
                        scores(m + 1)
                    p_transposes(m)
                sums(i)
                if i + 1 < 2 * LT:
                    q_transposes(i + 1)
                    scores(HPK * (i + 1))
                values(i)
            pe.wait_ge(s_a_o, 2 * LT)
            for half in range(2):
                u = arrived("out1", half)
                for t in range(LT):
                    j = LT * half + t
                    if j >= 4:
                        pe.wait_ge(s_z_t, j - 3)
                    token_major(u, j % 4, lambda k: OT[:, k, t * P:t * P + P], s_z_mm)


_ROPE = (np.arange(SEQ)[:, None] // 64, np.arange(SEQ)[:, None] % 64)


def kernel(**inputs):
    import concourse.bacc as bacc
    from concourse.bass_utils import run_bass_kernel_spmd

    nc = bacc.Bacc("TRN2", target_bir_lowering=False, num_devices=1, dynamic_dma_scratch_size=64)
    arrays, args = {}, []

    def declare(name, a):
        arrays[name] = a
        args.append(nc.dram_tensor(name, a.shape, mybir.dt.from_np(a.dtype), kind="ExternalInput").ap())

    names = ["x", "c", "ctx", "c_ctx", "norm_g", "w_mod", "b_mod", "we_in", "we_out", "gm_v_g", "gm_w_s", "gm_b_s",
             "s5_lam_re", "s5_lam_im", "s5_log_dt", "s5_b_re", "s5_b_im", "s5_c_re", "s5_c_im", "s5_d",
             "s5_w_glu", "s5_b_glu", "wo_in", "wo_out", "q_norm_g", "k_norm_g", "final_g"]
    for name in names:
        declare(f"in_{name}", np.ascontiguousarray(inputs[name]))
    freqs = 10000.0 ** (-np.arange(HD // 4, dtype=np.float32) / np.float32(HD // 4))
    ang = np.concatenate([(p.astype(np.float32) * freqs).astype(np.float32) for p in _ROPE], axis=1)
    declare("identity", np.eye(P, dtype=np.float32))
    declare("rope_cos", np.cos(ang).astype(np.float32))
    declare("rope_sin", np.sin(ang).astype(np.float32))
    out = nc.dram_tensor("out", (1, SEQ, D), F32, kind="ExternalOutput").ap()
    build(nc, *args, out)
    r = run_bass_kernel_spmd(nc, [arrays], core_ids=[0])
    return r.results[0]["out"]
```

```python
import math
from contextlib import ExitStack

import numpy as np

from concourse import mybir

F32 = mybir.dt.float32
F32R = mybir.dt.float32r
I32 = mybir.dt.int32
ACT = mybir.ActivationFunctionType
ALU = mybir.AluOpType
AX = mybir.AxisListType

P = 128
D = 1024
KT = D // P
NCTX, SEQ = 256, 1024
TOK = NCTX + SEQ
CT, LT = NCTX // P, SEQ // P
TT = CT + LT
EPS = 1e-6
W = 512
FB = W // P
CH = 8
G = 32
HC = 16
NS = 64
NCH = TOK // CH
CCH = NCTX // CH
HD = 128
NH = 8
NKV = 2
HPK = NH // NKV
SLOT = 4096
NSLOT = 3
CHUNKS = [(0, 256), (256, 512), (768, 512)]
LN2_HI, LN2_LO = 0.693359375, -2.12194440e-4
PIO2 = (1.5703125, 4.83751296997e-4, 7.54978995489e-8)


def build(nc, x, c, ctx_in, c_ctx, norm_g, w_mod, b_mod, we_in, we_out, gm_v_g, gm_w_s, gm_b_s,
          s5_lam_re, s5_lam_im, s5_log_dt, s5_b_re, s5_b_im, s5_c_re, s5_c_im, s5_d,
          s5_w_glu, s5_b_glu, wo_in, wo_out, q_norm_g, k_norm_g, final_g,
          ident_in, cos_in, sin_in, out):
    with ExitStack() as es:
        def sb(name, n, dt=F32):
            return es.enter_context(nc.sbuf_tensor(name, [P, n], dt))

        def sem(name):
            return es.enter_context(nc.semaphore(name))

        bop_d = nc.dram_tensor("bop_scratch", (2, P, 2, 16, P), F32, kind="Internal").ap()
        ct_d = nc.dram_tensor("cop_t_scratch", (4, P, 3, 8, P), F32, kind="Internal").ap()
        x1_d = nc.dram_tensor("x1_scratch", (SEQ, D), F32, kind="Internal").ap()

        def region(name, n, rounded):
            got = []
            with ExitStack() as own:
                at = 0
                for part, offset, words in rounded:
                    if offset > at:
                        own.enter_context(nc.sbuf_tensor(f"{name}_skip{at}", [P, offset - at], F32))
                    got.append(own.enter_context(nc.sbuf_tensor(part, [P, words], F32R)))
                    at = offset + words
            return [sb(name, n)] + got

        RA, = region("region_a", 10240, [])
        RB, ones_r, KTh, KTl = region("region_b", 10240, [("ones_r", 1152, P), ("k_t_hi", 5120, 2560), ("k_t_lo", 7680, 2560)])
        RC, nm = region("region_c", 10240, [("neg_max", 9216, 1024)])
        RD, qTh, qTl = region("region_d", (NCH + 1) * 2 * G, [("q_t_hi", 8192, 1024), ("q_t_lo", 9216, 1024)])
        ring = sb("weight_ring", NSLOT * SLOT)
        shared = sb("shared", 3072)
        ident = sb("ident", P)
        small = sb("small", 336)
        L8 = sb("lam8", P)
        rt = sb("rec_tmp", P)
        ps = es.enter_context(nc.psum_tensor("ps", [P, 8, 512], F32))

        def cutter(region, end):
            at = [0]

            def cut(n):
                a = region[:, at[0]:at[0] + n]
                at[0] += n
                assert at[0] <= end
                return a
            return cut

        sm = cutter(small, 336)
        NCOL = 84
        colv = sm(NCOL)
        cond = colv[:, 0:16].rearrange("p (c k) -> p k c", c=2)
        bmod = [colv[:, 16 + 24 * l:40 + 24 * l] for l in range(2)]
        ng = [colv[:, 64 + 8 * l:72 + 8 * l] for l in range(2)]
        bglu = colv[:, 80:84]
        modc = [sm(48).rearrange("p (b c) -> p b c", c=2) for _ in range(2)]
        hA = [sm(16).rearrange("p (k c) -> p k c", c=2) for _ in range(2)]
        ssq, msq, rstd = sm(10), sm(10), sm(10)
        smax = sm(8).rearrange("p (i h) -> p i h", i=2)
        epsc = sm(1)
        bnst = sm(6)
        mv = sm(20).rearrange("p (t a) -> p t a", a=2)

        X = RA[:, :].rearrange("p (t f) -> p t f", f=D)
        vt = RA[:, 0:5120].rearrange("p (t f) -> p t f", f=W)
        Tsb = RA[:, 5120:9216].rearrange("p (g m) -> p g m", m=P)
        dskip = RA[:, 9216:9728].rearrange("p (g h) -> p g h", h=HC)
        wsraw = RA[:, 9728:10240].rearrange("p (g q) -> p g q", g=4)
        U = RA[:, 5120:10240].rearrange("p (g n) -> p g n", n=NCH)
        hT1 = RA[:, :].rearrange("p (k t) -> p k t", t=TOK)
        xr = RA[:, 0:8192].rearrange("p (t f) -> p t f", f=D)
        PT = RA[:, 5120:10240].rearrange("p (s q) -> p s q", q=512)

        hT0 = RB[:, :].rearrange("p (k t) -> p k t", t=TOK)
        Hn = RB[:, :].rearrange("p (r g n) -> p r g n", r=2, n=NCH)
        Yt = RB[:, 0:4096].rearrange("p (s f) -> p s f", f=W)
        Ytc = RB[:, 4096:8192].rearrange("p (s f) -> p s f", f=W)
        x1 = RB[:, :].rearrange("p (t f) -> p t f", f=D)
        Kraw = RB[:, 0:2560].rearrange("p (t f) -> p t f", f=256)
        GR = RB[:, 0:512]
        ri = RB[:, 512:1024]
        ones = RB[:, 1024:1152]
        Vt = RB[:, 2560:5120].rearrange("p (t f) -> p t f", f=256)
        fjunk = RB[:, 5120:6144]
        KTh, KTl = (q[:, :].rearrange("p (j t) -> p j t", t=TOK) for q in (KTh, KTl))

        lraw = RC[:, 0:384].rearrange("p (a m) -> p a m", a=3)
        ldraw = RC[:, 384:386]
        colrow = RC[:, 1536:1664]
        craw = RC[:, 512:1536].rearrange("p (r q m) -> p r q m", r=2, m=P)
        BL = RC[:, 0:8192].rearrange("p (r g s h) -> p r g s h", r=2, g=G, h=HC)
        btmp = RC[:, 8192:9216].rearrange("p (g s h) -> p g s h", g=8, h=HC)
        bstage = RC[:, 9216:10240].rearrange("p (a m) -> p a m", a=2)
        Yl = RC[:, 0:4096].rearrange("p (g s c) -> p g s c", s=CH, c=HC)
        Yc = RC[:, 4096:8192].rearrange("p (g s c) -> p g s c", s=CH, c=HC)
        hperm = RC[:, 8192:10240].rearrange("p (k t) -> p k t", t=NCTX)
        mixT = RC[:, :].rearrange("p (k t) -> p k t", t=TOK)
        Qt = RC[:, 0:8192].rearrange("p (t f) -> p t f", f=D)
        rope_t = [RC[:, 8192 + 512 * i:8704 + 512 * i] for i in range(2)]
        cs = RC[:, 9216:10240].rearrange("p (a t m) -> p a t m", a=2, m=64)
        OT = RC[:, 0:8192].rearrange("p (t h q) -> p t h q", h=NH, q=P)
        psum_p = RC[:, 8192:9216].rearrange("p (i n) -> p i n", i=2)
        nm = nm[:, :].rearrange("p (i n) -> p i n", i=2)

        braw = RD[:, 0:1024].rearrange("p (r g h) -> p r g h", r=2, h=HC)
        cltmp = RD[:, 0:576].rearrange("p (g k o) -> p g k o", g=4, o=HC)
        BB = RD[:, 1024:2048].rearrange("p (r g h) -> p r g h", r=2, h=HC)
        Cx = RD[:, 2048:3072].rearrange("p (r g h) -> p r g h", r=2, h=HC)
        Kt = RD[:, 3072:5120].rearrange("p (g k o) -> p g k o", k=CH, o=HC)
        CL = RD[:, 5120:9728].rearrange("p (r g k o) -> p r g k o", r=2, g=16, o=HC)
        ctmp = RD[:, 9728:10240]
        vgb = RD[:, 9728:10240]
        ddtmp = RD[:, 10240:10304].rearrange("p (g o) -> p g o", o=HC)
        H = RD[:, :].rearrange("p (i r g) -> p i r g", r=2, g=G)
        ys = RD[:, 0:5120].rearrange("p (g n) -> p g n", n=NCH)
        yT = RD[:, 5120:10240].rearrange("p (k t) -> p k t", t=TOK)
        otmp = RD[:, 0:1024].rearrange("p (a n) -> p a n", a=2)
        gateT = RD[:, 0:8192].rearrange("p (h t) -> p h t", t=SEQ)
        qjunk = RD[:, 8192:8704]
        qTh, qTl = (q[:, :].rearrange("p (i h q) -> p i h q", i=2, q=P) for q in (qTh, qTl))

        shc = cutter(shared, 3072)
        lamr, lami, ldt = shc(G), shc(G), shc(G)
        s5t = [shc(G) for _ in range(24)]
        ki, kj = shc(G).bitcast(I32), shc(G).bitcast(I32)
        LP = shc(9 * 64).rearrange("p (k r g) -> p k r g", r=2, g=G)
        LPc = shc(9 * 64).rearrange("p (k r g) -> p k r g", r=2, g=G)
        LPb = shc(8 * 64).rearrange("p (k r g) -> p k r g", r=2, g=G)
        gtb = shared[:, 0:2048].rearrange("p (c f) -> p c f", c=2)
        wsT = shared[:, 2048:2560].rearrange("p (g q) -> p g q", g=4)
        bsb = shared[:, 2560:3072]
        fgb = shared[:, 1024:2048]
        qss, qms, qrs = (shared[:, 2048 + 84 * i:2132 + 84 * i] for i in range(3))

        s_ld_const, s_ld_par, s_ld_b, s_ld_v, s_ld_ws, s_ld_bs = (
            sem("ld_const"), sem("ld_par"), sem("ld_b"), sem("ld_v"), sem("ld_ws"), sem("ld_bs"))
        s_ld_tab, s_ld_gain, s_ld_fin, s_x1_out, s_stored = (
            sem("ld_tab"), sem("ld_gain"), sem("ld_fin"), sem("x1_out"), sem("stored"))
        s_x1_back = [sem(f"x1_back{i}") for i in range(2)]
        s_chain, s_pchain, s_lraw_ok, s_par_tr, s_par_ok, s_cond_ok = (
            sem("chain"), sem("pchain"), sem("lraw_ok"), sem("par_tr"), sem("par_ok"), sem("cond_ok"))
        s_col_ok, s_mod_mm, s_mod_ok, s_sq, s_rt_req, s_rt_ok = (
            sem("col_ok"), sem("mod_mm"), sem("mod_ok"), sem("sq"), sem("rt_req"), sem("rt_ok"))
        s_xn, s_h_tr, s_h_eva, s_h_evd, s_v_mm, s_v_ev = (
            sem("xn"), sem("h_tr"), sem("h_eva"), sem("h_evd"), sem("v_mm"), sem("v_ev"))
        s_vn_ok, s_vg_ok, s_bl_ok, s_bl_tr, s_bl_ev, s_cl_ok = (
            sem("vn_ok"), sem("vg_ok"), sem("bl_ok"), sem("bl_tr"), sem("bl_ev"), sem("cl_ok"))
        s_cop_out, s_k_mm, s_k_ev, s_t_in, s_t_out, s_par_dead = (
            sem("cop_out"), sem("k_mm"), sem("k_ev"), sem("t_in"), sem("t_out"), sem("par_dead"))
        s_hperm_ok, s_xs_mm, s_xs_eva, s_xs_evd, s_ws_tr, s_ws_ev = (
            sem("hperm_ok"), sem("xs_mm"), sem("xs_eva"), sem("xs_evd"), sem("ws_tr"), sem("ws_ev"))
        s_u_tr, s_u_ev, s_b_mm, s_b_evf, s_b_evb, s_gt_tr = (
            sem("u_tr"), sem("u_ev"), sem("b_mm"), sem("b_evf"), sem("b_evb"), sem("gt_tr"))
        s_gt_ev, s_rec, s_rec_ok, s_f_mm, s_f_ev, s_ga_ok = (
            sem("gt_ev"), sem("rec"), sem("rec_ok"), sem("f_mm"), sem("f_ev"), sem("ga_ok"))
        s_gm_mm, s_gm_ok, s_hn_f, s_hn_b, s_c_mm, s_c_ev = (
            sem("gm_mm"), sem("gm_ok"), sem("hn_f"), sem("hn_b"), sem("c_mm"), sem("c_ev"))
        s_y1_tr, s_y1_eva, s_y1_evd, s_y2_tr, s_y2_eva, s_y2_evd = (
            sem("y1_tr"), sem("y1_eva"), sem("y1_evd"), sem("y2_tr"), sem("y2_eva"), sem("y2_evd"))
        s_glu_mm, s_glu_sg, s_glu_y, s_glu_ok, s_o_mm, s_o_t = (
            sem("glu_mm"), sem("glu_sg"), sem("glu_y"), sem("glu_ok"), sem("o_mm"), sem("o_t"))
        s_o_ok, s_kv_mm, s_kv_ev, s_q_mm, s_q_ev, s_g_mm = (
            sem("o_ok"), sem("kv_mm"), sem("kv_ev"), sem("q_mm"), sem("q_ev"), sem("g_mm"))
        s_g_ev, s_k_ok, s_q_ok, s_kt_tr, s_kt_hi, s_kt_lo = (
            sem("g_ev"), sem("k_ok"), sem("q_ok"), sem("kt_tr"), sem("kt_hi"), sem("kt_lo"))
        s_gt1_tr, s_gt1_ev, s_hd_sq, s_hd_rt, s_ones = (
            sem("gt1_tr"), sem("gt1_ev"), sem("hd_sq"), sem("hd_rt"), sem("ones"))
        s_a_qT, s_a_qh, s_a_ql, s_a_mx, s_a_max, s_a_nt, s_a_nm = (
            sem("a_qT"), sem("a_qh"), sem("a_ql"), sem("a_mx"), sem("a_max"), sem("a_nt"), sem("a_nm"))
        s_a_s, s_a_p, s_a_sum, s_a_sm, s_a_gr, s_a_pv, s_a_o = (
            sem("a_s"), sem("a_p"), sem("a_sum"), sem("a_sm"), sem("a_gr"), sem("a_pv"), sem("a_o"))
        s_z_mm, s_z_t, s_z_ok, s_fin_sq, s_fin_rt, s_fin_g = (
            sem("z_mm"), sem("z_t"), sem("z_ok"), sem("fin_sq"), sem("fin_rt"), sem("fin_g"))
        s_bop_out = [sem(f"bop_out{i}") for i in range(2)]
        ld_x, ld_x2 = ([sem(f"{n}_{i}") for i in range(5)] for n in ("ld_x", "ld_x2"))
        w_in = [sem(f"w_in{i}") for i in range(NSLOT)]

        uses = [("mod0", b) for b in range(4)]
        uses += [("v", 0), ("xs", 0), ("mod0", 4), ("mod0", 5), ("bop", 0), ("bop", 1), ("u", 0), ("ga", 0), ("gb", 0)]
        uses += [("mod1", b) for b in range(6)] + [("ct", q) for q in range(4)]
        uses += [("glu", 0), ("out0", 0), ("out0", 1), ("kv", 0), ("q", 0), ("q", 1), ("gate", 0), ("gate", 1),
                 ("out1", 0), ("out1", 1)]
        place = {u: i for i, u in enumerate(uses)}
        done_when = {("mod0", b): (s_mod_mm, b + 1) for b in range(6)} | {("mod1", b): (s_mod_mm, b + 7) for b in range(6)}
        done_when |= {("v", 0): (s_v_mm, TT), ("xs", 0): (s_xs_mm, CH + 2), ("u", 0): (s_f_mm, 12), ("ga", 0): (s_f_mm, 24),
                      ("gb", 0): (s_f_mm, 36), ("glu", 0): (s_glu_mm, 12), ("kv", 0): (s_kv_mm, TT)}
        for b in range(2):
            done_when |= {("bop", b): (s_b_mm, 16 * (b + 1)), ("out0", b): (s_o_mm, TT * (b + 1)),
                          ("q", b): (s_q_mm, LT * (b + 1)), ("gate", b): (s_g_mm, LT * (b + 1))}
        done_when |= {("ct", q): (s_c_mm, 4 * (q + 1)) for q in range(4)}
        source = {"v": (we_in, W), "xs": (we_in, 3 * W), "u": (we_in, 0), "ga": (we_in, 2 * W), "gb": (we_in, 4 * W),
                  "mod0": (w_mod[0:1], 0), "mod1": (w_mod[1:2], 0), "out0": (we_out, 0), "out1": (wo_out, 0),
                  "kv": (wo_in, D), "q": (wo_in, 0), "gate": (wo_in, D + 512)}

        def slot(u):
            i = place[u] % NSLOT
            return ring[:, i * SLOT:(i + 1) * SLOT]

        def slot_kn(u):
            return slot(u).rearrange("p (k n) -> p k n", n=512)

        block = es.enter_context(nc.Block())

        @block.sync
        def _(sp):
            def ring_load(kind, b):
                u = (kind, b)
                i = place[u]
                if i >= NSLOT:
                    sp.wait_ge(*done_when[uses[i - NSLOT]])
                dst = slot(u)
                if kind == "bop":
                    if b == 0:
                        sp.wait_ge(s_bop_out[0], 16 * 8)
                        sp.wait_ge(s_bop_out[1], 16 * 8)
                    src = bop_d[b].rearrange("p r g m -> p (r g m)")
                elif kind == "ct":
                    if b == 0:
                        sp.wait_ge(s_cop_out, 16 * 16)
                        sp.wait_ge(s_t_out, 16 * 4)
                    dst, src = dst[:, 0:3072], ct_d[b].rearrange("p r g m -> p (r g m)")
                elif kind == "glu":
                    dst = dst[:, 0:2048].rearrange("p (k n) -> p k n", n=512)
                    src = s5_w_glu[0].rearrange("(k p) n -> p k n", p=P)
                else:
                    wt, a = source[kind]
                    dst = dst.rearrange("p (k n) -> p k n", n=512)
                    src = wt[0][:, a + 512 * b:a + 512 * b + 512].rearrange("(k p) n -> p k n", p=P)
                sp.dma_start(dst, src).then_inc(w_in[i % NSLOT], 16)

            def token_loads(dst, name):
                sp.dma_start(dst[:, 0:CT, :], ctx_in[0].rearrange("(t p) f -> p t f", p=P)).then_inc(name[0], 16)
                for t in range(0, LT, 2):
                    sp.dma_start(dst[:, CT + t:CT + t + 2, :],
                                 x[0, t * P:(t + 2) * P, :].rearrange("(t p) f -> p t f", p=P)).then_inc(name[1 + t // 2], 16)

            sp.dma_start(ident[:], ident_in).then_inc(s_ld_const, 16)
            r0 = 0
            for rows in (c[0], c_ctx, b_mod[0], b_mod[1], norm_g[0], norm_g[1], s5_b_glu[0]):
                rows = rows.rearrange("(k p) -> k p", p=P)
                sp.dma_start(colrow[r0:r0 + rows.shape[0]], rows).then_inc(s_ld_const, 16)
                r0 += rows.shape[0]
            ring_load("mod0", 0)
            ring_load("mod0", 1)
            ring_load("mod0", 2)
            token_loads(X, ld_x)
            ring_load("mod0", 3)
            ring_load("v", 0)
            ring_load("xs", 0)
            ring_load("mod0", 4)
            sp.wait_ge(s_par_ok, 1)
            sp.dma_start(vgb, gm_v_g.broadcast_to([P, W])).then_inc(s_ld_v, 16)
            sp.wait_ge(s_h_tr, 24)
            sp.dma_start(dskip[0:HC].rearrange("p g h -> p (g h)"), s5_d.broadcast_to([HC, W])).then_inc(s_ld_ws, 16)
            sp.dma_start(wsraw, gm_w_s[0].rearrange("g p q -> p g q")).then_inc(s_ld_ws, 16)
            ring_load("mod0", 5)
            for j in range(16):
                r, q = divmod(j, 8)
                sp.wait_ge(s_bl_ev, j + 1)
                sp.dma_start(bop_d[q // 4, :, r, 4 * (q % 4):4 * (q % 4) + 4, :],
                             bstage[:, j % 2].rearrange("p (g m) -> p g m", m=P)).then_inc(s_bop_out[j % 2], 16)
            for half in range(2):
                sp.wait_ge(s_cl_ok, half + 1)
                for q in range(2):
                    for r in range(2):
                        for d in range(2):
                            rows, k0 = slice(d * NS, (d + 1) * NS), 1 - d
                            sp.dma_start(ct_d[2 * half + q, rows, r].rearrange("p g (s o) -> p g s o", o=HC),
                                         CL[rows, r, 8 * q:8 * q + 8, k0:k0 + CH, :]).then_inc(s_cop_out, 16)
                sp.wait_ge(s_k_ev, 4 * (half + 1))
                gs = slice(16 * half, 16 * half + 16)
                for s in range(CH):
                    rows = slice(HC * s, HC * s + HC)
                    sp.dma_start(Tsb[rows, gs, HC * s:P].rearrange("p g (k o) -> p g k o", o=HC),
                                 Kt[0:HC, :, 0:CH - s, :]).then_inc(s_t_in, 16)
                    if s:
                        sp.dma_start(Tsb[rows, gs, 0:HC * s].rearrange("p g (k o) -> p g k o", o=HC),
                                     Kt[32:32 + HC, :, 7 - s:7, :]).then_inc(s_t_in, 16)
                if half:
                    ring_load("bop", 0)
                sp.wait_ge(s_t_in, 16 * 15 * (half + 1))
                for q in range(2):
                    a = 16 * half + 8 * q
                    sp.dma_start(ct_d[2 * half + q, :, 2], Tsb[:, a:a + 8, :]).then_inc(s_t_out, 16)
            ring_load("bop", 1)
            sp.wait_ge(s_par_dead, 1)
            sp.dma_start(bsb, gm_b_s[0].rearrange("g (o q) -> o (g q)", o=1).broadcast_to([P, 512])).then_inc(s_ld_bs, 16)
            for u in uses[place[("u", 0)]:place[("out0", 0)] + 2]:
                ring_load(*u)
            sp.wait_ge(s_y2_tr, 12)
            token_loads(x1, ld_x2)
            ring_load("kv", 0)
            sp.wait_ge(s_o_mm, 2 * TT)
            sp.dma_start(cs[:, 0], cos_in.rearrange("(t p) m -> p t m", p=P)).then_inc(s_ld_tab, 16)
            sp.dma_start(cs[:, 1], sin_in.rearrange("(t p) m -> p t m", p=P)).then_inc(s_ld_tab, 16)
            sp.dma_start(L8[:], q_norm_g.broadcast_to([P, HD])).then_inc(s_ld_gain, 16)
            sp.dma_start(rt[:], k_norm_g.broadcast_to([P, HD])).then_inc(s_ld_gain, 16)
            sp.wait_ge(s_o_ok, 2 * TT)
            sp.dma_start(x1_d.rearrange("(t p) f -> p t f", p=P), x1[:, CT:TT, :]).then_inc(s_x1_out, 16)
            sp.dma_start(fgb, final_g.rearrange("(o f) -> o f", o=1).broadcast_to([P, D])).then_inc(s_ld_fin, 16)
            for u in uses[place[("q", 0)]:]:
                ring_load(*u)
            sp.wait_ge(s_x1_out, 16)
            sp.wait_ge(s_g_mm, 2 * NH)
            xd = x1_d.rearrange("(t p) f -> p t f", p=P)
            sp.dma_start(xr[:, 0:5], xd[:, 0:5]).then_inc(s_x1_back[0], 16)
            sp.wait_ge(s_a_pv, 2 * LT)
            sp.wait_ge(s_a_sum, 9 * 2 * LT)
            sp.dma_start(xr[:, 5:8], xd[:, 5:8]).then_inc(s_x1_back[1], 16)
            for t in range(LT):
                sp.wait_ge(s_fin_g, t + 1)
                sp.dma_start(out[0, t * P:(t + 1) * P, :], xr[:, t, :]).then_inc(s_stored, 16)
            sp.wait_ge(s_stored, 16 * LT)

        @block.gpsimd
        def _(pool):
            g = nc.gpsimd
            n = [0]

            def step(ins):
                n[0] += 1
                ins.then_inc(s_pchain, 1)
                pool.wait_ge(s_pchain, n[0])

            pool.wait_ge(s_par_ok, 1)
            for q in range(4):
                gs = slice(8 * q, 8 * q + 8)
                L = [LPb[:, :, r, gs].rearrange("p s g -> p g s").unsqueeze(3).broadcast_to([P, 8, CH, HC])
                     for r in range(2)]
                B = [BB[:, r, gs, :].unsqueeze(2).broadcast_to([P, 8, CH, HC]) for r in range(2)]
                step(g.tensor_tensor(BL[:, 0, gs], B[0], L[0], ALU.mult))
                step(g.tensor_tensor(btmp, B[1], L[1], ALU.mult))
                step(g.tensor_tensor(BL[:, 0, gs], BL[:, 0, gs], btmp, ALU.subtract))
                step(g.tensor_tensor(BL[:, 1, gs], B[0], L[1], ALU.mult))
                step(g.tensor_tensor(btmp, B[1], L[0], ALU.mult))
                g.tensor_tensor(BL[:, 1, gs], BL[:, 1, gs], btmp, ALU.add).then_inc(s_bl_ok, 1)
                pool.wait_ge(s_bl_ok, q + 1)
            pool.wait_ge(s_ld_v, 16)
            for t in range(TT):
                pool.wait_ge(s_vn_ok, t + 1)
                g.tensor_tensor(vt[:, t], vt[:, t], vgb, ALU.mult).then_inc(s_vg_ok, 1)
            j = 0
            for fb in range(FB):
                for t0, nt in CHUNKS:
                    pool.wait_ge(s_f_ev, 12 + j + 1)
                    g.tensor_tensor(mixT[:, fb, t0:t0 + nt], mixT[:, fb, t0:t0 + nt], mixT[:, FB + fb, t0:t0 + nt],
                                    ALU.mult).then_inc(s_ga_ok, 1)
                    j += 1
            j = 0
            for half in range(2):
                for t in range(TT):
                    pool.wait_ge(s_o_t, j + 1)
                    if half == 0:
                        pool.wait_ge(ld_x2[t // 2], 16)
                    xs_ = x1[:, t, half * 512:half * 512 + 512]
                    g.tensor_tensor(xs_, xs_, otmp[:, j % 2], ALU.add).then_inc(s_o_ok, 1)
                    j += 1
            for i in range(2 * LT):
                for t in range(1, TT):
                    pool.wait_ge(s_a_p, TT * i + t + 1)
                    if t == 1 and i >= 2:
                        pool.wait_ge(s_a_sm, i - 1)
                    if t >= 2:
                        pool.wait_ge(s_a_sum, 9 * i + t - 1)
                    g.tensor_tensor(psum_p[:, i % 2], PT[:, 0] if t == 1 else psum_p[:, i % 2], PT[:, t],
                                    ALU.add).then_inc(s_a_sum, 1)
            for j in range(2 * LT):
                t, half = divmod(j, 2)
                if j == 0:
                    pool.wait_ge(s_x1_back[0], 16)
                if t == 5:
                    pool.wait_ge(s_x1_back[1], 16)
                pool.wait_ge(s_z_t, j + 1)
                xs_ = xr[:, t, half * 512:half * 512 + 512]
                g.tensor_tensor(xs_, xs_, otmp[:, j % 2], ALU.add).then_inc(s_z_ok, 1)

        @block.scalar
        def _(act):
            a = nc.scalar

            def copy(o, i):
                return a.activation(o, i, ACT.Copy)

            for k, tensor in enumerate((s5_lam_re, s5_lam_im)):
                act.dma_start(lraw[0:G, k].rearrange("g (d p) -> g d p", d=2),
                              tensor[0].rearrange("d g p -> g d p")).then_inc(s_ld_par, 16)
            act.dma_start(ldraw[0:G], s5_log_dt[0].rearrange("d g -> g d"), allow_slow_non_contiguous=True).then_inc(s_ld_par, 16)
            for r, tensor in enumerate((s5_c_re, s5_c_im)):
                for d in range(2):
                    act.dma_start(craw[:, r, :, d * NS:(d + 1) * NS],
                                  tensor[0, d].rearrange("(q g) h p -> (g h) q p", q=4)).then_inc(s_ld_par, 16)
            for r, tensor in enumerate((s5_b_re, s5_b_im)):
                for d in range(2):
                    act.dma_start(braw[d * NS:(d + 1) * NS, r],
                                  tensor[0, d].rearrange("g p h -> p g h")).then_inc(s_ld_b, 16)

            def root(i):
                act.wait_ge(s_rt_req, i)
                a.activation(rstd, msq, ACT.Sqrt).then_inc(s_rt_ok, 1)

            def squares(l, Xr, junk, ready):
                for t in range(TT):
                    ready(t)
                    a.activation(junk, Xr[:, t], ACT.Square, accum_out=ssq[:, t:t + 1]).then_inc(s_sq, 1)
                    act.wait_ge(s_sq, TT * l + t + 1)

            def h_evac(l, hT):
                for q, (t0, nt) in enumerate(CHUNKS):
                    ci = 1 if q == 0 else 0
                    for k in range(0, KT, 2):
                        j = KT * q + k
                        act.wait_ge(s_h_tr, 24 * l + j + 1)
                        a.activation(hT[:, k, t0:t0 + nt], ps[:, j % 4, 0:nt], ACT.Identity,
                                     bias=modc[l][:, k, ci:ci + 1], scale=hA[l][:, k, ci:ci + 1]).then_inc(s_h_eva, 1)

            act.wait_ge(s_col_ok, 1)
            a.activation(cond, cond, ACT.Silu).then_inc(s_cond_ok, 1)
            squares(0, X, RB[:, 0:D], lambda t: act.wait_ge(ld_x[t // 2], 16))
            root(1)
            act.wait_ge(s_mod_ok, 1)
            h_evac(0, hT0)
            for t in range(TT):
                act.wait_ge(s_v_mm, t + 1)
                copy(vt[:, t], ps[:, 4 + t % 4, :]).then_inc(s_v_ev, 1)
            for j in range(16):
                act.wait_ge(s_bl_tr, j + 1)
                if j >= 2:
                    act.wait_ge(s_bop_out[j % 2], 16 * (j // 2))
                copy(bstage[:, j % 2], ps[:, j % 4, :]).then_inc(s_bl_ev, 1)
            root(2)
            act.wait_ge(s_h_evd, 12)
            act.wait_ge(s_bop_out[0], 16 * 8)
            act.wait_ge(s_bop_out[1], 16 * 8)
            copy(hperm.rearrange("p k (s n) -> p k s n", s=CH),
                 hT0[:, :, 0:NCTX].rearrange("p k (n s) -> p k s n", s=CH)).then_inc(s_hperm_ok, 1)
            for s in range(CH):
                act.wait_ge(s_xs_mm, s + 1)
                copy(Yl[:, :, s, :], ps[:, 4 + s % 4, :].rearrange("p (g c) -> p g c", c=HC)).then_inc(s_xs_eva, 1)
            act.wait_ge(s_t_out, 16 * 4)
            act.wait_ge(s_ws_ev, 1)
            for j in range(11):
                m = min(3, G - 3 * j)
                act.wait_ge(s_u_tr, j + 1)
                copy(U[:, 3 * j:3 * j + m, :].rearrange("p g n -> p (g n)"), ps[:, j % 4, 0:m * NCH]).then_inc(s_u_ev, 1)
            act.wait_ge(s_cop_out, 16 * 16)
            act.wait_ge(s_t_in, 16 * 30)
            act.wait_ge(s_vg_ok, TT)
            for j in range(32):
                q, r = divmod(j, 2)
                act.wait_ge(s_b_mm, j + 1)
                copy(H[0:NS, 1:NCH + 1, r, 2 * q:2 * q + 2].rearrange("p n g -> p g n"),
                     ps[0:NS, j % 4, 0:2 * NCH].rearrange("p (g n) -> p g n", n=NCH)).then_inc(s_b_evf, 1)
            act.wait_ge(s_par_dead, 1)
            for j in range(4):
                act.wait_ge(s_gt_tr, j + 1)
                copy(gtb[:, j // 2, (j % 2) * 512:(j % 2) * 512 + 512], ps[:, 4 + j, :]).then_inc(s_gt_ev, 1)
            for part in range(3):
                for fb in range(FB):
                    for q, (t0, nt) in enumerate(CHUNKS):
                        j = 12 * part + 3 * fb + q
                        act.wait_ge(s_f_mm, j + 1)
                        if part == 2:
                            act.wait_ge(s_ga_ok, 3 * fb + q + 1)
                        a.activation(mixT[:, (FB if part else 0) + fb, t0:t0 + nt], ps[:, j % 4, 0:nt],
                                     ACT.Silu if part else ACT.Copy).then_inc(s_f_ev, 1)
            act.wait_ge(s_rec_ok, 1)
            for r in range(2):
                copy(Hn[0:NS, r], H[0:NS, 0:NCH, r, :].rearrange("p n g -> p g n")).then_inc(s_hn_f, 1)
            act.wait_ge(s_hn_f, 2)
            act.wait_ge(s_hn_b, 4)
            for j in range(16):
                act.wait_ge(s_c_mm, j + 1)
                a.activation(ys[:, 2 * j:2 * j + 2, :], ps[:, 4 + j % 4, 0:2 * NCH].rearrange("p (g n) -> p g n", n=NCH),
                             ACT.Gelu_apprx_tanh).then_inc(s_c_ev, 1)
            for j in range(8):
                act.wait_ge(s_y1_tr, 2 * j + 1)
                copy(Yt[:, :, 64 * j:64 * j + 64].rearrange("p s (g o) -> p g s o", o=HC),
                     ps[:, 2 * (j % 2), :].rearrange("p (g s o) -> p g s o", g=4, o=HC)).then_inc(s_y1_eva, 1)
            for j in range(8):
                fb, q = divmod(j, 2)
                act.wait_ge(s_y2_tr, j + 1)
                copy(yT[:, fb, NCTX:TOK].rearrange("p (n s) -> p s n", s=CH)[:, 4 * q:4 * q + 4, :],
                     ps[:, 4 + j % 4, :].rearrange("p (s n) -> p s n", s=4)).then_inc(s_y2_eva, 1)
            for j in range(12):
                act.wait_ge(s_glu_mm, j + 1)
                nt = CHUNKS[j % 3][1]
                a.activation(ps[:, j % 4, 0:nt], ps[:, j % 4, 0:nt], ACT.Sigmoid,
                             bias=bglu[:, j // 3:j // 3 + 1]).then_inc(s_glu_sg, 1)
            squares(1, x1, RA[:, 0:D], lambda t: act.wait_ge(s_o_ok, TT + t + 1))
            root(3)
            act.wait_ge(s_mod_ok, 2)
            h_evac(1, hT1)

            def head_squares(bank, c0, nh, seen):
                act.wait_ge(s_hd_sq, seen)
                for h in range(nh):
                    a.activation(qjunk[:, P * h:P * h + P], ps[:, bank, P * h:P * h + P], ACT.Square,
                                 accum_out=qss[:, c0 + h:c0 + h + 1]).then_inc(s_hd_sq, 1)

            def head_root(c0, n, seen):
                act.wait_ge(s_hd_sq, seen)
                a.activation(qrs[:, c0:c0 + n], qss[:, c0:c0 + n], ACT.Sqrt, bias=epsc, scale=1.0 / HD).then_inc(s_hd_rt, 1)

            for t in range(TT):
                act.wait_ge(s_kv_mm, t + 1)
                head_squares(4 + t % 4, 64 + 2 * t, NKV, 2 * t)
                copy(Kraw[:, t], ps[:, 4 + t % 4, 0:256]).then_inc(s_kv_ev, 1)
                copy(Vt[:, t], ps[:, 4 + t % 4, 256:512]).then_inc(s_kv_ev, 1)
            head_root(64, 20, 20)
            for j in range(2 * LT):
                half, t = divmod(j, LT)
                act.wait_ge(s_q_mm, j + 1)
                head_squares(j % 4, 4 * j, HPK, 20 + 4 * j)
                copy(Qt[:, t, half * 512:half * 512 + 512], ps[:, j % 4, :]).then_inc(s_q_ev, 1)
                if j % 4 == 3:
                    head_root(4 * j - 12, 16, 24 + 4 * j)
            for j in range(2 * NH):
                h, q = divmod(j, 2)
                act.wait_ge(s_g_mm, j + 1)
                a.activation(gateT[:, h, q * 512:q * 512 + 512], ps[:, j % 4, :], ACT.Silu).then_inc(s_g_ev, 1)
                if j == 8:
                    for k in range(6):
                        act.wait_ge(s_kt_tr, k + 1)
                        h_, q_ = divmod(k, 3)
                        nt = 256 if q_ == 2 else 512
                        copy(KTh[:, h_, 512 * q_:512 * q_ + nt], ps[:, 4 + k % 4, 0:nt]).then_inc(s_kt_hi, 1)
                    for k in range(2):
                        act.wait_ge(s_gt1_tr, k + 1)
                        copy(gtb[:, 0, 512 * k:512 * k + 512], ps[:, 6 + k, :]).then_inc(s_gt1_ev, 1)

            def q_round(i):
                act.wait_ge(s_a_qT, i + 1)
                copy(qTh[:, i % 2], ps[:, 7, :].rearrange("p (h q) -> p h q", q=P)).then_inc(s_a_qh, 1)

            q_round(0)
            q_round(1)
            for i in range(2 * LT):
                for t in range(TT):
                    m = TT * i + t
                    act.wait_ge(s_a_s, m + 1)
                    if i:
                        act.wait_ge(s_a_sum, 9 * (i - 1) + max(t, 1))
                    a.activation(PT[:, t], ps[:, 3 + m % 2, :], ACT.Exp).then_inc(s_a_p, 1)
                if i + 2 < 2 * LT:
                    q_round(i + 2)
            for t in range(LT):
                act.wait_ge(s_z_ok, 2 * t + 2)
                a.activation(fjunk, xr[:, t], ACT.Square, accum_out=ssq[:, t:t + 1]).then_inc(s_fin_sq, 1)
                act.wait_ge(s_fin_sq, t + 1)
                a.activation(rstd[:, t:t + 1], ssq[:, t:t + 1], ACT.Sqrt, bias=epsc, scale=1.0 / D).then_inc(s_fin_rt, 1)

        @block.vector
        def _(dve):
            v = nc.vector
            n = [0]

            def step(ins):
                n[0] += 1
                ins.then_inc(s_chain, 1)
                dve.wait_ge(s_chain, n[0])

            def tt(o, a, b, op):
                step(v.tensor_tensor(o, a, b, op))

            def ts(o, a, s1, op1, s2=None, op2=ALU.bypass):
                step(v.tensor_scalar(o, a, s1, s2, op1, op2))

            def cp(o, a):
                step(v.tensor_copy(o, a))

            def refined(ss, m, rr):
                step(v.reciprocal(rr, rr))
                tt(ss, rr, rr, ALU.mult)
                tt(ss, ss, m, ALU.mult)
                ts(ss, ss, -0.5, ALU.mult, 1.5, ALU.add)
                tt(rr, rr, ss, ALU.mult)

            def rsqrt(i, ss, m, rr, scale):
                v.tensor_scalar(m, ss, scale, EPS, ALU.mult, ALU.add).then_inc(s_rt_req, 1)
                dve.wait_ge(s_rt_req, i)
                dve.wait_ge(s_rt_ok, i)
                refined(ss, m, rr)

            dve.wait_ge(s_par_tr, 1)
            v.tensor_copy(colv, ps[:, 3, 0:NCOL]).then_inc(s_col_ok, 1)
            dve.wait_ge(s_ld_par, 16 * 7)
            v.tensor_copy(lraw[0:G, 2].rearrange("g (d p) -> g d p", d=2),
                          ldraw[0:G].unsqueeze(2).broadcast_to([G, 2, NS])).then_inc(s_lraw_ok, 1)
            dve.wait_ge(s_par_tr, 2)
            for k, dst in enumerate((lamr, lami, ldt)):
                cp(dst, ps[:, 0, 32 * k:32 * k + 32])
            (dt, xe, kf, rr, ex, mg, s_, c_, r2, odd, sg, sn, cn, lr, li, fr, fi, t1, t2, t3, den, msk, t4, th) = s5t

            def exp_(o, xin):
                ts(msk, xin, -87.0, ALU.is_ge)
                ts(t4, xin, -87.0, ALU.max, 88.0, ALU.min)
                ts(ki, t4, 1.0 / math.log(2.0), ALU.mult)
                cp(kf, ki)
                ts(t1, kf, -LN2_HI, ALU.mult)
                tt(rr, t4, t1, ALU.add)
                ts(t1, kf, -LN2_LO, ALU.mult)
                tt(rr, rr, t1, ALU.add)
                ts(ex, rr, 1.0 / 5040, ALU.mult, 1.0 / 720, ALU.add)
                for q in (120.0, 24.0, 6.0, 2.0, 1.0, 1.0):
                    tt(ex, ex, rr, ALU.mult)
                    ts(ex, ex, 1.0 / q, ALU.add)
                ts(kf, kf, 127.0, ALU.add)
                cp(ki, kf)
                ts(kj, ki, 23, ALU.logical_shift_left)
                tt(ex, ex, kj.bitcast(F32), ALU.mult)
                tt(o, ex, msk, ALU.mult)

            exp_(dt, ldt)
            tt(xe, lamr, dt, ALU.mult)
            exp_(mg, xe)
            tt(th, lami, dt, ALU.mult)
            ts(ki, th, 2.0 / math.pi, ALU.mult)
            cp(kf, ki)
            cp(rr, th)
            for q in PIO2:
                ts(t1, kf, -q, ALU.mult)
                tt(rr, rr, t1, ALU.add)
            tt(r2, rr, rr, ALU.mult)
            ts(s_, r2, 1.0 / 362880, ALU.mult, -1.0 / 5040, ALU.add)
            for q in (1.0 / 120, -1.0 / 6, 1.0):
                tt(s_, s_, r2, ALU.mult)
                ts(s_, s_, q, ALU.add)
            tt(s_, s_, rr, ALU.mult)
            ts(c_, r2, -1.0 / 3628800, ALU.mult, 1.0 / 40320, ALU.add)
            for q in (-1.0 / 720, 1.0 / 24, -0.5, 1.0):
                tt(c_, c_, r2, ALU.mult)
                ts(c_, c_, q, ALU.add)
            ts(kj, ki, 1, ALU.bitwise_and)
            cp(odd, kj)
            ts(sg, odd, -1.0, ALU.mult, 1.0, ALU.add)
            tt(sn, s_, sg, ALU.mult)
            tt(t1, c_, odd, ALU.mult)
            tt(sn, sn, t1, ALU.add)
            tt(cn, c_, sg, ALU.mult)
            tt(t1, s_, odd, ALU.mult)
            tt(cn, cn, t1, ALU.add)
            for o, add in ((sn, 0.0), (cn, 1.0)):
                ts(kf, kf, add, ALU.add)
                cp(ki, kf)
                ts(kj, ki, 1, ALU.logical_shift_right, 1, ALU.bitwise_and)
                cp(sg, kj)
                ts(sg, sg, -2.0, ALU.mult, 1.0, ALU.add)
                tt(o, o, sg, ALU.mult)
            tt(lr, mg, cn, ALU.mult)
            tt(li, mg, sn, ALU.mult)
            tt(den, lamr, lamr, ALU.mult)
            tt(t1, lami, lami, ALU.mult)
            tt(den, den, t1, ALU.add)
            step(v.reciprocal(den, den))
            ts(t3, lr, -1.0, ALU.add)
            tt(t1, t3, lamr, ALU.mult)
            tt(t2, li, lami, ALU.mult)
            tt(t1, t1, t2, ALU.add)
            tt(fr, t1, den, ALU.mult)
            tt(t1, li, lamr, ALU.mult)
            tt(t2, t3, lami, ALU.mult)
            tt(t1, t1, t2, ALU.subtract)
            tt(fi, t1, den, ALU.mult)
            step(v.memset(LP[:, 0, 0], 1.0))
            step(v.memset(LP[:, 0, 1], 0.0))
            cp(LP[:, 1, 0], lr)
            cp(LP[:, 1, 1], li)
            for m in (1, 2, 4):
                A = [LP[:, 1:m + 1, r] for r in range(2)]
                M = [LP[:, m, r].unsqueeze(1).broadcast_to([P, m, G]) for r in range(2)]
                O = [LP[:, m + 1:2 * m + 1, r] for r in range(2)]
                tmp = ctmp[:, 0:m * G].rearrange("p (m g) -> p m g", g=G)
                tt(O[0], A[0], M[0], ALU.mult)
                tt(tmp, A[1], M[1], ALU.mult)
                tt(O[0], O[0], tmp, ALU.subtract)
                tt(O[1], A[0], M[1], ALU.mult)
                tt(tmp, A[1], M[0], ALU.mult)
                tt(O[1], O[1], tmp, ALU.add)
            fwd, bwd = slice(0, NS), slice(NS, P)
            cp(LPc[fwd], LP[fwd])
            cp(LPc[bwd], LP[bwd, ::-1])
            cp(LPb[fwd], LP[fwd, 7::-1])
            cp(LPb[bwd], LP[bwd, 0:8])
            cp(L8[:, 0:32], LP[:, 8, 0])
            cp(L8[:, 32:64], LP[:, 8, 0])
            cp(L8[:, 64:96], LP[:, 8, 1])
            ts(L8[:, 96:128], LP[:, 8, 1], -1.0, ALU.mult)
            dve.wait_ge(s_ld_b, 16 * 4)
            F = [q.unsqueeze(2).broadcast_to([P, G, HC]) for q in (fr, fi)]
            tmp = ctmp.rearrange("p (g h) -> p g h", h=HC)
            tt(BB[:, 0], braw[:, 0], F[0], ALU.mult)
            tt(tmp, braw[:, 1], F[1], ALU.mult)
            tt(BB[:, 0], BB[:, 0], tmp, ALU.subtract)
            tt(BB[:, 1], braw[:, 1], F[0], ALU.mult)
            tt(tmp, braw[:, 0], F[1], ALU.mult)
            tt(BB[:, 1], BB[:, 1], tmp, ALU.add)
            dve.wait_ge(s_par_tr, 4)
            cp(Cx[:, 0], ps[:, 1, :].rearrange("p (g h) -> p g h", h=HC))
            v.tensor_scalar(Cx[:, 1], ps[:, 2, :].rearrange("p (g h) -> p g h", h=HC), -1.0, None,
                            ALU.mult).then_inc(s_par_ok, 1)
            dve.wait_ge(s_par_ok, 1)

            def mod_evac(l, k, b0, b1, bank):
                dve.wait_ge(s_mod_mm, k)
                tt(modc[l][:, b0:b1], ps[:, bank, 2 * b0:2 * b1].rearrange("p (b c) -> p b c", c=2),
                   bmod[l][:, b0:b1].unsqueeze(2).broadcast_to([P, b1 - b0, 2]), ALU.add)

            def make_a(l):
                ts(hA[l], modc[l][:, 8:16], 1.0, ALU.add)
                v.tensor_tensor(hA[l], hA[l], ng[l].unsqueeze(2).broadcast_to([P, KT, 2]), ALU.mult).then_inc(s_mod_ok, 1)
                dve.wait_ge(s_mod_ok, l + 1)

            def normed(l, Xr, i):
                dve.wait_ge(s_sq, TT * (l + 1))
                rsqrt(i, ssq, msq, rstd, 1.0 / D)
                for t in range(TT):
                    v.tensor_scalar(Xr[:, t], Xr[:, t], rstd[:, t:t + 1], None, ALU.mult).then_inc(s_xn, 1)

            def h_evac(l, hT):
                for q, (t0, nt) in enumerate(CHUNKS):
                    ci = 1 if q == 0 else 0
                    for k in range(1, KT, 2):
                        j = KT * q + k
                        dve.wait_ge(s_h_tr, 24 * l + j + 1)
                        v.tensor_scalar(hT[:, k, t0:t0 + nt], ps[:, j % 4, 0:nt], hA[l][:, k, ci:ci + 1],
                                        modc[l][:, k, ci:ci + 1], ALU.mult, ALU.add).then_inc(s_h_evd, 1)

            normed(0, X, 1)
            mod_evac(0, 4, 0, 16, 4)
            make_a(0)
            h_evac(0, hT0)

            def build_cl(half):
                if half:
                    dve.wait_ge(s_cop_out, 16 * 8)
                    dve.wait_ge(s_k_mm, 4)
                for q in range(4):
                    g4 = slice(4 * q, 4 * q + 4)
                    a4 = slice(16 * half + 4 * q, 16 * half + 4 * q + 4)
                    L = [LPc[:, :, r, a4].rearrange("p k g -> p g k").unsqueeze(3).broadcast_to([P, 4, 9, HC])
                         for r in range(2)]
                    C_ = [Cx[:, r, a4, :].unsqueeze(2).broadcast_to([P, 4, 9, HC]) for r in range(2)]
                    tt(CL[:, 0, g4], C_[0], L[0], ALU.mult)
                    tt(cltmp, C_[1], L[1], ALU.mult)
                    tt(CL[:, 0, g4], CL[:, 0, g4], cltmp, ALU.add)
                    tt(CL[:, 1, g4], C_[1], L[0], ALU.mult)
                    tt(cltmp, C_[0], L[1], ALU.mult)
                    tt(CL[:, 1, g4], CL[:, 1, g4], cltmp, ALU.subtract)
                v.tensor_copy(cltmp[:, 0, 0, :], cltmp[:, 0, 1, :]).then_inc(s_cl_ok, 1)
                dve.wait_ge(s_cl_ok, half + 1)

            def k_evac(half):
                dve.wait_ge(s_ld_ws, 16 * 2)
                if half:
                    dve.wait_ge(s_t_in, 16 * 15)
                for q in range(4):
                    dve.wait_ge(s_k_mm, 4 * half + q + 1)
                    g4 = slice(4 * q, 4 * q + 4)
                    a4 = slice(16 * half + 4 * q, 16 * half + 4 * q + 4)
                    bk = ps[:, q, :].rearrange("p (g k o) -> p g k o", k=CH, o=HC)
                    cp(Kt[32:32 + HC, g4, 0:7], bk[32:32 + HC, :, 0:7])
                    cp(Kt[0:HC, g4], bk[0:HC])
                    tt(ddtmp[0:HC], ident[0:HC, 0:HC].unsqueeze(1).broadcast_to([HC, 4, HC]), dskip[0:HC, a4, :], ALU.mult)
                    v.tensor_tensor(Kt[0:HC, g4, 0], Kt[0:HC, g4, 0], ddtmp[0:HC], ALU.add).then_inc(s_k_ev, 1)
                    dve.wait_ge(s_k_ev, 4 * half + q + 1)

            build_cl(0)
            for t in range(TT):
                dve.wait_ge(s_v_ev, t + 1)
                step(v.bn_stats(bnst, vt[:, t]))
                step(v.bn_aggr(mv[:, t], bnst))
            cp(ssq.unsqueeze(2), mv[:, :, 1:2])
            rsqrt(2, ssq, msq, rstd, 1.0)
            for t in range(TT):
                v.tensor_scalar(vt[:, t], vt[:, t], mv[:, t, 0:1], rstd[:, t:t + 1], ALU.subtract, ALU.mult).then_inc(s_vn_ok, 1)
            k_evac(0)
            build_cl(1)
            dve.wait_ge(s_bl_tr, 16)
            for j in range(2):
                dve.wait_ge(s_xs_mm, CH + j + 1)
                for q in range(4):
                    v.tensor_copy(Yc[0:CCH, :, 4 * j + q, :],
                                  ps[32 * q:32 * q + 32, 4 + j, :].rearrange("p (g c) -> p g c", c=HC)).then_inc(s_xs_evd, 1)
            k_evac(1)
            dve.wait_ge(s_k_mm, 8)
            dve.wait_ge(s_bl_ok, 4)
            dve.wait_ge(s_ws_tr, 1)
            v.tensor_copy(wsT, ps[:, 5, :].rearrange("p (g q) -> p g q", g=4)).then_inc(s_ws_ev, 1)
            mod_evac(0, 6, 16, 24, 4)
            v.tensor_copy(rt[:, 0:1], L8[:, 0:1]).then_inc(s_par_dead, 1)
            dve.wait_ge(s_cop_out, 16 * 16)
            dve.wait_ge(s_t_in, 16 * 30)
            dve.wait_ge(s_vg_ok, TT)
            v.memset(H[:, 0], 0.0).then_inc(s_b_evb, 1)
            for j in range(32):
                q, r = divmod(j, 2)
                dve.wait_ge(s_b_mm, j + 1)
                src = ps[NS:P, j % 4, 0:2 * NCH].rearrange("p (g n) -> p g n", n=NCH)
                v.tensor_copy(H[NS:P, CCH:0:-1, r, 2 * q:2 * q + 2].rearrange("p n g -> p g n"),
                              src[:, :, 0:CCH]).then_inc(s_b_evb, 1)
                v.tensor_copy(H[NS:P, NCH:CCH:-1, r, 2 * q:2 * q + 2].rearrange("p n g -> p g n"),
                              src[:, :, CCH:NCH]).then_inc(s_b_evb, 1)
            dve.wait_ge(s_b_evb, 65)
            dve.wait_ge(s_b_evf, 32)
            Hf = H.rearrange("p i r g -> p i (r g)")
            LR, LI = L8[:, 0:64], L8[:, 64:128].rearrange("p (r g) -> p r g", r=2)
            m0, m1 = rt[:, 0:64], rt[:, 64:128]
            UNR = 4
            with dve.Fori(0, NCH // UNR) as it:
                for k in range(UNR):
                    i = it * UNR + k
                    v.tensor_tensor(m0, Hf[:, i, :], LR, ALU.mult).then_inc(s_rec, 1)
                    v.tensor_tensor(m1.rearrange("p (r g) -> p r g", r=2)[:, ::-1, :], H[:, i, :, :], LI, ALU.mult).then_inc(s_rec, 1)
                    dve.wait_ge(s_rec, i * 4 + 1)
                    v.tensor_tensor(Hf[:, i + 1, :], Hf[:, i + 1, :], m0, ALU.add).then_inc(s_rec, 1)
                    dve.wait_ge(s_rec, i * 4 + 3)
                    v.tensor_tensor(Hf[:, i + 1, :], Hf[:, i + 1, :], m1, ALU.add).then_inc(s_rec, 1)
                    dve.wait_ge(s_rec, i * 4 + 4)
            v.tensor_copy(rt[:, 0:1], rt[:, 1:2]).then_inc(s_rec_ok, 1)
            dve.wait_ge(s_ld_bs, 16)
            dve.wait_ge(s_ga_ok, 12)
            for t in range(TT):
                dve.wait_ge(s_gm_mm, t + 1)
                pb = ps[:, 4 + t % 4, :]
                tt(pb, pb, bsb, ALU.add)
                v.tensor_tensor(mixT[:, 0:FB, t * P:(t + 1) * P], mixT[:, 0:FB, t * P:(t + 1) * P],
                                pb.rearrange("p (g q) -> p g q", g=FB), ALU.mult).then_inc(s_gm_ok, 1)
            dve.wait_ge(s_f_mm, 36)
            dve.wait_ge(s_rec_ok, 1)
            for r in range(2):
                v.tensor_copy(Hn[NS:P, r, :, 0:CCH], H[NS:P, CCH - 1::-1, r, :].rearrange("p n g -> p g n")).then_inc(s_hn_b, 1)
                v.tensor_copy(Hn[NS:P, r, :, CCH:NCH], H[NS:P, NCH - 1:CCH - 1:-1, r, :].rearrange("p n g -> p g n")).then_inc(s_hn_b, 1)
            mod_evac(1, 12, 0, 24, 0)
            step(v.memset(epsc, EPS))
            make_a(1)
            for j in range(8):
                dve.wait_ge(s_y1_tr, 2 * j + 2)
                v.tensor_copy(Ytc[0:CCH, :, 64 * j:64 * j + 64].rearrange("p s (g o) -> p g s o", o=HC),
                              ps[0:CCH, 2 * (j % 2) + 1, :].rearrange("p (g s o) -> p g s o", g=4, o=HC)).then_inc(s_y1_evd, 1)
            for j in range(4):
                dve.wait_ge(s_y2_tr, 8 + j + 1)
                v.tensor_copy(yT[:, j, 0:NCTX].rearrange("p (n s) -> p s n", s=CH),
                              ps[:, 4 + j, 0:NCTX].rearrange("p (s n) -> p s n", s=CH)).then_inc(s_y2_evd, 1)
            for j in range(12):
                fb, q = divmod(j, 3)
                t0, nt = CHUNKS[q]
                dve.wait_ge(s_glu_sg, j + 1)
                pb, m = ps[:, j % 4, 0:nt], mixT[:, FB + fb, t0:t0 + nt]
                tt(pb, pb, yT[:, fb, t0:t0 + nt], ALU.mult)
                v.tensor_tensor(m, m, pb, ALU.mult).then_inc(s_glu_ok, 1)
            for j in range(2 * TT):
                half, t = divmod(j, TT)
                dve.wait_ge(s_o_mm, j + 1)
                if j >= 2:
                    dve.wait_ge(s_o_ok, j - 1)
                v.tensor_tensor(otmp[:, j % 2], ps[:, 4 + j % 4, :],
                                gtb[:, 1 if t < CT else 0, half * 512:half * 512 + 512], ALU.mult).then_inc(s_o_t, 1)
            dve.wait_ge(s_x1_out, 16)
            normed(1, x1, 3)
            h_evac(1, hT1)
            dve.wait_ge(s_ld_gain, 16 * 2)
            ts(L8[:], L8[:], HD ** -0.5, ALU.mult)

            def gained(q, nh, r, gain):
                qv = q.rearrange("p (h d) -> p h d", d=HD)
                tt(qv, qv, r.unsqueeze(2).broadcast_to([P, nh, HD]), ALU.mult)
                tt(qv, qv, gain.unsqueeze(1).broadcast_to([P, nh, HD]), ALU.mult)

            def rope(q, nh, t):
                q4 = q.rearrange("p (h a b m) -> p h a b m", h=nh, a=2, b=2)
                co, si = (cs[:, k, t].rearrange("p (a m) -> p a m", a=2).unsqueeze(1).broadcast_to([P, nh, 2, 32])
                          for k in range(2))
                t_ = [rope_t[k][:, 0:nh * 64].rearrange("p (h a m) -> p h a m", h=nh, a=2) for k in range(2)]
                x1_, x2_ = q4[:, :, :, 0], q4[:, :, :, 1]
                tt(t_[0], x1_, si, ALU.mult)
                tt(t_[1], x2_, si, ALU.mult)
                tt(x1_, x1_, co, ALU.mult)
                tt(x1_, x1_, t_[1], ALU.subtract)
                tt(x2_, x2_, co, ALU.mult)
                v.tensor_tensor(x2_, x2_, t_[0], ALU.add).then_inc(s_q_ok if nh == HPK else s_k_ok, 1)

            def head_rstd(b, c0, n):
                cols = slice(c0, c0 + n)
                dve.wait_ge(s_hd_rt, b)
                ts(qms[:, cols], qss[:, cols], 1.0 / HD, ALU.mult, EPS, ALU.add)
                refined(qss[:, cols], qms[:, cols], qrs[:, cols])

            dve.wait_ge(s_ld_tab, 16 * 2)
            dve.wait_ge(s_kv_ev, 2 * TT)
            head_rstd(1, 64, 20)
            for t in range(TT):
                gained(Kraw[:, t], NKV, qrs[:, 64 + 2 * t:66 + 2 * t], rt[:])
                if t >= CT:
                    rope(Kraw[:, t], NKV, t - CT)
                    dve.wait_ge(s_k_ok, t - CT + 1)
            for j in range(2 * LT):
                half, t = divmod(j, LT)
                if j % 4 == 0:
                    dve.wait_ge(s_q_ev, j + 4)
                    head_rstd(2 + j // 4, 4 * j, 16)
                q = Qt[:, t, half * 512:half * 512 + 512]
                gained(q, HPK, qrs[:, 4 * j:4 * j + 4], L8[:])
                rope(q, HPK, t)
                dve.wait_ge(s_q_ok, j + 1)
            for j in range(6):
                dve.wait_ge(s_kt_hi, j + 1)
                h, q = divmod(j, 3)
                nt = 256 if q == 2 else 512
                cols = slice(512 * q, 512 * q + nt)
                v.tensor_tensor(KTl[:, h, cols], ps[:, 4 + j % 4, 0:nt], KTh[:, h, cols].bitcast(F32), ALU.subtract).then_inc(s_kt_lo, 1)
            v.memset(ones, 1.0).then_inc(s_ones, 1)
            dve.wait_ge(s_ones, 1)
            v.tensor_copy(ones_r[:], ones).then_inc(s_ones, 1)
            dve.wait_ge(s_g_ev, 2 * NH)

            def q_rest(i):
                dve.wait_ge(s_a_qh, i + 1)
                v.tensor_tensor(qTl[:, i % 2], ps[:, 7, :].rearrange("p (h q) -> p h q", q=P),
                                qTh[:, i % 2].bitcast(F32), ALU.subtract).then_inc(s_a_ql, 1)

            def row_max(i, h):
                dve.wait_ge(s_a_mx, HPK * i + h + 1)
                v.tensor_reduce(smax[:, i % 2, h:h + 1], ps[:, 0:3, :].rearrange("p b n -> p (b n)")[:, 0:TOK],
                                AX.X, ALU.max).then_inc(s_a_max, 1)

            def neg_max(i):
                dve.wait_ge(s_a_nt, i + 1)
                v.scalar_tensor_tensor(out=nm[0:HPK, i % 2].rearrange("p (h q) -> p h q", q=P),
                                       in0=ps[0:HPK, 6, 0:P].unsqueeze(1).broadcast_to([HPK, HPK, P]), scalar=-1.0,
                                       in1=ident[0:HPK, 0:HPK].unsqueeze(2).broadcast_to([HPK, HPK, P]),
                                       op0=ALU.mult, op1=ALU.mult).then_inc(s_a_nm, 1)

            def gate_over_sums(i):
                b, kv = divmod(i, 2)
                dve.wait_ge(s_a_sm, i + 1)
                step(v.reciprocal(ri, ps[:, 6, :]))
                if i:
                    dve.wait_ge(s_a_o, i)
                v.tensor_tensor(GR.rearrange("p (h q) -> p h q", q=P), ri.rearrange("p (h q) -> p h q", q=P),
                                gateT[:, HPK * kv:HPK * kv + HPK, b * P:(b + 1) * P], ALU.mult).then_inc(s_a_gr, 1)

            def output(i):
                b, kv = divmod(i, 2)
                dve.wait_ge(s_a_pv, i + 1)
                dve.wait_ge(s_a_gr, i + 1)
                v.tensor_tensor(OT[:, b, HPK * kv:HPK * kv + HPK, :], GR.rearrange("p (h q) -> p h q", q=P),
                                ps[:, 5, :].rearrange("p (h q) -> p h q", q=P), ALU.mult).then_inc(s_a_o, 1)

            q_rest(0)
            q_rest(1)
            for h in range(HPK):
                row_max(0, h)
            neg_max(0)
            for i in range(2 * LT + 1):
                for h in range(HPK):
                    if i + 1 < 2 * LT:
                        row_max(i + 1, h)
                    if h == 0 and i:
                        gate_over_sums(i - 1)
                if i + 1 < 2 * LT:
                    neg_max(i + 1)
                if i:
                    output(i - 1)
                if i + 2 < 2 * LT:
                    q_rest(i + 2)
            dve.wait_ge(s_ld_fin, 16)
            for t in range(LT + 1):
                if t < LT:
                    for half in range(2):
                        j = 2 * t + half
                        dve.wait_ge(s_z_mm, j + 1)
                        if j >= 2:
                            dve.wait_ge(s_z_ok, j - 1)
                        v.tensor_tensor(otmp[:, half], ps[:, j % 4, :], gtb[:, 0, half * 512:half * 512 + 512],
                                        ALU.mult).then_inc(s_z_t, 1)
                if t:
                    c = slice(t - 1, t)
                    dve.wait_ge(s_fin_rt, t)
                    ts(msq[:, c], ssq[:, c], 1.0 / D, ALU.mult, EPS, ALU.add)
                    refined(ssq[:, c], msq[:, c], rstd[:, c])
                    v.scalar_tensor_tensor(out=xr[:, t - 1], in0=xr[:, t - 1], scalar=rstd[:, c], in1=fgb,
                                           op0=ALU.mult, op1=ALU.mult).then_inc(s_fin_g, 1)

        @block.tensor
        def _(pe):
            te = nc.tensor

            def arrived(kind, b):
                u = (kind, b)
                pe.wait_ge(w_in[place[u] % NSLOT], 16 * (place[u] // NSLOT + 1))
                return u

            def tr(o, i):
                m = i.shape[0]
                return te.transpose(o, i, ident[0:m, 0:m])

            pe.wait_ge(s_ld_const, 16 * 8)
            tr(ps[:, 3, 0:NCOL], colrow[0:NCOL]).then_inc(s_par_tr, 1)
            pe.wait_ge(s_ld_par, 16 * 7)
            pe.wait_ge(s_lraw_ok, 1)
            for k in range(3):
                last = tr(ps[:, 0, 32 * k:32 * k + 32], lraw[0:G, k])
            last.then_inc(s_par_tr, 1)
            for r in range(2):
                for q in range(4):
                    last = tr(ps[:, 1 + r, P * q:P * q + P], craw[:, r, q])
                last.then_inc(s_par_tr, 1)

            def modulation(kind, b0, b1, bank):
                for b in range(b0, b1):
                    u = arrived(kind, b)
                    for f in range(4):
                        o = 2 * (4 * b + f)
                        for k in range(KT):
                            last = te.matmul(ps[:, bank, o:o + 2], slot_kn(u)[:, k, P * f:P * f + P], cond[:, k],
                                             start=k == 0, stop=k == KT - 1)
                    last.then_inc(s_mod_mm, 1)

            pe.wait_ge(s_cond_ok, 1)
            modulation("mod0", 0, 4, 4)

            def to_features(l, Xr):
                for q, (t0, nt) in enumerate(CHUNKS):
                    for k in range(KT):
                        j = KT * q + k
                        if j >= 4:
                            pe.wait_ge(s_h_evd if j % 2 else s_h_eva, 12 * l + (j - 4) // 2 + 1)
                        for t in range(nt // P):
                            if k == 0:
                                pe.wait_ge(s_xn, TT * l + t0 // P + t + 1)
                            last = tr(ps[:, j % 4, t * P:t * P + P], Xr[:, t0 // P + t, P * k:P * k + P])
                        last.then_inc(s_h_tr, 1)

            pe.wait_ge(s_par_ok, 1)
            to_features(0, X)

            def token_major(u, bank, lhs, signal):
                for k in range(KT):
                    last = te.matmul(ps[:, bank, :], lhs(k), slot_kn(u)[:, k], start=k == 0, stop=k == KT - 1)
                last.then_inc(signal, 1)

            pe.wait_ge(s_h_eva, 12)
            pe.wait_ge(s_h_evd, 12)
            pe.wait_ge(s_mod_ok, 1)
            u = arrived("v", 0)
            for t in range(TT):
                if t >= 4:
                    pe.wait_ge(s_v_ev, t - 3)
                token_major(u, 4 + t % 4, lambda k: hT0[:, k, t * P:t * P + P], s_v_mm)
            for j in range(16):
                r, q = divmod(j, 8)
                pe.wait_ge(s_bl_ok, 4)
                if j >= 4:
                    pe.wait_ge(s_bl_ev, j - 3)
                for m in range(4):
                    last = tr(ps[:, j % 4, P * m:P * m + P], BL[:, r, 4 * q + m].rearrange("p s h -> p (s h)"))
                last.then_inc(s_bl_tr, 1)

            def lags(half):
                pe.wait_ge(s_cl_ok, half + 1)
                if half:
                    pe.wait_ge(s_k_ev, 4 * half)
                else:
                    pe.wait_ge(s_bl_ev, 16)
                for q in range(4):
                    for m in range(4):
                        gl, g = 4 * q + m, 16 * half + 4 * q + m
                        base = P * m
                        for r in range(2):
                            te.matmul(ps[0:HC, q, base:base + HC], BB[:, r, g], Cx[:, r, g], start=r == 0, stop=r == 1)
                        for d in range(2):
                            rows, o = slice(d * NS, (d + 1) * NS), base + (HC if d == 0 else 0)
                            for r in range(2):
                                last = te.matmul(ps[32 * d:32 * d + HC, q, o:o + 7 * HC], BB[rows, r, g],
                                                 CL[rows, r, gl, 1:8].rearrange("p k o -> p (k o)"), start=r == 0, stop=r == 1)
                    last.then_inc(s_k_mm, 1)

            lags(0)
            u = arrived("xs", 0)
            pe.wait_ge(s_v_ev, TT)
            for s in range(CH):
                if s >= 4:
                    pe.wait_ge(s_xs_eva, s - 3)
                token_major(u, 4 + s % 4, lambda k: hT0[:, k, NCTX + s:TOK:CH], s_xs_mm)
            pe.wait_ge(s_hperm_ok, 1)
            for j in range(2):
                pe.wait_ge(s_xs_eva, 5 + j)
                token_major(u, 4 + j, lambda k: hperm[:, k, P * j:P * j + P], s_xs_mm)
            lags(1)
            pe.wait_ge(s_xs_evd, 8)
            pe.wait_ge(s_xs_eva, 8)
            modulation("mod0", 4, 6, 4)
            pe.wait_ge(s_ld_ws, 32)
            for g in range(4):
                last = tr(ps[:, 5, P * g:P * g + P], wsraw[:, g])
            last.then_inc(s_ws_tr, 1)
            pe.wait_ge(s_k_ev, 8)
            for j in range(11):
                if j >= 4:
                    pe.wait_ge(s_u_ev, j - 3)
                for m in range(min(3, G - 3 * j)):
                    g = 3 * j + m
                    tr(ps[:, j % 4, NCH * m:NCH * m + CCH], Yc[0:CCH, g].rearrange("p s c -> p (s c)"))
                    last = tr(ps[:, j % 4, NCH * m + CCH:NCH * (m + 1)], Yl[:, g].rearrange("p s c -> p (s c)"))
                last.then_inc(s_u_tr, 1)
            pe.wait_ge(s_u_ev, 11)
            for j in range(32):
                q, r = divmod(j, 2)
                u = arrived("bop", q // 8)
                op = slot(u).rearrange("p (r g m) -> p r g m", r=2, m=P)
                if j >= 4:
                    pe.wait_ge(s_b_evf, j - 3)
                    pe.wait_ge(s_b_evb, 2 * (j - 3) + 1)
                for m in range(2):
                    last = te.matmul(ps[:, j % 4, NCH * m:NCH * (m + 1)], op[:, r, (2 * q + m) % 16], U[:, 2 * q + m],
                                     start=True, stop=True)
                last.then_inc(s_b_mm, 1)

            def gt_rows(l, c, bank, signal):
                for half in range(2):
                    for m in range(4):
                        k = 16 + 4 * half + m
                        last = tr(ps[:, bank + half, P * m:P * m + P], modc[l][:, k, c:c + 1].broadcast_to([P, P]))
                    last.then_inc(signal, 1)

            pe.wait_ge(s_par_dead, 1)
            gt_rows(0, 0, 4, s_gt_tr)
            gt_rows(0, 1, 6, s_gt_tr)
            pe.wait_ge(s_b_evf, 32)
            pe.wait_ge(s_b_evb, 65)
            for part, kind in enumerate(("u", "ga", "gb")):
                u = arrived(kind, 0)
                for fb in range(FB):
                    for q, (t0, nt) in enumerate(CHUNKS):
                        j = 12 * part + 3 * fb + q
                        if j >= 4:
                            pe.wait_ge(s_f_ev, j - 3)
                        for k in range(KT):
                            last = te.matmul(ps[:, j % 4, 0:nt], slot_kn(u)[:, k, P * fb:P * fb + P], hT0[:, k, t0:t0 + nt],
                                             start=k == 0, stop=k == KT - 1)
                        last.then_inc(s_f_mm, 1)
            pe.wait_ge(s_gt_ev, 4)
            pe.wait_ge(s_vg_ok, TT)
            pe.wait_ge(s_ws_ev, 1)
            for t in range(TT):
                if t >= 4:
                    pe.wait_ge(s_gm_ok, t - 3)
                for g in range(FB):
                    last = te.matmul(ps[:, 4 + t % 4, P * g:P * g + P], vt[:, t, P * g:P * g + P], wsT[:, g], start=True, stop=True)
                last.then_inc(s_gm_mm, 1)
            pe.wait_ge(s_f_ev, 36)
            modulation("mod1", 0, 6, 0)
            pe.wait_ge(s_gm_ok, TT)
            pe.wait_ge(s_hn_f, 2)
            pe.wait_ge(s_hn_b, 4)
            for j in range(16):
                u = arrived("ct", j // 4)
                op = slot(u)[:, 0:3072].rearrange("p (r g m) -> p r g m", r=3, m=P)
                if j >= 4:
                    pe.wait_ge(s_c_ev, j - 3)
                for m in range(2):
                    g, gl = 2 * j + m, (2 * j + m) % 8
                    o = ps[:, 4 + j % 4, NCH * m:NCH * (m + 1)]
                    te.matmul(o, op[:, 2, gl], U[:, g], start=True, stop=False)
                    te.matmul(o, op[:, 0, gl], Hn[:, 0, g], start=False, stop=False)
                    last = te.matmul(o, op[:, 1, gl], Hn[:, 1, g], start=False, stop=True)
                last.then_inc(s_c_mm, 1)
            pe.wait_ge(s_mod_ok, 2)
            pe.wait_ge(s_c_ev, 16)
            for j in range(8):
                if j >= 2:
                    pe.wait_ge(s_y1_eva, j - 1)
                    pe.wait_ge(s_y1_evd, j - 1)
                bk = 2 * (j % 2)
                for m in range(4):
                    last = tr(ps[:, bk, P * m:P * m + P], ys[:, 4 * j + m, CCH:NCH])
                last.then_inc(s_y1_tr, 1)
                for m in range(4):
                    last = tr(ps[0:CCH, bk + 1, P * m:P * m + P], ys[:, 4 * j + m, 0:CCH])
                last.then_inc(s_y1_tr, 1)
            pe.wait_ge(s_y1_eva, 8)
            pe.wait_ge(s_y1_evd, 8)
            for j in range(8):
                fb, q = divmod(j, 2)
                if j >= 4:
                    pe.wait_ge(s_y2_eva, j - 3)
                for m in range(4):
                    last = tr(ps[:, 4 + j % 4, P * m:P * m + P], Yt[:, 4 * q + m, P * fb:P * fb + P])
                last.then_inc(s_y2_tr, 1)
            for j in range(4):
                pe.wait_ge(s_y2_eva, 5 + j)
                for s in range(CH):
                    last = tr(ps[:, 4 + j, CCH * s:CCH * s + CCH], Ytc[0:CCH, s, P * j:P * j + P])
                last.then_inc(s_y2_tr, 1)
            u = arrived("glu", 0)
            wg = slot(u)[:, 0:2048].rearrange("p (k n) -> p k n", n=512)
            pe.wait_ge(s_y2_eva, 8)
            pe.wait_ge(s_y2_evd, 4)
            for j in range(12):
                fb, q = divmod(j, 3)
                t0, nt = CHUNKS[q]
                if j >= 4:
                    pe.wait_ge(s_glu_ok, j - 3)
                for k in range(FB):
                    last = te.matmul(ps[:, j % 4, 0:nt], wg[:, k, P * fb:P * fb + P], yT[:, k, t0:t0 + nt],
                                     start=k == 0, stop=k == FB - 1)
                last.then_inc(s_glu_mm, 1)
            pe.wait_ge(s_gm_ok, TT)
            pe.wait_ge(s_glu_ok, 12)
            for half in range(2):
                u = arrived("out0", half)
                for t in range(TT):
                    j = TT * half + t
                    if j >= 4:
                        pe.wait_ge(s_o_t, j - 3)
                    token_major(u, 4 + j % 4, lambda k: mixT[:, k, t * P:t * P + P], s_o_mm)

            to_features(1, x1)
            pe.wait_ge(s_o_t, 2 * TT)
            pe.wait_ge(s_h_eva, 24)
            pe.wait_ge(s_h_evd, 24)
            u = arrived("kv", 0)
            for t in range(TT):
                if t >= 4:
                    pe.wait_ge(s_kv_ev, 2 * (t - 3))
                token_major(u, 4 + t % 4, lambda k: hT1[:, k, t * P:t * P + P], s_kv_mm)
            for half in range(2):
                u = arrived("q", half)
                for t in range(LT):
                    j = LT * half + t
                    if j >= 4:
                        pe.wait_ge(s_q_ev, j - 3)
                        pe.wait_ge(s_hd_sq, 20 + 4 * (j - 3))
                    token_major(u, j % 4, lambda k: hT1[:, k, NCTX + t * P:NCTX + t * P + P], s_q_mm)
            pe.wait_ge(s_q_ev, 2 * LT)
            pe.wait_ge(s_hd_sq, 20 + 4 * 2 * LT)

            def k_transposes():
                pe.wait_ge(s_k_ok, LT)
                pe.wait_ge(s_kv_ev, 2 * TT)
                for j in range(6):
                    h, q = divmod(j, 3)
                    if j >= 4:
                        pe.wait_ge(s_kt_lo, j - 3)
                    for t in range(4 * q, min(4 * q + 4, TT)):
                        last = tr(ps[:, 4 + j % 4, P * (t - 4 * q):P * (t - 4 * q) + P], Kraw[:, t, HD * h:HD * h + HD])
                    last.then_inc(s_kt_tr, 1)
                pe.wait_ge(s_kt_lo, 4)
                gt_rows(1, 0, 6, s_gt1_tr)

            for j in range(2 * NH):
                h, q = divmod(j, 2)
                u = arrived("gate", h // 4)
                if j >= 4:
                    pe.wait_ge(s_g_ev, j - 3)
                for k in range(KT):
                    last = te.matmul(ps[:, j % 4, :], slot_kn(u)[:, k, P * (h % 4):P * (h % 4) + P],
                                     hT1[:, k, NCTX + 512 * q:NCTX + 512 * q + 512], start=k == 0, stop=k == KT - 1)
                last.then_inc(s_g_mm, 1)
                if j == 8:
                    k_transposes()
            pe.wait_ge(s_g_ev, 2 * NH)
            pe.wait_ge(s_kt_lo, 6)
            pe.wait_ge(s_gt1_ev, 2)
            pe.wait_ge(s_ones, 2)
            pe.wait_ge(s_q_ok, 2 * LT)

            def q_transposes(i):
                if i:
                    pe.wait_ge(s_a_qh, i)
                    pe.wait_ge(s_a_ql, i)
                for h in range(HPK):
                    c = HD * (HPK * (i % 2) + h)
                    last = tr(ps[:, 7, P * h:P * h + P], Qt[:, i // 2, c:c + HD])
                last.then_inc(s_a_qT, 1)

            def max_scores(i, h):
                if h == 0:
                    pe.wait_ge(s_a_qh, i + 1)
                if i or h:
                    pe.wait_ge(s_a_max, HPK * i + h)
                for b, (t0, nt) in enumerate(((0, 512), (512, 512), (1024, 256))):
                    last = te.matmul(ps[:, b, 0:nt], qTh[:, i % 2, h], KTh[:, i % 2, t0:t0 + nt], start=True, stop=True)
                last.then_inc(s_a_mx, 1)

            def max_rows(i):
                pe.wait_ge(s_a_max, HPK * (i + 1))
                if i >= 2:
                    pe.wait_ge(s_a_gr, i - 1)
                tr(ps[0:HPK, 6, 0:P], smax[:, i % 2]).then_inc(s_a_nt, 1)

            def scores(i, t):
                m = TT * i + t
                if t == 0:
                    pe.wait_ge(s_a_nm, i + 1)
                    pe.wait_ge(s_a_ql, i + 1)
                if m >= 2:
                    pe.wait_ge(s_a_p, m - 1)
                o = ps[:, 3 + m % 2, :]
                kh, kl = (q[:, i % 2, P * t:P * t + P] for q in (KTh, KTl))
                qh, ql = (q[:, i % 2].rearrange("p h q -> p (h q)") for q in (qTh, qTl))
                te.matmul(o, ones_r[0:HPK, :], nm[0:HPK, i % 2], start=True, stop=False)
                te.matmul(o, kh, qh, start=False, stop=False)
                te.matmul(o, kh, ql, start=False, stop=False)
                te.matmul(o, kl, qh, start=False, stop=True).then_inc(s_a_s, 1)

            def values(i, t):
                pe.wait_ge(s_a_p, TT * i + t + 1)
                if t == 0 and i:
                    pe.wait_ge(s_a_o, i)
                mm = te.matmul(ps[:, 5, :], Vt[:, t, HD * (i % 2):HD * (i % 2) + HD], PT[:, t],
                               start=t == 0, stop=t == TT - 1)
                if t == TT - 1:
                    mm.then_inc(s_a_pv, 1)

            def row_sums(i):
                pe.wait_ge(s_a_sum, 9 * (i + 1))
                if i + 1 < 2 * LT:
                    pe.wait_ge(s_a_nm, i + 2)
                te.matmul(ps[:, 6, :], ones, psum_p[:, i % 2], start=True, stop=True).then_inc(s_a_sm, 1)

            q_transposes(0)
            q_transposes(1)
            for h in range(HPK):
                max_scores(0, h)
            max_rows(0)
            for i in range(2 * LT + 1):
                for t in range(TT):
                    if i:
                        values(i - 1, t)
                    if i < 2 * LT:
                        scores(i, t)
                    if t == 1 and i:
                        row_sums(i - 1)
                    if i + 1 < 2 * LT:
                        if t % 2 == 0 and t < 8:
                            max_scores(i + 1, t // 2)
                        if t == 8:
                            max_rows(i + 1)
                if i + 2 < 2 * LT:
                    q_transposes(i + 2)
            pe.wait_ge(s_a_o, 2 * LT)
            us = [arrived("out1", half) for half in range(2)]
            for t in range(LT):
                for half in range(2):
                    j = 2 * t + half
                    if j >= 4:
                        pe.wait_ge(s_z_t, j - 3)
                    token_major(us[half], j % 4, lambda k: OT[:, t, k], s_z_mm)


_ROPE = (np.arange(SEQ)[:, None] // 64, np.arange(SEQ)[:, None] % 64)


def kernel(**inputs):
    import concourse.bacc as bacc
    from concourse.bass_utils import run_bass_kernel_spmd

    nc = bacc.Bacc("TRN2", target_bir_lowering=False, num_devices=1, dynamic_dma_scratch_size=64)
    arrays, args = {}, []

    def declare(name, a):
        arrays[name] = a
        args.append(nc.dram_tensor(name, a.shape, mybir.dt.from_np(a.dtype), kind="ExternalInput").ap())

    names = ["x", "c", "ctx", "c_ctx", "norm_g", "w_mod", "b_mod", "we_in", "we_out", "gm_v_g", "gm_w_s", "gm_b_s",
             "s5_lam_re", "s5_lam_im", "s5_log_dt", "s5_b_re", "s5_b_im", "s5_c_re", "s5_c_im", "s5_d",
             "s5_w_glu", "s5_b_glu", "wo_in", "wo_out", "q_norm_g", "k_norm_g", "final_g"]
    for name in names:
        declare(f"in_{name}", np.ascontiguousarray(inputs[name]))
    freqs = 10000.0 ** (-np.arange(HD // 4, dtype=np.float32) / np.float32(HD // 4))
    ang = np.concatenate([(p.astype(np.float32) * freqs).astype(np.float32) for p in _ROPE], axis=1)
    declare("identity", np.eye(P, dtype=np.float32))
    declare("rope_cos", np.cos(ang).astype(np.float32))
    declare("rope_sin", np.sin(ang).astype(np.float32))
    out = nc.dram_tensor("out", (1, SEQ, D), F32, kind="ExternalOutput").ap()
    build(nc, *args, out)
    r = run_bass_kernel_spmd(nc, [arrays], core_ids=[0])
    return r.results[0]["out"]
```

```python
import math
from contextlib import ExitStack

import numpy as np

from concourse import mybir

F32 = mybir.dt.float32
F32R = mybir.dt.float32r
I32 = mybir.dt.int32
ACT = mybir.ActivationFunctionType
ALU = mybir.AluOpType
AX = mybir.AxisListType

P = 128
D = 1024
KT = D // P
NCTX, SEQ = 256, 1024
TOK = NCTX + SEQ
CT, LT = NCTX // P, SEQ // P
TT = CT + LT
EPS = 1e-6
W = 512
FB = W // P
CH = 8
G = 32
HC = 16
NS = 64
NCH = TOK // CH
CCH = NCTX // CH
HD = 128
NH = 8
NKV = 2
HPK = NH // NKV
SLOT = 4096
NSLOT = 3
QC = 256
CHUNKS = [(0, 256), (256, 512), (768, 512)]
LN2_HI, LN2_LO = 0.693359375, -2.12194440e-4
PIO2 = (1.5703125, 4.83751296997e-4, 7.54978995489e-8)


def build(nc, x, c, ctx_in, c_ctx, norm_g, w_mod, b_mod, we_in, we_out, gm_v_g, gm_w_s, gm_b_s,
          s5_lam_re, s5_lam_im, s5_log_dt, s5_b_re, s5_b_im, s5_c_re, s5_c_im, s5_d,
          s5_w_glu, s5_b_glu, wo_in, wo_out, q_norm_g, k_norm_g, final_g,
          ident_in, cos_in, sin_in, out):
    with ExitStack() as es:
        def sb(name, n, dt=F32):
            return es.enter_context(nc.sbuf_tensor(name, [P, n], dt))

        def sem(name):
            return es.enter_context(nc.semaphore(name))

        bop_d = nc.dram_tensor("bop_scratch", (2, P, 2, 16, P), F32, kind="Internal").ap()
        ct_d = nc.dram_tensor("cop_t_scratch", (4, P, 3, 8, P), F32, kind="Internal").ap()
        gate_d = nc.dram_tensor("gate_scratch", (LT, NKV, P, HPK, P), F32, kind="Internal").ap()
        x1_d = nc.dram_tensor("x1_scratch", (SEQ, D), F32, kind="Internal").ap()

        def region(name, n, *layouts):
            got = []
            for i, parts in enumerate(layouts):
                with ExitStack() as own:
                    at = 0
                    for part, offset, words in parts:
                        if offset > at:
                            own.enter_context(nc.sbuf_tensor(f"{name}_skip{i}_{at}", [P, offset - at], F32))
                        got.append(own.enter_context(nc.sbuf_tensor(part, [P, words], F32R))[:, :])
                        at = offset + words
            return [sb(name, n)] + got

        RA, a_hi, ot_hi_a, p_lo, p_hi = region("region_a", 10240, [("a_hi", 0, 10240)],
                                               [("ot_hi_a", 0, 5120), ("p_lo", 5120, 2560), ("p_hi", 7680, 2560)])
        RB, ones_r, nm, KTh, KTl, Vl = region(
            "region_b", 10240, [("ones_r", 1152, P), ("neg_max", 1280, 1024), ("k_t_hi", 5120, 2560), ("k_t_lo", 7680, 2560)],
            [("v_lo", 2560, 2560)])
        RC, c_lo, Vh, ot_hi_c = region("region_c", 10240, [("c_lo", 0, 10240)], [("v_hi", 0, 2560), ("ot_hi_c", 6144, 3072)])
        RD, OTl, qTh, qTl = region("region_d", (NCH + 1) * 2 * G, [("ot_lo", 0, 8192), ("q_t_hi", 8192, 1024), ("q_t_lo", 9216, 1024)])
        ring, *w_split = region("weight_ring", NSLOT * SLOT,
                                [(f"w_{part}{i}", i * SLOT + off, SLOT // 2) for i in range(NSLOT)
                                 for part, off in (("lo", 0), ("hi", SLOT // 2))])
        shared = sb("shared", 3072)
        ident = sb("ident", P)
        small = sb("small", 336)
        L8 = sb("lam8", P)
        rt = sb("rec_tmp", P)
        ps = es.enter_context(nc.psum_tensor("ps", [P, 8, 512], F32))

        def cutter(region, end):
            at = [0]

            def cut(n):
                a = region[:, at[0]:at[0] + n]
                at[0] += n
                assert at[0] <= end
                return a
            return cut

        sm = cutter(small, 336)
        NCOL = 84
        colv = sm(NCOL)
        cond = colv[:, 0:16].rearrange("p (c k) -> p k c", c=2)
        bmod = [colv[:, 16 + 24 * l:40 + 24 * l] for l in range(2)]
        ng = [colv[:, 64 + 8 * l:72 + 8 * l] for l in range(2)]
        bglu = colv[:, 80:84]
        modc = [sm(48).rearrange("p (b c) -> p b c", c=2) for _ in range(2)]
        hA = [sm(16).rearrange("p (k c) -> p k c", c=2) for _ in range(2)]
        ssq, msq, rstd = sm(10), sm(10), sm(10)
        smax = sm(8).rearrange("p (i h) -> p i h", i=2)
        rinv = sm(HPK)
        epsc, onec = sm(1), sm(1)
        bnst = sm(6)
        mv = sm(20).rearrange("p (t a) -> p t a", a=2)

        X = RA[:, :].rearrange("p (t f) -> p t f", f=D)
        vt = RA[:, 0:5120].rearrange("p (t f) -> p t f", f=W)
        Tsb = RA[:, 5120:9216].rearrange("p (g m) -> p g m", m=P)
        dskip = RA[:, 9216:9728].rearrange("p (g h) -> p g h", h=HC)
        wsraw = RA[:, 9728:10240].rearrange("p (g q) -> p g q", g=4)
        U = RA[:, 5120:10240].rearrange("p (g n) -> p g n", n=NCH)
        hi, lo = (q.rearrange("p (k t) -> p k t", t=TOK) for q in (a_hi, c_lo))
        NP, LAG = 5, 4
        p_lo, p_hi = (q.rearrange("p (s q) -> p s q", q=512) for q in (p_lo, p_hi))

        hT0 = RB[:, :].rearrange("p (k t) -> p k t", t=TOK)
        Hn = RB[:, :].rearrange("p (r g n) -> p r g n", r=2, n=NCH)
        Yt = RB[:, 0:4096].rearrange("p (s f) -> p s f", f=W)
        Ytc = RB[:, 4096:8192].rearrange("p (s f) -> p s f", f=W)
        x1 = RB[:, :].rearrange("p (t f) -> p t f", f=D)
        xr = RB[:, 0:8192].rearrange("p (t f) -> p t f", f=D)
        Kraw = RB[:, 0:2560].rearrange("p (t f) -> p t f", f=256)
        gst = RB[:, 0:1024].rearrange("p (a n) -> p a n", a=2)
        ones = RB[:, 1024:1152]
        Vt = RB[:, 2560:5120].rearrange("p (t f) -> p t f", f=256)
        KTh, KTl = (q.rearrange("p (j t) -> p j t", t=TOK) for q in (KTh, KTl))

        lraw = RC[:, 0:384].rearrange("p (a m) -> p a m", a=3)
        ldraw = RC[:, 384:386]
        colrow = RC[:, 1536:1664]
        craw = RC[:, 512:1536].rearrange("p (r q m) -> p r q m", r=2, m=P)
        BL = RC[:, 0:8192].rearrange("p (r g s h) -> p r g s h", r=2, g=G, h=HC)
        btmp = RC[:, 8192:9216].rearrange("p (g s h) -> p g s h", g=8, h=HC)
        bstage = RC[:, 9216:10240].rearrange("p (a m) -> p a m", a=2)
        Yl = RC[:, 0:4096].rearrange("p (g s c) -> p g s c", s=CH, c=HC)
        Yc = RC[:, 4096:8192].rearrange("p (g s c) -> p g s c", s=CH, c=HC)
        hperm = RC[:, 8192:10240].rearrange("p (k t) -> p k t", t=NCTX)
        mixT = RC[:, :].rearrange("p (k t) -> p k t", t=TOK)
        qTh, qTl = (q.rearrange("p (i h q) -> p i h q", i=2, q=P) for q in (qTh, qTl))
        nm = nm.rearrange("p (i n) -> p i n", i=2)
        PF = [RC[:, a:a + 512] for a in (2560, 9216, 9728)] + [gst[:, 0], gst[:, 1]]
        Vl, Vh = (q.rearrange("p (t f) -> p t f", f=256) for q in (Vl, Vh))
        psum_p = RC[:, 3072:4096].rearrange("p (i n) -> p i n", i=2)
        GR = RC[:, 4096:4608]
        gbuf = RC[:, 5120:6144].rearrange("p (i n) -> p i n", i=2)
        OTh = [(ot_hi_a[:, D * t:D * t + D] if t < 5 else ot_hi_c[:, D * (t - 5):D * (t - 4)]).rearrange("p (h q) -> p h q", q=P)
               for t in range(LT)]
        fjunk = RC[:, 0:1024]
        zt = RA[:, 5120:7168].rearrange("p (a n) -> p a n", a=8)

        braw = RD[:, 0:1024].rearrange("p (r g h) -> p r g h", r=2, h=HC)
        cltmp = RD[:, 0:576].rearrange("p (g k o) -> p g k o", g=4, o=HC)
        BB = RD[:, 1024:2048].rearrange("p (r g h) -> p r g h", r=2, h=HC)
        Cx = RD[:, 2048:3072].rearrange("p (r g h) -> p r g h", r=2, h=HC)
        Kt = RD[:, 3072:5120].rearrange("p (g k o) -> p g k o", k=CH, o=HC)
        CL = RD[:, 5120:9728].rearrange("p (r g k o) -> p r g k o", r=2, g=16, o=HC)
        ctmp = RD[:, 9728:10240]
        vgb = RD[:, 9728:10240]
        ddtmp = RD[:, 10240:10304].rearrange("p (g o) -> p g o", o=HC)
        H = RD[:, :].rearrange("p (i r g) -> p i r g", r=2, g=G)
        ys = RD[:, 0:5120].rearrange("p (g n) -> p g n", n=NCH)
        yT = RD[:, 5120:10240].rearrange("p (k t) -> p k t", t=TOK)
        otmp = RD[:, 0:512].rearrange("p (a n) -> p a n", a=2)
        xjunk = RD[:, 1024:2048]
        xn = [x1[:, t] if t < 4 else RD[:, 2048 + D * (t - 4):2048 + D * (t - 3)] for t in range(TT)]
        Qt = RD[:, 0:8192].rearrange("p (t f) -> p t f", f=D)
        OT = RD[:, 0:8192].rearrange("p (t h q) -> p t h q", h=NH, q=P)
        OTl = OTl.rearrange("p (t h q) -> p t h q", h=NH, q=P)
        rope_t = [RD[:, 8192 + 512 * i:8704 + 512 * i] for i in range(2)]
        cs = RD[:, 9216:10240].rearrange("p (a t m) -> p a t m", a=2, m=64)

        shc = cutter(shared, 3072)
        lamr, lami, ldt = shc(G), shc(G), shc(G)
        s5t = [shc(G) for _ in range(24)]
        ki, kj = shc(G).bitcast(I32), shc(G).bitcast(I32)
        LP = shc(9 * 64).rearrange("p (k r g) -> p k r g", r=2, g=G)
        LPc = shc(9 * 64).rearrange("p (k r g) -> p k r g", r=2, g=G)
        LPb = shc(8 * 64).rearrange("p (k r g) -> p k r g", r=2, g=G)
        gtb = shared[:, 0:2048].rearrange("p (c f) -> p c f", c=2)
        wsT = shared[:, 2048:2560].rearrange("p (g q) -> p g q", g=4)
        bsb = shared[:, 2560:3072]
        fgb = shared[:, 1024:2048]
        qjunk = shared[:, 2304:2560]
        qss, qms, qrs = (shared[:, 2048 + 84 * i:2132 + 84 * i] for i in range(3))

        s_ld_const, s_ld_par, s_ld_b, s_ld_v, s_ld_ws, s_ld_bs = (
            sem("ld_const"), sem("ld_par"), sem("ld_b"), sem("ld_v"), sem("ld_ws"), sem("ld_bs"))
        s_ld_tab, s_ld_gain, s_ld_fin, s_stored, s_w_hi, s_w_lo = (
            sem("ld_tab"), sem("ld_gain"), sem("ld_fin"), sem("stored"), sem("w_hi"), sem("w_lo"))
        s_mod_row, s_mod_tr, s_lam_ok, s_mod_ev, s_rt0, s_rs0, s_xna, s_xnp, s_h_ev = (
            sem("mod_row"), sem("mod_tr"), sem("lam_ok"), sem("mod_ev"), sem("rt0"), sem("rs0"), sem("xna"), sem("xnp"), sem("h_ev"))
        s_x1 = [sem(f"x1_{i}") for i in range(4)]
        s_gate_out, s_gate_in = ([sem(f"{n}{i}") for i in range(2)] for n in ("gate_out", "gate_in"))
        s_mix_hi, s_mix_lo, s_sq1, s_rt1, s_xn1, s_h1_tr = (
            sem("mix_hi"), sem("mix_lo"), sem("sq1"), sem("rt1"), sem("xn1"), sem("h1_tr"))
        s_h1_hi, s_h1_t, s_h1_lo, s_a_oh, s_a_ol = (
            sem("h1_hi"), sem("h1_t"), sem("h1_lo"), sem("a_oh"), sem("a_ol"))
        s_chain, s_pchain, s_lraw_ok, s_par_tr, s_par_ok, s_cond_ok = (
            sem("chain"), sem("pchain"), sem("lraw_ok"), sem("par_tr"), sem("par_ok"), sem("cond_ok"))
        s_col_ok, s_mod_mm, s_mod_ok, s_sq, s_rt_req, s_rt_ok = (
            sem("col_ok"), sem("mod_mm"), sem("mod_ok"), sem("sq"), sem("rt_req"), sem("rt_ok"))
        s_h_tr, s_h_eva, s_h_evd, s_v_mm, s_v_ev = (
            sem("h_tr"), sem("h_eva"), sem("h_evd"), sem("v_mm"), sem("v_ev"))
        s_vn_ok, s_vg_ok, s_bl_ok, s_bl_tr, s_bl_ev, s_cl_ok = (
            sem("vn_ok"), sem("vg_ok"), sem("bl_ok"), sem("bl_tr"), sem("bl_ev"), sem("cl_ok"))
        s_cop_out, s_k_mm, s_k_ev, s_t_in, s_t_out, s_par_dead = (
            sem("cop_out"), sem("k_mm"), sem("k_ev"), sem("t_in"), sem("t_out"), sem("par_dead"))
        s_hperm_ok, s_xs_mm, s_xs_eva, s_xs_evd, s_ws_tr, s_ws_ev = (
            sem("hperm_ok"), sem("xs_mm"), sem("xs_eva"), sem("xs_evd"), sem("ws_tr"), sem("ws_ev"))
        s_u_tr, s_u_ev, s_b_mm, s_b_evf, s_b_evb, s_gt_tr = (
            sem("u_tr"), sem("u_ev"), sem("b_mm"), sem("b_evf"), sem("b_evb"), sem("gt_tr"))
        s_gt_ev, s_rec, s_rec_ok, s_f_mm, s_f_ev, s_ga_ok = (
            sem("gt_ev"), sem("rec"), sem("rec_ok"), sem("f_mm"), sem("f_ev"), sem("ga_ok"))
        s_gm_mm, s_gm_ok, s_hn_f, s_hn_b, s_c_mm, s_c_ev = (
            sem("gm_mm"), sem("gm_ok"), sem("hn_f"), sem("hn_b"), sem("c_mm"), sem("c_ev"))
        s_y1_tr, s_y1_eva, s_y1_evd, s_y2_tr, s_y2_eva, s_y2_evd = (
            sem("y1_tr"), sem("y1_eva"), sem("y1_evd"), sem("y2_tr"), sem("y2_eva"), sem("y2_evd"))
        s_glu_mm, s_glu_sg, s_glu_ok, s_o_mm, s_o_t = (
            sem("glu_mm"), sem("glu_sg"), sem("glu_ok"), sem("o_mm"), sem("o_t"))
        s_o_ok, s_kv_mm, s_kv_ev, s_q_mm, s_q_ev, s_g_mm = (
            sem("o_ok"), sem("kv_mm"), sem("kv_ev"), sem("q_mm"), sem("q_ev"), sem("g_mm"))
        s_g_ev, s_k_ok, s_q_ok, s_kt_tr, s_kt_hi, s_kt_lo = (
            sem("g_ev"), sem("k_ok"), sem("q_ok"), sem("kt_tr"), sem("kt_hi"), sem("kt_lo"))
        s_hd_sq, s_hd_rt, s_ones = (
            sem("hd_sq"), sem("hd_rt"), sem("ones"))
        s_a_qT, s_a_qh, s_a_ql, s_a_mx, s_a_max, s_a_nt, s_a_nm = (
            sem("a_qT"), sem("a_qh"), sem("a_ql"), sem("a_mx"), sem("a_max"), sem("a_nt"), sem("a_nm"))
        s_a_ri, s_a_rt = sem("a_ri"), sem("a_rt")
        s_v_hi, s_v_lo, s_a_ph, s_a_pld, s_a_plp = (
            sem("v_hi"), sem("v_lo"), sem("a_ph"), sem("a_pld"), sem("a_plp"))
        s_a_s, s_a_p, s_a_sum, s_a_sm, s_a_gr, s_a_pv, s_a_o = (
            sem("a_s"), sem("a_p"), sem("a_sum"), sem("a_sm"), sem("a_gr"), sem("a_pv"), sem("a_o"))
        s_z_mm, s_z_t, s_z_ok, s_fin_sq, s_fin_rt, s_fin_g = (
            sem("z_mm"), sem("z_t"), sem("z_ok"), sem("fin_sq"), sem("fin_rt"), sem("fin_g"))
        s_bop_out = [sem(f"bop_out{i}") for i in range(2)]
        ld_x = [sem(f"ld_x{i}") for i in range(5)]
        w_in = [sem(f"w_in{i}") for i in range(NSLOT)]

        M = [("mod0", b) for b in range(6)] + [("mod1", b) for b in range(6)]
        early = [(M[0], 0), (M[1], 1), (M[2], 2), (M[3], 0), (("v", 0), 1), (("xs", 0), 2), (M[4], 0), (M[5], 0), (M[6], 1),
                 (M[7], 0), (M[8], 1), (M[9], 0), (("bop", 0), 1), (("bop", 1), 0), (("u", 0), 2), (("ga", 0), 1),
                 (("gb", 0), 0), (M[10], 2), (M[11], 1), (("ct", 0), 2), (("ct", 1), 1), (("ct", 2), 0)]
        splits = [("out0", q) for q in range(4)] + [("kv", q) for q in range(2)]
        splits += [(kind, q) for kind in ("q", "gate", "out1") for q in range(4)]
        late = [("ct", 3), ("glu", 0)] + splits
        uses = [u for u, _ in early] + late
        slots = [i for _, i in early] + [2 - i % NSLOT for i in range(len(late))]
        place = {u: (slots[i], slots[:i].count(slots[i])) for i, u in enumerate(uses)}
        before = {u: ([None] + [w for w in uses[:i] if place[w][0] == place[u][0]])[-1] for i, u in enumerate(uses)}
        done_when = {M[m]: (s_mod_tr, m + 1) for m in range(12)}
        done_when |= {("v", 0): (s_v_mm, TT), ("xs", 0): (s_xs_mm, CH + 2), ("u", 0): (s_f_mm, 12), ("ga", 0): (s_f_mm, 24),
                      ("gb", 0): (s_f_mm, 36), ("glu", 0): (s_glu_mm, 12)}
        done_when |= {("bop", b): (s_b_mm, 16 * (b + 1)) for b in range(2)}
        done_when |= {("kv", b): (s_kv_mm, TT * (b + 1)) for b in range(2)}
        for b in range(4):
            done_when |= {("ct", b): (s_c_mm, 4 * (b + 1)), ("out0", b): (s_o_mm, TT * (b + 1)), ("q", b): (s_q_mm, LT * (b + 1)),
                          ("gate", b): (s_g_mm, 4 * (b + 1)), ("out1", b): (s_z_mm, LT * (b + 1))}
        source = {"v": (we_in, W), "xs": (we_in, 3 * W), "u": (we_in, 0), "ga": (we_in, 2 * W), "gb": (we_in, 4 * W),
                  "mod0": (w_mod[0:1], 0), "mod1": (w_mod[1:2], 0), "out0": (we_out, 0), "out1": (wo_out, 0),
                  "kv": (wo_in, D), "q": (wo_in, 0), "gate": (wo_in, D + 512)}

        def slot(u):
            i = place[u][0]
            return ring[:, i * SLOT:(i + 1) * SLOT]

        def slot_kn(u):
            return slot(u).rearrange("p (k n) -> p k n", n=512)

        def slot_raw(u):
            return slot(u)[:, 0:SLOT // 2].rearrange("p (k n) -> p k n", n=QC)

        def slot_parts(u):
            i = place[u][0]
            return [q.rearrange("p (k n) -> p k n", n=QC) for q in (w_split[2 * i + 1], w_split[2 * i])]

        after_v = {2: [("lags", 0)], 4: [("bop", 0)], 5: [("bop", 4)], 6: [("bop", 8)],
                   7: [("bop", 12), ("rows", 4)], 8: [("cols", 4), ("lags", 1)]}
        after_xs = {0: [("rows", 5)], 1: [("cols", 5), ("rows", 6)], 2: [("cols", 6)], 3: [("rows", 7)],
                    4: [("cols", 7), ("rows", 8)], 5: [("cols", 8)], 6: [("rows", 9)], 7: [("cols", 9)]}

        on_pool = (1, 3, 5)

        def p_rest_done(m):
            n = len(on_pool) * (m // TT) + sum(t <= m % TT for t in on_pool)
            return (s_a_plp, n) if m % TT in on_pool else (s_a_pld, m + 1 - n)

        block = es.enter_context(nc.Block())

        @block.sync
        def _(sp):
            def ring_load(kind, b):
                u = (kind, b)
                if before[u]:
                    sp.wait_ge(*done_when[before[u]])
                dst = slot(u)
                if kind == "bop":
                    if b == 0:
                        sp.wait_ge(s_bop_out[0], 16 * 8)
                        sp.wait_ge(s_bop_out[1], 16 * 8)
                    src = bop_d[b].rearrange("p r g m -> p (r g m)")
                elif kind == "ct":
                    if b == 0:
                        sp.wait_ge(s_cop_out, 16 * 16)
                        sp.wait_ge(s_t_out, 16 * 4)
                    dst, src = dst[:, 0:3072], ct_d[b].rearrange("p r g m -> p (r g m)")
                elif kind == "glu":
                    dst = dst[:, 0:2048].rearrange("p (k n) -> p k n", n=512)
                    src = s5_w_glu[0].rearrange("(k p) n -> p k n", p=P)
                elif u in splits:
                    wt, a = source[kind]
                    dst = slot_raw(u)
                    src = wt[0][:, a + QC * b:a + QC * b + QC].rearrange("(k p) n -> p k n", p=P)
                else:
                    wt, a = source[kind]
                    dst = dst.rearrange("p (k n) -> p k n", n=512)
                    src = wt[0][:, a + 512 * b:a + 512 * b + 512].rearrange("(k p) n -> p k n", p=P)
                sp.dma_start(dst, src).then_inc(w_in[place[u][0]], 16)

            def token_loads(dst, name):
                sp.dma_start(dst[:, 0:CT, :], ctx_in[0].rearrange("(t p) f -> p t f", p=P)).then_inc(name[0], 16)
                for t in range(0, LT, 2):
                    sp.dma_start(dst[:, CT + t:CT + t + 2, :],
                                 x[0, t * P:(t + 2) * P, :].rearrange("(t p) f -> p t f", p=P)).then_inc(name[1 + t // 2], 16)

            sp.dma_start(ident[:], ident_in).then_inc(s_ld_const, 16)
            r0 = 0
            for rows in (c[0], c_ctx, b_mod[0], b_mod[1], norm_g[0], norm_g[1], s5_b_glu[0]):
                rows = rows.rearrange("(k p) -> k p", p=P)
                sp.dma_start(colrow[r0:r0 + rows.shape[0]], rows).then_inc(s_ld_const, 16)
                r0 += rows.shape[0]
            ring_load(*M[0])
            token_loads(X, ld_x)
            for u in uses[1:6]:
                ring_load(*u)
            sp.wait_ge(s_par_ok, 1)
            sp.dma_start(vgb, gm_v_g.broadcast_to([P, W])).then_inc(s_ld_v, 16)
            sp.wait_ge(s_h_tr, 24)
            sp.dma_start(dskip[0:HC].rearrange("p g h -> p (g h)"), s5_d.broadcast_to([HC, W])).then_inc(s_ld_ws, 16)
            sp.dma_start(wsraw, gm_w_s[0].rearrange("g p q -> p g q")).then_inc(s_ld_ws, 16)

            def cop_out(half):
                sp.wait_ge(s_cl_ok, half + 1)
                for q in range(2):
                    for r in range(2):
                        for d in range(2):
                            rows, k0 = slice(d * NS, (d + 1) * NS), 1 - d
                            sp.dma_start(ct_d[2 * half + q, rows, r].rearrange("p g (s o) -> p g s o", o=HC),
                                         CL[rows, r, 8 * q:8 * q + 8, k0:k0 + CH, :]).then_inc(s_cop_out, 16)

            def t_in(half):
                sp.wait_ge(s_k_ev, 4 * (half + 1))
                gs = slice(16 * half, 16 * half + 16)
                for s in range(CH):
                    rows = slice(HC * s, HC * s + HC)
                    sp.dma_start(Tsb[rows, gs, HC * s:P].rearrange("p g (k o) -> p g k o", o=HC),
                                 Kt[0:HC, :, 0:CH - s, :]).then_inc(s_t_in, 16)
                    if s:
                        sp.dma_start(Tsb[rows, gs, 0:HC * s].rearrange("p g (k o) -> p g k o", o=HC),
                                     Kt[32:32 + HC, :, 7 - s:7, :]).then_inc(s_t_in, 16)

            def t_out(half):
                sp.wait_ge(s_t_in, 16 * 15 * (half + 1))
                for q in range(2):
                    a = 16 * half + 8 * q
                    sp.dma_start(ct_d[2 * half + q, :, 2], Tsb[:, a:a + 8, :]).then_inc(s_t_out, 16)

            cop_out(0)
            t_in(0)
            t_out(0)
            ring_load(*M[4])
            for j in range(16):
                q, r = divmod(j, 2)
                sp.wait_ge(s_bl_ev, j + 1)
                sp.dma_start(bop_d[q // 4, :, r, 4 * (q % 4):4 * (q % 4) + 4, :],
                             bstage[:, j % 2].rearrange("p (g m) -> p g m", m=P)).then_inc(s_bop_out[j % 2], 16)
            cop_out(1)
            ring_load(*M[5])
            t_in(1)
            t_out(1)
            ring_load(*M[6])
            ring_load(*M[7])
            ring_load(*M[8])
            ring_load(*M[9])
            ring_load("bop", 0)
            ring_load("bop", 1)
            sp.wait_ge(s_par_dead, 1)
            sp.dma_start(bsb, gm_b_s[0].rearrange("g (o q) -> o (g q)", o=1).broadcast_to([P, 512])).then_inc(s_ld_bs, 16)
            for u in uses[uses.index(("u", 0)):uses.index(("out0", 1)) + 1]:
                ring_load(*u)
            sp.wait_ge(s_y2_tr, 12)
            token_loads(x1, ld_x)
            ring_load("out0", 2)
            sp.wait_ge(s_glu_ok, 12)
            sp.dma_start(cs[:, 0], cos_in.rearrange("(t p) m -> p t m", p=P)).then_inc(s_ld_tab, 16)
            sp.dma_start(cs[:, 1], sin_in.rearrange("(t p) m -> p t m", p=P)).then_inc(s_ld_tab, 16)
            sp.dma_start(L8[:], q_norm_g.broadcast_to([P, HD])).then_inc(s_ld_gain, 16)
            sp.dma_start(rt[:], k_norm_g.broadcast_to([P, HD])).then_inc(s_ld_gain, 16)
            ring_load("out0", 3)
            ring_load("kv", 0)
            ring_load("kv", 1)
            xd = x1_d.rearrange("(t p) f -> p t f", p=P)
            for q in range(4):
                sp.wait_ge(s_o_ok, 3 * TT + CT + 2 * q + 2)
                sp.dma_start(xd[:, 2 * q:2 * q + 2], x1[:, CT + 2 * q:CT + 2 * q + 2, :]).then_inc(s_x1[q], 16)
            for u in uses[uses.index(("q", 0)):uses.index(("gate", 2)) + 1]:
                ring_load(*u)
            for j in range(2 * NH):
                h, half = divmod(j, 2)
                sp.wait_ge(s_g_ev, j + 1)
                sp.dma_start(gate_d[4 * half:4 * half + 4, h // HPK, :, h % HPK, :].rearrange("b p q -> p b q"),
                             gst[:, half].rearrange("p (b q) -> p b q", q=P)).then_inc(s_gate_out[half], 16)
                if j % 4 == 3:
                    ring_load(*uses[uses.index(("gate", 3)) + j // 4])
            for half in range(2):
                sp.wait_ge(s_gate_out[half], 16 * NH)
            for i in range(2 * LT):
                if i >= 2:
                    sp.wait_ge(s_a_gr, i - 1)
                sp.dma_start(gbuf[:, i % 2], gate_d[i // 2, i % 2].rearrange("p h q -> p (h q)")).then_inc(s_gate_in[i % 2], 16)
                if i == 0:
                    sp.wait_ge(s_q_ok, 4 * LT)
                    sp.wait_ge(s_gt_ev, 6)
                    sp.dma_start(fgb, final_g.rearrange("(o f) -> o f", o=1).broadcast_to([P, D])).then_inc(s_ld_fin, 16)
            sp.wait_ge(s_a_o, 2 * LT)
            for q in range(4):
                sp.wait_ge(s_x1[q], 16)
                sp.dma_start(xr[:, 2 * q:2 * q + 2], xd[:, 2 * q:2 * q + 2]).then_inc(s_x1[q], 16)
            ring_load("out1", 3)
            for t in range(LT):
                sp.wait_ge(s_fin_g, t + 1)
                sp.dma_start(out[0, t * P:(t + 1) * P, :], xr[:, t, :]).then_inc(s_stored, 16)
            sp.wait_ge(s_stored, 16 * LT)

        @block.gpsimd
        def _(pool):
            g = nc.gpsimd
            n = [0]

            def step(ins):
                n[0] += 1
                ins.then_inc(s_pchain, 1)
                pool.wait_ge(s_pchain, n[0])

            pool.wait_ge(s_rs0, 1)
            for t in range(1, TT, 2):
                g.tensor_scalar(X[:, t], X[:, t], rstd[:, t:t + 1], None, ALU.mult).then_inc(s_xnp, 1)

            pool.wait_ge(s_par_ok, 1)
            for q in range(4):
                gs = slice(8 * q, 8 * q + 8)
                L = [LPb[:, :, r, gs].rearrange("p s g -> p g s").unsqueeze(3).broadcast_to([P, 8, CH, HC])
                     for r in range(2)]
                B = [BB[:, r, gs, :].unsqueeze(2).broadcast_to([P, 8, CH, HC]) for r in range(2)]
                step(g.tensor_tensor(BL[:, 0, gs], B[0], L[0], ALU.mult))
                step(g.tensor_tensor(btmp, B[1], L[1], ALU.mult))
                step(g.tensor_tensor(BL[:, 0, gs], BL[:, 0, gs], btmp, ALU.subtract))
                step(g.tensor_tensor(BL[:, 1, gs], B[0], L[1], ALU.mult))
                step(g.tensor_tensor(btmp, B[1], L[0], ALU.mult))
                g.tensor_tensor(BL[:, 1, gs], BL[:, 1, gs], btmp, ALU.add).then_inc(s_bl_ok, 1)
                pool.wait_ge(s_bl_ok, q + 1)
            def weights_rest(u):
                pool.wait_ge(s_w_hi, splits.index(u) + 1)
                wh, wl = slot_parts(u)
                g.tensor_tensor(wl, slot_raw(u), wh.bitcast(F32), ALU.subtract).then_inc(s_w_lo, 1)

            pool.wait_ge(s_ld_v, 16)
            for t in range(TT):
                pool.wait_ge(s_vn_ok, t + 1)
                g.tensor_tensor(vt[:, t], vt[:, t], vgb, ALU.mult).then_inc(s_vg_ok, 1)
            j = 0
            for fb in range(FB):
                for t0, nt in CHUNKS:
                    pool.wait_ge(s_f_ev, 12 + j + 1)
                    g.tensor_tensor(mixT[:, fb, t0:t0 + nt], mixT[:, fb, t0:t0 + nt], mixT[:, FB + fb, t0:t0 + nt],
                                    ALU.mult).then_inc(s_ga_ok, 1)
                    j += 1
            def mix_rest(j, k, t0, nt):
                pool.wait_ge(s_mix_hi, j)
                g.tensor_tensor(lo[:, k, t0:t0 + nt], mixT[:, k, t0:t0 + nt], hi[:, k, t0:t0 + nt].bitcast(F32),
                                ALU.subtract).then_inc(s_mix_lo, 1)

            mix_rest(1, slice(0, FB), 0, TOK)
            weights_rest(("out0", 0))
            for j in range(12):
                mix_rest(2 + j, FB + j // 3, *CHUNKS[j % 3])
            weights_rest(("out0", 1))
            for j in range(4 * TT):
                q, t = divmod(j, TT)
                pool.wait_ge(s_o_t, j + 1)
                if q == 0:
                    pool.wait_ge(ld_x[t // 2], 32)
                xs_ = x1[:, t, QC * q:QC * q + QC]
                g.tensor_tensor(xs_, xs_, otmp[:, j % 2], ALU.add).then_inc(s_o_ok, 1)
                if t == 4 and q < 3:
                    weights_rest(splits[2 + q])
            for q, (t0, nt) in enumerate(CHUNKS):
                for k in range(KT):
                    pool.wait_ge(s_h1_hi, KT * q + k + 1)
                    g.tensor_tensor(lo[:, k, t0:t0 + nt], mixT[:, k, t0:t0 + nt], hi[:, k, t0:t0 + nt].bitcast(F32),
                                    ALU.subtract).then_inc(s_h1_lo, 1)
            for u in splits[5:15]:
                weights_rest(u)
            def output_rest(i):
                pool.wait_ge(s_a_oh, i + 1)
                b, hs = i // 2, slice(HPK * (i % 2), HPK * (i % 2) + HPK)
                g.tensor_tensor(OTl[:, b, hs], OT[:, b, hs], OTh[b][:, hs].bitcast(F32), ALU.subtract).then_inc(s_a_ol, 1)

            for m in range(TT * 2 * LT):
                i, t = divmod(m, TT)
                if t == 0 and i in (1, 2):
                    weights_rest(("out1", i))
                if t:
                    pool.wait_ge(s_a_p, m + 1)
                    if t == 1 and i >= 2:
                        pool.wait_ge(s_a_sm, i - 1)
                    if t >= 2:
                        pool.wait_ge(s_a_sum, 9 * i + t - 1)
                    g.tensor_tensor(psum_p[:, i % 2], PF[(m - 1) % NP] if t == 1 else psum_p[:, i % 2], PF[m % NP],
                                    ALU.add).then_inc(s_a_sum, 1)
                if t in on_pool:
                    pool.wait_ge(s_a_ph, m + 1)
                    g.tensor_tensor(p_lo[:, m % NP], PF[m % NP], p_hi[:, m % NP].bitcast(F32), ALU.subtract).then_inc(s_a_plp, 1)
                if t == 0 and i >= 2:
                    output_rest(i - 2)
            output_rest(2 * LT - 2)
            output_rest(2 * LT - 1)
            for j in range(4 * LT):
                q, t = divmod(j, LT)
                pool.wait_ge(s_z_t, j + 1)
                if q == 0:
                    pool.wait_ge(s_x1[t // 2], 32)
                xs_ = xr[:, t, QC * q:QC * q + QC]
                g.tensor_tensor(xs_, xs_, zt[:, j % 8], ALU.add).then_inc(s_z_ok, 1)
                if j == 11:
                    weights_rest(("out1", 3))

        @block.scalar
        def _(act):
            a = nc.scalar

            def copy(o, i):
                return a.activation(o, i, ACT.Copy)

            for k, tensor in enumerate((s5_lam_re, s5_lam_im)):
                act.dma_start(lraw[0:G, k].rearrange("g (d p) -> g d p", d=2),
                              tensor[0].rearrange("d g p -> g d p")).then_inc(s_ld_par, 16)
            act.dma_start(ldraw[0:G], s5_log_dt[0].rearrange("d g -> g d"), allow_slow_non_contiguous=True).then_inc(s_ld_par, 16)
            for r, tensor in enumerate((s5_c_re, s5_c_im)):
                for d in range(2):
                    act.dma_start(craw[:, r, :, d * NS:(d + 1) * NS],
                                  tensor[0, d].rearrange("(q g) h p -> (g h) q p", q=4)).then_inc(s_ld_par, 16)
            for r, tensor in enumerate((s5_b_re, s5_b_im)):
                for d in range(2):
                    act.dma_start(braw[d * NS:(d + 1) * NS, r],
                                  tensor[0, d].rearrange("g p h -> p g h")).then_inc(s_ld_b, 16)

            def squares(Xt, junk, t, done):
                if t:
                    act.wait_ge(done, t)
                a.activation(junk, Xt, ACT.Square, accum_out=ssq[:, t:t + 1]).then_inc(done, 1)

            def weights_round(u):
                act.wait_ge(w_in[place[u][0]], 16 * (place[u][1] + 1))
                copy(slot_parts(u)[0], slot_raw(u)).then_inc(s_w_hi, 1)

            def mod_row(m):
                act.wait_ge(s_mod_mm, m + 1)
                copy(slot(M[m])[0:2, 0:512], ps[0:2, 6, :]).then_inc(s_mod_row, 1)

            def bop_evac(j):
                act.wait_ge(s_bl_tr, j + 1)
                if j >= 2:
                    act.wait_ge(s_bop_out[j % 2], 16 * (j // 2))
                copy(bstage[:, j % 2], ps[:, j % 4, :]).then_inc(s_bl_ev, 1)

            def between_tiles(work):
                for kind, i in work:
                    if kind == "rows":
                        mod_row(i)
                    if kind == "bop":
                        for j in range(i, i + 4):
                            bop_evac(j)

            act.wait_ge(s_col_ok, 1)
            a.activation(cond, cond, ACT.Silu).then_inc(s_cond_ok, 1)
            for t in range(TT):
                act.wait_ge(ld_x[t // 2], 16)
                squares(X[:, t], RB[:, 0:D], t, s_sq)
                if t == 5:
                    mod_row(0)
            act.wait_ge(s_sq, TT)
            a.activation(rstd, ssq, ACT.Sqrt, bias=epsc, scale=1.0 / D).then_inc(s_rt0, 1)
            mod_row(1)
            act.wait_ge(s_rs0, 1)
            for t in range(0, TT, 2):
                a.activation(X[:, t], X[:, t], ACT.Copy, scale=rstd[:, t:t + 1]).then_inc(s_xna, 1)
            for q, (t0, nt) in enumerate(CHUNKS):
                for k in range(KT):
                    j = KT * q + k
                    act.wait_ge(s_h_tr, j + 1)
                    copy(hT0[:, k, t0:t0 + nt], ps[:, j % 4, 0:nt]).then_inc(s_h_ev, 1)
                if q < 2:
                    mod_row(q + 2)
            act.wait_ge(s_mod_ok, 1)
            act.wait_ge(s_h_ev, 24)
            for q, (t0, nt) in enumerate(CHUNKS):
                ci = 1 if q == 0 else 0
                for k in range(0, KT, 2):
                    a.activation(hT0[:, k, t0:t0 + nt], hT0[:, k, t0:t0 + nt], ACT.Identity,
                                 bias=modc[0][:, k, ci:ci + 1], scale=hA[0][:, k, ci:ci + 1]).then_inc(s_h_eva, 1)
            for t in range(TT):
                act.wait_ge(s_v_mm, t + 1)
                copy(vt[:, t], ps[:, 4 + t % 2, :]).then_inc(s_v_ev, 1)
                between_tiles(after_v.get(t, ()))
            act.wait_ge(s_h_evd, 12)
            act.wait_ge(s_bop_out[0], 16 * 8)
            act.wait_ge(s_bop_out[1], 16 * 8)
            copy(hperm.rearrange("p k (s n) -> p k s n", s=CH),
                 hT0[:, :, 0:NCTX].rearrange("p k (n s) -> p k s n", s=CH)).then_inc(s_hperm_ok, 1)
            for s in range(CH):
                act.wait_ge(s_xs_mm, s + 1)
                copy(Yl[:, :, s, :], ps[:, 4 + s % 2, :].rearrange("p (g c) -> p g c", c=HC)).then_inc(s_xs_eva, 1)
                if s == 5:
                    act.wait_ge(s_rt_req, 1)
                    a.activation(rstd, msq, ACT.Sqrt).then_inc(s_rt_ok, 1)
                between_tiles(after_xs.get(s, ()))
            act.wait_ge(s_t_out, 16 * 4)
            act.wait_ge(s_ws_ev, 1)
            for j in range(11):
                m = min(3, G - 3 * j)
                act.wait_ge(s_u_tr, j + 1)
                copy(U[:, 3 * j:3 * j + m, :].rearrange("p g n -> p (g n)"), ps[:, j % 4, 0:m * NCH]).then_inc(s_u_ev, 1)
            act.wait_ge(s_cop_out, 16 * 16)
            act.wait_ge(s_t_in, 16 * 30)
            act.wait_ge(s_vg_ok, TT)
            for j in range(32):
                q, r = divmod(j, 2)
                act.wait_ge(s_b_mm, j + 1)
                copy(H[0:NS, 1:NCH + 1, r, 2 * q:2 * q + 2].rearrange("p n g -> p g n"),
                     ps[0:NS, j % 4, 0:2 * NCH].rearrange("p (g n) -> p g n", n=NCH)).then_inc(s_b_evf, 1)
            act.wait_ge(s_par_dead, 1)
            for j in range(4):
                act.wait_ge(s_gt_tr, j + 1)
                copy(gtb[:, j // 2, (j % 2) * 512:(j % 2) * 512 + 512], ps[:, 4 + j, :]).then_inc(s_gt_ev, 1)
            for part in range(3):
                for fb in range(FB):
                    for q, (t0, nt) in enumerate(CHUNKS):
                        j = 12 * part + 3 * fb + q
                        act.wait_ge(s_f_mm, j + 1)
                        if part == 2:
                            act.wait_ge(s_ga_ok, 3 * fb + q + 1)
                        a.activation(mixT[:, (FB if part else 0) + fb, t0:t0 + nt], ps[:, j % 4, 0:nt],
                                     ACT.Silu if part else ACT.Copy).then_inc(s_f_ev, 1)
            act.wait_ge(s_rec_ok, 1)
            for r in range(2):
                mod_row(10 + r)
                copy(Hn[0:NS, r], H[0:NS, 0:NCH, r, :].rearrange("p n g -> p g n")).then_inc(s_hn_f, 1)
            act.wait_ge(s_gm_ok, TT)
            copy(hi[:, 0:FB], mixT[:, 0:FB]).then_inc(s_mix_hi, 1)
            act.wait_ge(s_hn_f, 2)
            act.wait_ge(s_hn_b, 4)
            for j in range(16):
                act.wait_ge(s_c_mm, j + 1)
                a.activation(ys[:, 2 * j:2 * j + 2, :], ps[:, 4 + j % 4, 0:2 * NCH].rearrange("p (g n) -> p g n", n=NCH),
                             ACT.Gelu_apprx_tanh).then_inc(s_c_ev, 1)
            for j in range(8):
                act.wait_ge(s_y1_tr, 2 * j + 1)
                copy(Yt[:, :, 64 * j:64 * j + 64].rearrange("p s (g o) -> p g s o", o=HC),
                     ps[:, 2 * (j % 2), :].rearrange("p (g s o) -> p g s o", g=4, o=HC)).then_inc(s_y1_eva, 1)
            for j in range(8):
                fb, q = divmod(j, 2)
                act.wait_ge(s_y2_tr, j + 1)
                copy(yT[:, fb, NCTX:TOK].rearrange("p (n s) -> p s n", s=CH)[:, 4 * q:4 * q + 4, :],
                     ps[:, 4 + j % 4, :].rearrange("p (s n) -> p s n", s=4)).then_inc(s_y2_eva, 1)
            weights_round(("out0", 0))

            def h1_evac(q):
                t0, nt = CHUNKS[q]
                for k in range(KT):
                    act.wait_ge(s_h1_t, KT * q + k + 1)
                    copy(hi[:, k, t0:t0 + nt], mixT[:, k, t0:t0 + nt]).then_inc(s_h1_hi, 1)

            def mix_round(j):
                fb, q = divmod(j, 3)
                t0, nt = CHUNKS[q]
                act.wait_ge(s_glu_ok, j + 1)
                copy(hi[:, FB + fb, t0:t0 + nt], mixT[:, FB + fb, t0:t0 + nt]).then_inc(s_mix_hi, 1)

            for j in range(12):
                act.wait_ge(s_glu_mm, j + 1)
                nt = CHUNKS[j % 3][1]
                a.activation(ps[:, j % 4, 0:nt], ps[:, j % 4, 0:nt], ACT.Sigmoid,
                             bias=bglu[:, j // 3:j // 3 + 1]).then_inc(s_glu_sg, 1)
                if j:
                    mix_round(j - 1)
            mix_round(11)
            for u in splits[1:5]:
                weights_round(u)
            def x1_norms(q, tiles):
                act.wait_ge(s_rs0, q + 1)
                for t in tiles:
                    if t == 3:
                        act.wait_ge(s_x1[0], 16)
                    a.activation(xn[t], x1[:, t], ACT.Copy, scale=rstd[:, t:t + 1]).then_inc(s_xna, 1)

            for q, (t0, nt) in enumerate(CHUNKS):
                for t in range(t0 // P, (t0 + nt) // P):
                    act.wait_ge(s_o_ok, 3 * TT + t + 1)
                    squares(x1[:, t], xjunk, t, s_sq1)
                act.wait_ge(s_sq1, (t0 + nt) // P)
                cols = slice(t0 // P, (t0 + nt) // P)
                a.activation(rstd[:, cols], ssq[:, cols], ACT.Sqrt, bias=epsc, scale=1.0 / D).then_inc(s_rt1, 1)
                if q == 2:
                    h1_evac(0)
                if q:
                    x1_norms(q, (4 * q - 1, 4 * q + 1))
            h1_evac(1)
            h1_evac(2)

            def head_squares(bank, c0, nh, seen):
                act.wait_ge(s_hd_sq, seen)
                for h in range(nh):
                    a.activation(qjunk[:, P * h:P * h + P], ps[:, bank, P * h:P * h + P], ACT.Square,
                                 accum_out=qss[:, c0 + h:c0 + h + 1]).then_inc(s_hd_sq, 1)

            def head_root(c0, n, seen):
                act.wait_ge(s_hd_sq, seen)
                a.activation(qrs[:, c0:c0 + n], qss[:, c0:c0 + n], ACT.Sqrt, bias=epsc, scale=1.0 / HD).then_inc(s_hd_rt, 1)

            for q in range(4):
                act.wait_ge(s_x1[q], 16)
            for j in range(2 * TT):
                part, t = divmod(j, TT)
                act.wait_ge(s_kv_mm, j + 1)
                if part == 0:
                    head_squares(4 + j % 4, 64 + 2 * t, NKV, 2 * t)
                copy((Vt if part else Kraw)[:, t], ps[:, 4 + j % 4, 0:QC]).then_inc(s_kv_ev, 1)
                if j == TT - 1:
                    head_root(64, 20, 20)
                if t == 3:
                    weights_round(splits[5 + part])
            for j in range(4 * LT):
                q, t = divmod(j, LT)
                act.wait_ge(s_q_mm, j + 1)
                head_squares(j % 4, 2 * j, 2, 20 + 2 * j)
                copy(Qt[:, t, QC * q:QC * q + QC], ps[:, j % 4, 0:QC]).then_inc(s_q_ev, 1)
                if t == 3:
                    weights_round(splits[7 + q])
                if t == 7:
                    head_root(16 * q, 16, 22 + 2 * j)
                if j == 18:
                    for k in range(6):
                        act.wait_ge(s_kt_tr, k + 1)
                        h_, q_ = divmod(k, 3)
                        nt = 256 if q_ == 2 else 512
                        copy(KTh[:, h_, 512 * q_:512 * q_ + nt], ps[:, 4 + k % 4, 0:nt]).then_inc(s_kt_hi, 1)
                    for k in range(2):
                        act.wait_ge(s_gt_tr, k + 5)
                        copy(gtb[:, 0, 512 * k:512 * k + 512], ps[:, 6 + k, :]).then_inc(s_gt_ev, 1)
            def q_round(i):
                act.wait_ge(s_a_qT, i + 1)
                copy(qTh[:, i % 2], ps[:, 7, :].rearrange("p (h q) -> p h q", q=P)).then_inc(s_a_qh, 1)

            for j in range(2 * NH):
                act.wait_ge(s_g_mm, j + 1)
                if j >= 2:
                    act.wait_ge(s_gate_out[j % 2], 16 * (j // 2))
                a.activation(gst[:, j % 2], ps[:, 3 + j % 2, :], ACT.Silu).then_inc(s_g_ev, 1)
                if j % 4 == 1:
                    weights_round(splits[11 + j // 4])
                if j in (11, 12):
                    q_round(j - 11)
            act.wait_ge(s_g_mm, 2 * NH)
            copy(Vh, Vt).then_inc(s_v_hi, 1)

            def output_round(i):
                act.wait_ge(s_a_o, i + 1)
                b, hs = i // 2, slice(HPK * (i % 2), HPK * (i % 2) + HPK)
                copy(OTh[b][:, hs], OT[:, b, hs]).then_inc(s_a_oh, 1)

            for m in range(TT * 2 * LT):
                i, t = divmod(m, TT)
                if t == 0 and i in (1, 2):
                    weights_round(("out1", i))
                if t == 9 and i:
                    output_round(i - 1)
                act.wait_ge(s_a_s, m + 1)
                if m == 3:
                    for half in range(2):
                        act.wait_ge(s_gate_out[half], 16 * NH)
                if m >= NP:
                    i3, t3 = divmod(m - NP, TT)
                    act.wait_ge(s_a_ph, m - NP + 1)
                    act.wait_ge(*p_rest_done(m - NP))
                    act.wait_ge(s_a_sum, 9 * i3 + max(t3, 1))
                a.activation(PF[m % NP], ps[:, 3 + m % 2, :], ACT.Exp).then_inc(s_a_p, 1)
                act.wait_ge(s_a_p, m + 1)
                copy(p_hi[:, m % NP], PF[m % NP]).then_inc(s_a_ph, 1)
                if t == 9 and i + 2 < 2 * LT:
                    q_round(i + 2)
            output_round(2 * LT - 1)
            weights_round(("out1", 3))
            for t in range(LT):
                act.wait_ge(s_z_ok, 3 * LT + t + 1)
                a.activation(fjunk, xr[:, t], ACT.Square, accum_out=ssq[:, t:t + 1]).then_inc(s_fin_sq, 1)
                act.wait_ge(s_fin_sq, t + 1)
                a.activation(rstd[:, t:t + 1], ssq[:, t:t + 1], ACT.Sqrt, bias=epsc, scale=1.0 / D).then_inc(s_fin_rt, 1)

        @block.vector
        def _(dve):
            v = nc.vector
            n = [0]

            def step(ins):
                n[0] += 1
                ins.then_inc(s_chain, 1)
                dve.wait_ge(s_chain, n[0])

            def tt(o, a, b, op):
                step(v.tensor_tensor(o, a, b, op))

            def ts(o, a, s1, op1, s2=None, op2=ALU.bypass):
                step(v.tensor_scalar(o, a, s1, s2, op1, op2))

            def cp(o, a):
                step(v.tensor_copy(o, a))

            def refined(ss, m, rr):
                step(v.reciprocal(rr, rr))
                tt(ss, rr, rr, ALU.mult)
                tt(ss, ss, m, ALU.mult)
                ts(ss, ss, -0.5, ALU.mult, 1.5, ALU.add)
                tt(rr, rr, ss, ALU.mult)

            def row_rstd(c):
                ts(msq[:, c], ssq[:, c], 1.0 / D, ALU.mult, EPS, ALU.add)
                refined(ssq[:, c], msq[:, c], rstd[:, c])

            step(v.memset(epsc, EPS))
            step(v.memset(onec, 1.0))
            dve.wait_ge(s_par_tr, 1)
            v.tensor_copy(colv, ps[:, 6, 0:NCOL]).then_inc(s_col_ok, 1)
            dve.wait_ge(s_ld_par, 16 * 7)
            v.tensor_copy(lraw[0:G, 2].rearrange("g (d p) -> g d p", d=2),
                          ldraw[0:G].unsqueeze(2).broadcast_to([G, 2, NS])).then_inc(s_lraw_ok, 1)
            dve.wait_ge(s_par_tr, 2)
            for k, dst in enumerate((lamr, lami, ldt)):
                v.tensor_copy(dst, ps[:, 7, 32 * k:32 * k + 32]).then_inc(s_lam_ok, 1)
            dve.wait_ge(s_lam_ok, 3)
            (dt, xe, kf, rr, ex, mg, s_, c_, r2, odd, sg, sn, cn, lr, li, fr, fi, t1, t2, t3, den, msk, t4, th) = s5t

            def exp_(o, xin):
                ts(msk, xin, -87.0, ALU.is_ge)
                ts(t4, xin, -87.0, ALU.max, 88.0, ALU.min)
                ts(ki, t4, 1.0 / math.log(2.0), ALU.mult)
                cp(kf, ki)
                ts(t1, kf, -LN2_HI, ALU.mult)
                tt(rr, t4, t1, ALU.add)
                ts(t1, kf, -LN2_LO, ALU.mult)
                tt(rr, rr, t1, ALU.add)
                ts(ex, rr, 1.0 / 5040, ALU.mult, 1.0 / 720, ALU.add)
                for q in (120.0, 24.0, 6.0, 2.0, 1.0, 1.0):
                    tt(ex, ex, rr, ALU.mult)
                    ts(ex, ex, 1.0 / q, ALU.add)
                ts(kf, kf, 127.0, ALU.add)
                cp(ki, kf)
                ts(kj, ki, 23, ALU.logical_shift_left)
                tt(ex, ex, kj.bitcast(F32), ALU.mult)
                tt(o, ex, msk, ALU.mult)

            exp_(dt, ldt)
            tt(xe, lamr, dt, ALU.mult)
            exp_(mg, xe)
            tt(th, lami, dt, ALU.mult)
            ts(ki, th, 2.0 / math.pi, ALU.mult)
            cp(kf, ki)
            cp(rr, th)
            for q in PIO2:
                ts(t1, kf, -q, ALU.mult)
                tt(rr, rr, t1, ALU.add)
            tt(r2, rr, rr, ALU.mult)
            ts(s_, r2, 1.0 / 362880, ALU.mult, -1.0 / 5040, ALU.add)
            for q in (1.0 / 120, -1.0 / 6, 1.0):
                tt(s_, s_, r2, ALU.mult)
                ts(s_, s_, q, ALU.add)
            tt(s_, s_, rr, ALU.mult)
            ts(c_, r2, -1.0 / 3628800, ALU.mult, 1.0 / 40320, ALU.add)
            for q in (-1.0 / 720, 1.0 / 24, -0.5, 1.0):
                tt(c_, c_, r2, ALU.mult)
                ts(c_, c_, q, ALU.add)
            ts(kj, ki, 1, ALU.bitwise_and)
            cp(odd, kj)
            ts(sg, odd, -1.0, ALU.mult, 1.0, ALU.add)
            tt(sn, s_, sg, ALU.mult)
            tt(t1, c_, odd, ALU.mult)
            tt(sn, sn, t1, ALU.add)
            tt(cn, c_, sg, ALU.mult)
            tt(t1, s_, odd, ALU.mult)
            tt(cn, cn, t1, ALU.add)
            for o, add in ((sn, 0.0), (cn, 1.0)):
                ts(kf, kf, add, ALU.add)
                cp(ki, kf)
                ts(kj, ki, 1, ALU.logical_shift_right, 1, ALU.bitwise_and)
                cp(sg, kj)
                ts(sg, sg, -2.0, ALU.mult, 1.0, ALU.add)
                tt(o, o, sg, ALU.mult)
            tt(lr, mg, cn, ALU.mult)
            tt(li, mg, sn, ALU.mult)
            dve.wait_ge(s_rt0, 1)
            row_rstd(slice(0, TT))
            v.tensor_copy(small[:, 335:336], small[:, 0:1]).then_inc(s_rs0, 1)
            tt(den, lamr, lamr, ALU.mult)
            tt(t1, lami, lami, ALU.mult)
            tt(den, den, t1, ALU.add)
            step(v.reciprocal(den, den))
            ts(t3, lr, -1.0, ALU.add)
            tt(t1, t3, lamr, ALU.mult)
            tt(t2, li, lami, ALU.mult)
            tt(t1, t1, t2, ALU.add)
            tt(fr, t1, den, ALU.mult)
            tt(t1, li, lamr, ALU.mult)
            tt(t2, t3, lami, ALU.mult)
            tt(t1, t1, t2, ALU.subtract)
            tt(fi, t1, den, ALU.mult)
            step(v.memset(LP[:, 0, 0], 1.0))
            step(v.memset(LP[:, 0, 1], 0.0))
            cp(LP[:, 1, 0], lr)
            cp(LP[:, 1, 1], li)
            for m in (1, 2, 4):
                A = [LP[:, 1:m + 1, r] for r in range(2)]
                M = [LP[:, m, r].unsqueeze(1).broadcast_to([P, m, G]) for r in range(2)]
                O = [LP[:, m + 1:2 * m + 1, r] for r in range(2)]
                tmp = ctmp[:, 0:m * G].rearrange("p (m g) -> p m g", g=G)
                tt(O[0], A[0], M[0], ALU.mult)
                tt(tmp, A[1], M[1], ALU.mult)
                tt(O[0], O[0], tmp, ALU.subtract)
                tt(O[1], A[0], M[1], ALU.mult)
                tt(tmp, A[1], M[0], ALU.mult)
                tt(O[1], O[1], tmp, ALU.add)
            fwd, bwd = slice(0, NS), slice(NS, P)
            cp(LPc[fwd], LP[fwd])
            cp(LPc[bwd], LP[bwd, ::-1])
            cp(LPb[fwd], LP[fwd, 7::-1])
            cp(LPb[bwd], LP[bwd, 0:8])
            cp(L8[:, 0:32], LP[:, 8, 0])
            cp(L8[:, 32:64], LP[:, 8, 0])
            cp(L8[:, 64:96], LP[:, 8, 1])
            ts(L8[:, 96:128], LP[:, 8, 1], -1.0, ALU.mult)
            dve.wait_ge(s_ld_b, 16 * 4)
            F = [q.unsqueeze(2).broadcast_to([P, G, HC]) for q in (fr, fi)]
            tmp = ctmp.rearrange("p (g h) -> p g h", h=HC)
            tt(BB[:, 0], braw[:, 0], F[0], ALU.mult)
            tt(tmp, braw[:, 1], F[1], ALU.mult)
            tt(BB[:, 0], BB[:, 0], tmp, ALU.subtract)
            tt(BB[:, 1], braw[:, 1], F[0], ALU.mult)
            tt(tmp, braw[:, 0], F[1], ALU.mult)
            tt(BB[:, 1], BB[:, 1], tmp, ALU.add)
            dve.wait_ge(s_par_tr, 4)
            cp(Cx[:, 0], ps[:, 4, :].rearrange("p (g h) -> p g h", h=HC))
            v.tensor_scalar(Cx[:, 1], ps[:, 5, :].rearrange("p (g h) -> p g h", h=HC), -1.0, None,
                            ALU.mult).then_inc(s_par_ok, 1)
            dve.wait_ge(s_par_ok, 1)

            def mod_evac(l, k, b0, b1):
                dve.wait_ge(s_mod_tr, k)
                v.tensor_tensor(modc[l][:, b0:b1], ps[:, 7, 64 * l + 2 * b0:64 * l + 2 * b1].rearrange("p (b c) -> p b c", c=2),
                                bmod[l][:, b0:b1].unsqueeze(2).broadcast_to([P, b1 - b0, 2]), ALU.add).then_inc(s_mod_ev, 1)
                dve.wait_ge(s_mod_ev, {4: 1, 6: 2, 10: 3, 12: 4}[k])

            def make_a(l):
                ts(hA[l], modc[l][:, 8:16], 1.0, ALU.add)
                v.tensor_tensor(hA[l], hA[l], ng[l].unsqueeze(2).broadcast_to([P, KT, 2]), ALU.mult).then_inc(s_mod_ok, 1)
                dve.wait_ge(s_mod_ok, l + 1)

            mod_evac(0, 4, 0, 16)
            make_a(0)
            dve.wait_ge(s_h_ev, 24)
            for q, (t0, nt) in enumerate(CHUNKS):
                ci = 1 if q == 0 else 0
                for k in range(1, KT, 2):
                    v.tensor_scalar(hT0[:, k, t0:t0 + nt], hT0[:, k, t0:t0 + nt], hA[0][:, k, ci:ci + 1],
                                    modc[0][:, k, ci:ci + 1], ALU.mult, ALU.add).then_inc(s_h_evd, 1)

            def build_cl(half):
                if half:
                    dve.wait_ge(s_cop_out, 16 * 8)
                    dve.wait_ge(s_k_mm, 4)
                for q in range(4):
                    g4 = slice(4 * q, 4 * q + 4)
                    a4 = slice(16 * half + 4 * q, 16 * half + 4 * q + 4)
                    L = [LPc[:, :, r, a4].rearrange("p k g -> p g k").unsqueeze(3).broadcast_to([P, 4, 9, HC])
                         for r in range(2)]
                    C_ = [Cx[:, r, a4, :].unsqueeze(2).broadcast_to([P, 4, 9, HC]) for r in range(2)]
                    tt(CL[:, 0, g4], C_[0], L[0], ALU.mult)
                    tt(cltmp, C_[1], L[1], ALU.mult)
                    tt(CL[:, 0, g4], CL[:, 0, g4], cltmp, ALU.add)
                    tt(CL[:, 1, g4], C_[1], L[0], ALU.mult)
                    tt(cltmp, C_[0], L[1], ALU.mult)
                    tt(CL[:, 1, g4], CL[:, 1, g4], cltmp, ALU.subtract)
                v.tensor_copy(cltmp[:, 0, 0, :], cltmp[:, 0, 1, :]).then_inc(s_cl_ok, 1)
                dve.wait_ge(s_cl_ok, half + 1)

            def k_evac(half):
                dve.wait_ge(s_ld_ws, 16 * 2)
                if half:
                    dve.wait_ge(s_t_in, 16 * 15)
                for q in range(4):
                    dve.wait_ge(s_k_mm, 4 * half + q + 1)
                    g4 = slice(4 * q, 4 * q + 4)
                    a4 = slice(16 * half + 4 * q, 16 * half + 4 * q + 4)
                    bk = ps[:, q, :].rearrange("p (g k o) -> p g k o", k=CH, o=HC)
                    cp(Kt[32:32 + HC, g4, 0:7], bk[32:32 + HC, :, 0:7])
                    cp(Kt[0:HC, g4], bk[0:HC])
                    tt(ddtmp[0:HC], ident[0:HC, 0:HC].unsqueeze(1).broadcast_to([HC, 4, HC]), dskip[0:HC, a4, :], ALU.mult)
                    v.tensor_tensor(Kt[0:HC, g4, 0], Kt[0:HC, g4, 0], ddtmp[0:HC], ALU.add).then_inc(s_k_ev, 1)
                    dve.wait_ge(s_k_ev, 4 * half + q + 1)

            build_cl(0)
            k_evac(0)
            build_cl(1)
            k_evac(1)
            for t in range(TT):
                dve.wait_ge(s_v_ev, t + 1)
                step(v.bn_stats(bnst, vt[:, t]))
                step(v.bn_aggr(mv[:, t], bnst))
            mod_evac(0, 6, 16, 24)
            ts(msq.unsqueeze(2), mv[:, :, 1:2], EPS, ALU.add)
            v.tensor_copy(ssq, msq).then_inc(s_rt_req, 1)
            dve.wait_ge(s_rt_ok, 1)
            refined(ssq, msq, rstd)
            for t in range(TT):
                v.tensor_scalar(vt[:, t], vt[:, t], mv[:, t, 0:1], rstd[:, t:t + 1], ALU.subtract, ALU.mult).then_inc(s_vn_ok, 1)
            dve.wait_ge(s_bl_tr, 16)
            for j in range(2):
                dve.wait_ge(s_xs_mm, CH + j + 1)
                for q in range(4):
                    v.tensor_copy(Yc[0:CCH, :, 4 * j + q, :],
                                  ps[32 * q:32 * q + 32, 4 + j, :].rearrange("p (g c) -> p g c", c=HC)).then_inc(s_xs_evd, 1)
            mod_evac(1, 10, 0, 16)
            make_a(1)
            dve.wait_ge(s_k_mm, 8)
            dve.wait_ge(s_bl_ok, 4)
            dve.wait_ge(s_ws_tr, 1)
            v.tensor_copy(wsT, ps[:, 5, :].rearrange("p (g q) -> p g q", g=4)).then_inc(s_ws_ev, 1)
            v.tensor_copy(rt[:, 0:1], L8[:, 0:1]).then_inc(s_par_dead, 1)
            dve.wait_ge(s_cop_out, 16 * 16)
            dve.wait_ge(s_t_in, 16 * 30)
            dve.wait_ge(s_vg_ok, TT)
            v.memset(H[:, 0], 0.0).then_inc(s_b_evb, 1)
            for j in range(32):
                q, r = divmod(j, 2)
                dve.wait_ge(s_b_mm, j + 1)
                src = ps[NS:P, j % 4, 0:2 * NCH].rearrange("p (g n) -> p g n", n=NCH)
                v.tensor_copy(H[NS:P, CCH:0:-1, r, 2 * q:2 * q + 2].rearrange("p n g -> p g n"),
                              src[:, :, 0:CCH]).then_inc(s_b_evb, 1)
                v.tensor_copy(H[NS:P, NCH:CCH:-1, r, 2 * q:2 * q + 2].rearrange("p n g -> p g n"),
                              src[:, :, CCH:NCH]).then_inc(s_b_evb, 1)
            dve.wait_ge(s_b_evb, 65)
            dve.wait_ge(s_b_evf, 32)
            Hf = H.rearrange("p i r g -> p i (r g)")
            LR, LI = L8[:, 0:64], L8[:, 64:128].rearrange("p (r g) -> p r g", r=2)
            m0, m1 = rt[:, 0:64], rt[:, 64:128]
            UNR = 4
            with dve.Fori(0, NCH // UNR) as it:
                for k in range(UNR):
                    i = it * UNR + k
                    v.tensor_tensor(m0, Hf[:, i, :], LR, ALU.mult).then_inc(s_rec, 1)
                    v.tensor_tensor(m1.rearrange("p (r g) -> p r g", r=2)[:, ::-1, :], H[:, i, :, :], LI, ALU.mult).then_inc(s_rec, 1)
                    dve.wait_ge(s_rec, i * 4 + 1)
                    v.tensor_tensor(Hf[:, i + 1, :], Hf[:, i + 1, :], m0, ALU.add).then_inc(s_rec, 1)
                    dve.wait_ge(s_rec, i * 4 + 3)
                    v.tensor_tensor(Hf[:, i + 1, :], Hf[:, i + 1, :], m1, ALU.add).then_inc(s_rec, 1)
                    dve.wait_ge(s_rec, i * 4 + 4)
            v.tensor_copy(rt[:, 0:1], rt[:, 1:2]).then_inc(s_rec_ok, 1)
            dve.wait_ge(s_f_mm, 36)
            dve.wait_ge(s_rec_ok, 1)
            for r in range(2):
                v.tensor_copy(Hn[NS:P, r, :, 0:CCH], H[NS:P, CCH - 1::-1, r, :].rearrange("p n g -> p g n")).then_inc(s_hn_b, 1)
                v.tensor_copy(Hn[NS:P, r, :, CCH:NCH], H[NS:P, NCH - 1:CCH - 1:-1, r, :].rearrange("p n g -> p g n")).then_inc(s_hn_b, 1)
            dve.wait_ge(s_ld_bs, 16)
            dve.wait_ge(s_ga_ok, 12)
            for t in range(TT):
                dve.wait_ge(s_gm_mm, t + 1)
                pb = ps[:, 4 + t % 2, :]
                tt(pb, pb, bsb, ALU.add)
                v.tensor_tensor(mixT[:, 0:FB, t * P:(t + 1) * P], mixT[:, 0:FB, t * P:(t + 1) * P],
                                pb.rearrange("p (g q) -> p g q", g=FB), ALU.mult).then_inc(s_gm_ok, 1)
            mod_evac(1, 12, 16, 24)
            for j in range(8):
                dve.wait_ge(s_y1_tr, 2 * j + 2)
                v.tensor_copy(Ytc[0:CCH, :, 64 * j:64 * j + 64].rearrange("p s (g o) -> p g s o", o=HC),
                              ps[0:CCH, 2 * (j % 2) + 1, :].rearrange("p (g s o) -> p g s o", g=4, o=HC)).then_inc(s_y1_evd, 1)
            for j in range(4):
                dve.wait_ge(s_y2_tr, 8 + j + 1)
                v.tensor_copy(yT[:, j, 0:NCTX].rearrange("p (n s) -> p s n", s=CH),
                              ps[:, 4 + j, 0:NCTX].rearrange("p (s n) -> p s n", s=CH)).then_inc(s_y2_evd, 1)
            for j in range(12):
                fb, q = divmod(j, 3)
                t0, nt = CHUNKS[q]
                dve.wait_ge(s_glu_sg, j + 1)
                pb, m = ps[:, j % 4, 0:nt], mixT[:, FB + fb, t0:t0 + nt]
                tt(pb, pb, yT[:, fb, t0:t0 + nt], ALU.mult)
                v.tensor_tensor(m, m, pb, ALU.mult).then_inc(s_glu_ok, 1)
            def x1_norm(t):
                if CT <= t < 4:
                    dve.wait_ge(s_x1[(t - CT) // 2], 16)
                v.tensor_scalar(xn[t], x1[:, t], rstd[:, t:t + 1], None, ALU.mult).then_inc(s_xn1, 1)

            def x1_rstd(c):
                row_rstd(c)
                v.tensor_copy(small[:, 299:300], small[:, 0:1]).then_inc(s_rs0, 1)

            def h1_full(q, k):
                t0, nt = CHUNKS[q]
                ci = 1 if q == 0 else 0
                j = KT * q + k
                dve.wait_ge(s_h1_tr, j + 1)
                v.tensor_scalar(mixT[:, k, t0:t0 + nt], ps[:, j % 4, 0:nt], hA[1][:, k, ci:ci + 1],
                                modc[1][:, k, ci:ci + 1], ALU.mult, ALU.add).then_inc(s_h1_t, 1)

            for j in range(4 * TT):
                q, t = divmod(j, TT)
                dve.wait_ge(s_o_mm, j + 1)
                if j >= 2:
                    dve.wait_ge(s_o_ok, j - 1)
                v.tensor_tensor(otmp[:, j % 2], ps[:, 4 + j % 4, 0:QC],
                                gtb[:, 1 if t < CT else 0, QC * q:QC * q + QC], ALU.mult).then_inc(s_o_t, 1)
                if q == 3 and t == 4:
                    dve.wait_ge(s_rt1, 1)
                    row_rstd(slice(0, 2))
                    x1_norm(0)
                    x1_norm(1)
                if q == 3 and t == 7:
                    for k in range(KT):
                        h1_full(0, k)
                if q == 3 and t == 8:
                    dve.wait_ge(s_rt1, 2)
                    x1_rstd(slice(2, 6))
                    x1_norm(2)
                    x1_norm(4)
            for k in range(6):
                h1_full(1, k)
            dve.wait_ge(s_rt1, 3)
            x1_rstd(slice(6, 10))
            for k in range(2):
                x1_norm(6 + 2 * k)
                h1_full(1, 6 + k)
            for k in range(KT):
                h1_full(2, k)
            dve.wait_ge(s_ld_gain, 16 * 2)
            ts(L8[:], L8[:], HD ** -0.5, ALU.mult)

            def gained(q, nh, r, gain):
                qv = q.rearrange("p (h d) -> p h d", d=HD)
                tt(qv, qv, r.unsqueeze(2).broadcast_to([P, nh, HD]), ALU.mult)
                tt(qv, qv, gain.unsqueeze(1).broadcast_to([P, nh, HD]), ALU.mult)

            def rope(q, t, done):
                q4 = q.rearrange("p (h a b m) -> p h a b m", h=2, a=2, b=2)
                co, si = (cs[:, k, t].rearrange("p (a m) -> p a m", a=2).unsqueeze(1).broadcast_to([P, 2, 2, 32])
                          for k in range(2))
                t_ = [rope_t[k][:, 0:128].rearrange("p (h a m) -> p h a m", h=2, a=2) for k in range(2)]
                x1_, x2_ = q4[:, :, :, 0], q4[:, :, :, 1]
                tt(t_[0], x1_, si, ALU.mult)
                tt(t_[1], x2_, si, ALU.mult)
                tt(x1_, x1_, co, ALU.mult)
                tt(x1_, x1_, t_[1], ALU.subtract)
                tt(x2_, x2_, co, ALU.mult)
                v.tensor_tensor(x2_, x2_, t_[0], ALU.add).then_inc(done, 1)

            def head_rstd(b, c0, n):
                cols = slice(c0, c0 + n)
                dve.wait_ge(s_hd_rt, b)
                ts(qms[:, cols], qss[:, cols], 1.0 / HD, ALU.mult, EPS, ALU.add)
                refined(qss[:, cols], qms[:, cols], qrs[:, cols])

            dve.wait_ge(s_ld_tab, 16 * 2)
            dve.wait_ge(s_kv_ev, TT)
            head_rstd(1, 64, 20)
            for t in range(TT):
                gained(Kraw[:, t], NKV, qrs[:, 64 + 2 * t:66 + 2 * t], rt[:])
                if t >= CT:
                    rope(Kraw[:, t], t - CT, s_k_ok)
                    dve.wait_ge(s_k_ok, t - CT + 1)
            for j in range(4 * LT):
                q, t = divmod(j, LT)
                if t == 0:
                    dve.wait_ge(s_q_ev, j + LT)
                    head_rstd(2 + q, 16 * q, 16)
                qh = Qt[:, t, QC * q:QC * q + QC]
                gained(qh, 2, qrs[:, 2 * j:2 * j + 2], L8[:])
                rope(qh, t, s_q_ok)
                dve.wait_ge(s_q_ok, j + 1)
                if j == LT - 1:
                    for k in range(6):
                        dve.wait_ge(s_kt_hi, k + 1)
                        h_, q_ = divmod(k, 3)
                        nt = 256 if q_ == 2 else 512
                        cols = slice(512 * q_, 512 * q_ + nt)
                        v.tensor_tensor(KTl[:, h_, cols], ps[:, 4 + k % 4, 0:nt], KTh[:, h_, cols].bitcast(F32),
                                        ALU.subtract).then_inc(s_kt_lo, 1)
                    v.memset(ones, 1.0).then_inc(s_ones, 1)
                    dve.wait_ge(s_ones, 1)
                    v.tensor_copy(ones_r[:], ones).then_inc(s_ones, 1)

            def q_rest(i):
                dve.wait_ge(s_a_qh, i + 1)
                v.tensor_tensor(qTl[:, i % 2], ps[:, 7, :].rearrange("p (h q) -> p h q", q=P),
                                qTh[:, i % 2].bitcast(F32), ALU.subtract).then_inc(s_a_ql, 1)

            def row_max(i, h):
                dve.wait_ge(s_a_mx, HPK * i + h + 1)
                v.tensor_reduce(smax[:, i % 2, h:h + 1], ps[:, 0:3, :].rearrange("p b n -> p (b n)")[:, 0:TOK],
                                AX.X, ALU.max).then_inc(s_a_max, 1)

            def neg_max(i):
                dve.wait_ge(s_a_nt, i + 1)
                v.scalar_tensor_tensor(out=nm[0:HPK, i % 2].rearrange("p (h q) -> p h q", q=P),
                                       in0=ps[0:HPK, 2, 256:256 + P].unsqueeze(1).broadcast_to([HPK, HPK, P]), scalar=-1.0,
                                       in1=ident[0:HPK, 0:HPK].unsqueeze(2).broadcast_to([HPK, HPK, P]),
                                       op0=ALU.mult, op1=ALU.mult).then_inc(s_a_nm, 1)

            def gate_over_sums(i):
                dve.wait_ge(s_gate_in[i % 2], 16 * (i // 2 + 1))
                if i:
                    dve.wait_ge(s_a_o, i)
                dve.wait_ge(s_a_rt, i + 1)
                v.tensor_tensor(GR, gbuf[:, i % 2], ps[:, 7, :], ALU.mult).then_inc(s_a_gr, 1)

            def sums_inverse(i):
                dve.wait_ge(s_a_sm, i + 1)
                v.reciprocal(rinv, ps[:, 7, 0:HPK]).then_inc(s_a_ri, 1)

            def output(i):
                b, kv = divmod(i, 2)
                dve.wait_ge(s_a_pv, i + 1)
                dve.wait_ge(s_a_gr, i + 1)
                v.tensor_tensor(OT[:, b, HPK * kv:HPK * kv + HPK, :], GR.rearrange("p (h q) -> p h q", q=P),
                                ps[:, 5 + i % 2, :].rearrange("p (h q) -> p h q", q=P), ALU.mult).then_inc(s_a_o, 1)

            q_rest(0)
            q_rest(1)
            for h in range(HPK):
                row_max(0, h)
            neg_max(0)
            dve.wait_ge(s_v_hi, 1)
            v.tensor_tensor(Vl, Vt, Vh.bitcast(F32), ALU.subtract).then_inc(s_v_lo, 1)
            for m in range(TT * 2 * LT + 1):
                i, t = divmod(m, TT)
                if m and (m - 1) % TT not in on_pool:
                    dve.wait_ge(s_a_ph, m)
                    v.tensor_tensor(p_lo[:, (m - 1) % NP], PF[(m - 1) % NP], p_hi[:, (m - 1) % NP].bitcast(F32),
                                    ALU.subtract).then_inc(s_a_pld, 1)
                if i + 1 < 2 * LT and t % 2 == 0 and t < 8:
                    row_max(i + 1, t // 2)
                if i and t == 5:
                    sums_inverse(i - 1)
                if i and t == 7:
                    gate_over_sums(i - 1)
                    output(i - 1)
                if i + 1 < 2 * LT and t == 8:
                    neg_max(i + 1)
                if i + 2 < 2 * LT and t == 9:
                    q_rest(i + 2)
            sums_inverse(2 * LT - 1)
            gate_over_sums(2 * LT - 1)
            output(2 * LT - 1)
            dve.wait_ge(s_ld_fin, 16)
            for j in range(4 * LT + 1):
                q, t = divmod(j, LT)
                if q < 4:
                    dve.wait_ge(s_z_mm, j + 1)
                    if j >= 8:
                        dve.wait_ge(s_z_ok, j - 7)
                    v.tensor_tensor(zt[:, j % 8], ps[:, j % 4, 0:QC], gtb[:, 0, QC * q:QC * q + QC], ALU.mult).then_inc(s_z_t, 1)
                if j > 3 * LT:
                    t = j - 3 * LT - 1
                    dve.wait_ge(s_fin_rt, t + 1)
                    row_rstd(slice(t, t + 1))
                    v.scalar_tensor_tensor(out=xr[:, t], in0=xr[:, t], scalar=rstd[:, t:t + 1], in1=fgb,
                                           op0=ALU.mult, op1=ALU.mult).then_inc(s_fin_g, 1)

        @block.tensor
        def _(pe):
            te = nc.tensor

            def arrived(kind, b):
                u = (kind, b)
                pe.wait_ge(w_in[place[u][0]], 16 * (place[u][1] + 1))
                return u

            def tr(o, i):
                m = i.shape[0]
                return te.transpose(o, i, ident[0:m, 0:m])

            pe.wait_ge(s_ld_const, 16 * 8)
            tr(ps[:, 6, 0:NCOL], colrow[0:NCOL]).then_inc(s_par_tr, 1)
            pe.wait_ge(s_ld_par, 16 * 7)
            pe.wait_ge(s_lraw_ok, 1)
            for k in range(3):
                last = tr(ps[:, 7, 32 * k:32 * k + 32], lraw[0:G, k])
            last.then_inc(s_par_tr, 1)
            for r in range(2):
                for q in range(4):
                    last = tr(ps[:, 4 + r, P * q:P * q + P], craw[:, r, q])
                last.then_inc(s_par_tr, 1)

            def mod_rows(m):
                u = arrived(*M[m])
                if m:
                    pe.wait_ge(s_mod_row, m)
                for k in range(KT):
                    last = te.matmul(ps[0:2, 6, :], cond[:, k], slot_kn(u)[:, k], start=k == 0, stop=k == KT - 1)
                last.then_inc(s_mod_mm, 1)

            def mod_cols(m):
                l, b = divmod(m, 6)
                pe.wait_ge(s_mod_row, m + 1)
                if m in (4, 6, 10):
                    pe.wait_ge(s_mod_ev, {4: 1, 6: 2, 10: 3}[m])
                for f in range(4):
                    o = 64 * l + 2 * (4 * b + f)
                    last = tr(ps[:, 7, o:o + 2], slot(M[m])[0:2, P * f:P * f + P])
                last.then_inc(s_mod_tr, 1)

            pe.wait_ge(s_cond_ok, 1)
            pe.wait_ge(s_lam_ok, 3)

            def to_features(q, Xr, x_ok, tr_done, readers):
                t0, nt = CHUNKS[q]
                for k in range(KT):
                    j = KT * q + k
                    if j >= 4:
                        readers(j - 4)
                    for t in range(nt // P):
                        if k == 0:
                            pe.wait_ge(*x_ok(t0 // P + t))
                        last = tr(ps[:, j % 4, t * P:t * P + P], Xr[t0 // P + t][:, P * k:P * k + P])
                    last.then_inc(tr_done, 1)

            def h0_readers(j):
                pe.wait_ge(s_h_ev, j + 1)

            def x0_ok(t):
                return (s_xnp, (t + 1) // 2) if t % 2 else (s_xna, t // 2 + 1)

            def x1_ok(t):
                if t >= 3 and t % 2:
                    return s_xna, TT // 2 + (t - 1) // 2
                return s_xn1, t + 1 if t < 3 else t // 2 + 2

            def h1_readers(j):
                pe.wait_ge(s_h1_t, j + 1)

            for m in range(2):
                mod_rows(m)
                mod_cols(m)
            for q in range(3):
                to_features(q, [X[:, t] for t in range(TT)], x0_ok, s_h_tr, h0_readers)
                if q < 2:
                    mod_rows(q + 2)
                    mod_cols(q + 2)
            pe.wait_ge(s_h_ev, 24)

            def token_major(u, bank, lhs, signal):
                for k in range(KT):
                    last = te.matmul(ps[:, bank, :], lhs(k), slot_kn(u)[:, k], start=k == 0, stop=k == KT - 1)
                last.then_inc(signal, 1)

            def lags(half):
                pe.wait_ge(s_cl_ok, half + 1)
                if half:
                    pe.wait_ge(s_k_ev, 4)
                    pe.wait_ge(s_bl_ev, 16)
                for q in range(4):
                    for m in range(4):
                        gl, g = 4 * q + m, 16 * half + 4 * q + m
                        base = P * m
                        for r in range(2):
                            te.matmul(ps[0:HC, q, base:base + HC], BB[:, r, g], Cx[:, r, g], start=r == 0, stop=r == 1)
                        for d in range(2):
                            rows, o = slice(d * NS, (d + 1) * NS), base + (HC if d == 0 else 0)
                            for r in range(2):
                                last = te.matmul(ps[32 * d:32 * d + HC, q, o:o + 7 * HC], BB[rows, r, g],
                                                 CL[rows, r, gl, 1:8].rearrange("p k o -> p (k o)"), start=r == 0, stop=r == 1)
                    last.then_inc(s_k_mm, 1)

            def bop_transposes(j):
                q, r = divmod(j, 2)
                pe.wait_ge(s_bl_ok, q // 2 + 1)
                if j >= 4:
                    pe.wait_ge(s_bl_ev, j - 3)
                else:
                    pe.wait_ge(s_k_ev, j + 1)
                for m in range(4):
                    last = tr(ps[:, j % 4, P * m:P * m + P], BL[:, r, 4 * q + m].rearrange("p s h -> p (s h)"))
                last.then_inc(s_bl_tr, 1)

            def between_tiles(work):
                for kind, i in work:
                    if kind == "rows":
                        mod_rows(i)
                    if kind == "cols":
                        mod_cols(i)
                    if kind == "lags":
                        lags(i)
                    if kind == "bop":
                        for j in range(i, i + 4):
                            bop_transposes(j)

            pe.wait_ge(s_par_ok, 1)
            u = arrived("v", 0)
            for t in range(TT):
                if t in (0, 2, 6):
                    pe.wait_ge(s_h_eva, {0: 4, 2: 8, 6: 12}[t])
                    pe.wait_ge(s_h_evd, {0: 4, 2: 8, 6: 12}[t])
                if t >= 2:
                    pe.wait_ge(s_v_ev, t - 1)
                token_major(u, 4 + t % 2, lambda k: hT0[:, k, t * P:t * P + P], s_v_mm)
                between_tiles(after_v.get(t, ()))
            u = arrived("xs", 0)
            pe.wait_ge(s_v_ev, TT)
            for s in range(CH):
                if s >= 2:
                    pe.wait_ge(s_xs_eva, s - 1)
                token_major(u, 4 + s % 2, lambda k: hT0[:, k, NCTX + s:TOK:CH], s_xs_mm)
                between_tiles(after_xs.get(s, ()))
            pe.wait_ge(s_hperm_ok, 1)
            for j in range(2):
                pe.wait_ge(s_xs_eva, 7 + j)
                token_major(u, 4 + j, lambda k: hperm[:, k, P * j:P * j + P], s_xs_mm)
            pe.wait_ge(s_xs_evd, 8)
            pe.wait_ge(s_ld_ws, 32)
            for g in range(4):
                last = tr(ps[:, 5, P * g:P * g + P], wsraw[:, g])
            last.then_inc(s_ws_tr, 1)
            pe.wait_ge(s_k_ev, 8)
            for j in range(11):
                if j >= 4:
                    pe.wait_ge(s_u_ev, j - 3)
                for m in range(min(3, G - 3 * j)):
                    g = 3 * j + m
                    tr(ps[:, j % 4, NCH * m:NCH * m + CCH], Yc[0:CCH, g].rearrange("p s c -> p (s c)"))
                    last = tr(ps[:, j % 4, NCH * m + CCH:NCH * (m + 1)], Yl[:, g].rearrange("p s c -> p (s c)"))
                last.then_inc(s_u_tr, 1)
            pe.wait_ge(s_u_ev, 11)
            for j in range(32):
                q, r = divmod(j, 2)
                u = arrived("bop", q // 8)
                op = slot(u).rearrange("p (r g m) -> p r g m", r=2, m=P)
                if j >= 4:
                    pe.wait_ge(s_b_evf, j - 3)
                    pe.wait_ge(s_b_evb, 2 * (j - 3) + 1)
                for m in range(2):
                    last = te.matmul(ps[:, j % 4, NCH * m:NCH * (m + 1)], op[:, r, (2 * q + m) % 16], U[:, 2 * q + m],
                                     start=True, stop=True)
                last.then_inc(s_b_mm, 1)

            def gt_rows(l, c, bank, signal):
                for half in range(2):
                    for m in range(4):
                        k = 16 + 4 * half + m
                        last = tr(ps[:, bank + half, P * m:P * m + P], modc[l][:, k, c:c + 1].broadcast_to([P, P]))
                    last.then_inc(signal, 1)

            pe.wait_ge(s_par_dead, 1)
            pe.wait_ge(s_mod_ev, 3)
            gt_rows(0, 0, 4, s_gt_tr)
            gt_rows(0, 1, 6, s_gt_tr)
            pe.wait_ge(s_b_evf, 32)
            pe.wait_ge(s_b_evb, 65)
            for part, kind in enumerate(("u", "ga", "gb")):
                u = arrived(kind, 0)
                for fb in range(FB):
                    for q, (t0, nt) in enumerate(CHUNKS):
                        j = 12 * part + 3 * fb + q
                        if j >= 4:
                            pe.wait_ge(s_f_ev, j - 3)
                        for k in range(KT):
                            last = te.matmul(ps[:, j % 4, 0:nt], slot_kn(u)[:, k, P * fb:P * fb + P], hT0[:, k, t0:t0 + nt],
                                             start=k == 0, stop=k == KT - 1)
                        last.then_inc(s_f_mm, 1)
            for m in (10, 11):
                mod_rows(m)
            for m in (10, 11):
                mod_cols(m)
            pe.wait_ge(s_gt_ev, 4)
            pe.wait_ge(s_vg_ok, TT)
            pe.wait_ge(s_ws_ev, 1)
            for t in range(TT):
                if t >= 2:
                    pe.wait_ge(s_gm_ok, t - 1)
                for g in range(FB):
                    last = te.matmul(ps[:, 4 + t % 2, P * g:P * g + P], vt[:, t, P * g:P * g + P], wsT[:, g], start=True, stop=True)
                last.then_inc(s_gm_mm, 1)
            pe.wait_ge(s_f_ev, 36)
            pe.wait_ge(s_gm_ok, TT)
            pe.wait_ge(s_hn_f, 2)
            pe.wait_ge(s_hn_b, 4)
            pe.wait_ge(s_mod_ev, 4)
            for j in range(16):
                u = arrived("ct", j // 4)
                op = slot(u)[:, 0:3072].rearrange("p (r g m) -> p r g m", r=3, m=P)
                if j >= 4:
                    pe.wait_ge(s_c_ev, j - 3)
                for m in range(2):
                    g, gl = 2 * j + m, (2 * j + m) % 8
                    o = ps[:, 4 + j % 4, NCH * m:NCH * (m + 1)]
                    te.matmul(o, op[:, 2, gl], U[:, g], start=True, stop=False)
                    te.matmul(o, op[:, 0, gl], Hn[:, 0, g], start=False, stop=False)
                    last = te.matmul(o, op[:, 1, gl], Hn[:, 1, g], start=False, stop=True)
                last.then_inc(s_c_mm, 1)
            pe.wait_ge(s_mod_ok, 2)
            pe.wait_ge(s_c_ev, 16)
            for j in range(8):
                if j >= 2:
                    pe.wait_ge(s_y1_eva, j - 1)
                    pe.wait_ge(s_y1_evd, j - 1)
                bk = 2 * (j % 2)
                for m in range(4):
                    last = tr(ps[:, bk, P * m:P * m + P], ys[:, 4 * j + m, CCH:NCH])
                last.then_inc(s_y1_tr, 1)
                for m in range(4):
                    last = tr(ps[0:CCH, bk + 1, P * m:P * m + P], ys[:, 4 * j + m, 0:CCH])
                last.then_inc(s_y1_tr, 1)
            pe.wait_ge(s_y1_eva, 8)
            pe.wait_ge(s_y1_evd, 8)
            for j in range(8):
                fb, q = divmod(j, 2)
                if j >= 4:
                    pe.wait_ge(s_y2_eva, j - 3)
                for m in range(4):
                    last = tr(ps[:, 4 + j % 4, P * m:P * m + P], Yt[:, 4 * q + m, P * fb:P * fb + P])
                last.then_inc(s_y2_tr, 1)
            for j in range(4):
                pe.wait_ge(s_y2_eva, 5 + j)
                for s in range(CH):
                    last = tr(ps[:, 4 + j, CCH * s:CCH * s + CCH], Ytc[0:CCH, s, P * j:P * j + P])
                last.then_inc(s_y2_tr, 1)
            u = arrived("glu", 0)
            wg = slot(u)[:, 0:2048].rearrange("p (k n) -> p k n", n=512)
            pe.wait_ge(s_y2_eva, 8)
            pe.wait_ge(s_y2_evd, 4)
            for j in range(12):
                fb, q = divmod(j, 3)
                t0, nt = CHUNKS[q]
                if j >= 4:
                    pe.wait_ge(s_glu_ok, j - 3)
                for k in range(FB):
                    last = te.matmul(ps[:, j % 4, 0:nt], wg[:, k, P * fb:P * fb + P], yT[:, k, t0:t0 + nt],
                                     start=k == 0, stop=k == FB - 1)
                last.then_inc(s_glu_mm, 1)
            def split_of(u):
                pe.wait_ge(s_w_lo, splits.index(u) + 1)
                return slot_parts(u)

            def token_major_split(weights, bank, tokens, signal):
                wh, wl = weights
                for k in range(KT):
                    th, tl = tokens(k)
                    te.matmul(ps[:, bank, 0:QC], th, wh[:, k], start=k == 0, stop=False)
                    te.matmul(ps[:, bank, 0:QC], th, wl[:, k], start=False, stop=False)
                    last = te.matmul(ps[:, bank, 0:QC], tl, wh[:, k], start=False, stop=k == KT - 1)
                last.then_inc(signal, 1)

            x1n = (xn, x1_ok, s_h1_tr, h1_readers)
            for q in range(4):
                ws = split_of(("out0", q))
                for t in range(TT):
                    j = TT * q + t
                    if j >= 4:
                        pe.wait_ge(s_o_t, j - 3)
                    if j in (0, CT, 6):
                        pe.wait_ge(s_mix_lo, {0: 11, CT: 12, 6: 13}[j])
                    token_major_split(ws, 4 + j % 4, lambda k: [z[:, k, t * P:t * P + P] for z in (hi, lo)], s_o_mm)
                    if q == 3 and t == 7:
                        to_features(0, *x1n)
            to_features(1, *x1n)
            to_features(2, *x1n)

            pe.wait_ge(s_o_t, 4 * TT)
            for j in range(2 * TT):
                part, t = divmod(j, TT)
                if t == 0:
                    ws = split_of(("kv", part))
                if j in (0, 2, 6):
                    pe.wait_ge(s_h1_lo, {0: 8, 2: 16, 6: 24}[j])
                if j >= 4:
                    pe.wait_ge(s_kv_ev, j - 3)
                    if j - 4 < TT:
                        pe.wait_ge(s_hd_sq, 2 * (j - 3))
                token_major_split(ws, 4 + j % 4, lambda k: [z[:, k, t * P:t * P + P] for z in (hi, lo)], s_kv_mm)

            def k_transposes():
                pe.wait_ge(s_k_ok, LT)
                pe.wait_ge(s_kv_ev, 2 * TT)
                for j in range(6):
                    h, q = divmod(j, 3)
                    if j >= 4:
                        pe.wait_ge(s_kt_lo, j - 3)
                    for t in range(4 * q, min(4 * q + 4, TT)):
                        last = tr(ps[:, 4 + j % 4, P * (t - 4 * q):P * (t - 4 * q) + P], Kraw[:, t, HD * h:HD * h + HD])
                    last.then_inc(s_kt_tr, 1)
                pe.wait_ge(s_kt_lo, 4)
                gt_rows(1, 0, 6, s_gt_tr)

            for j in range(4 * LT):
                q, t = divmod(j, LT)
                if t == 0:
                    ws = split_of(("q", q))
                if j >= 4:
                    pe.wait_ge(s_q_ev, j - 3)
                    pe.wait_ge(s_hd_sq, 20 + 2 * (j - 3))
                c = NCTX + t * P
                token_major_split(ws, j % 4, lambda k: [z[:, k, c:c + P] for z in (hi, lo)], s_q_mm)
                if j == 18:
                    k_transposes()
            pe.wait_ge(s_q_ev, 4 * LT)
            pe.wait_ge(s_hd_sq, 20 + 8 * LT)
            def q_transposes(i):
                if i:
                    pe.wait_ge(s_a_qh, i)
                    pe.wait_ge(s_a_ql, i)
                if i >= 3:
                    pe.wait_ge(s_a_gr, i - 2)
                for h in range(HPK):
                    c = HD * (HPK * (i % 2) + h)
                    last = tr(ps[:, 7, P * h:P * h + P], Qt[:, i // 2, c:c + HD])
                last.then_inc(s_a_qT, 1)

            def max_scores(i, h):
                if h == 0:
                    pe.wait_ge(s_a_qh, i + 1)
                if i or h:
                    pe.wait_ge(s_a_max, HPK * i + h)
                for b, (t0, nt) in enumerate(((0, 512), (512, 512), (1024, 256))):
                    last = te.matmul(ps[:, b, 0:nt], qTh[:, i % 2, h], KTh[:, i % 2, t0:t0 + nt], start=True, stop=True)
                last.then_inc(s_a_mx, 1)

            def max_rows(i):
                pe.wait_ge(s_a_max, HPK * (i + 1))
                tr(ps[0:HPK, 2, 256:256 + P], smax[:, i % 2]).then_inc(s_a_nt, 1)

            def scores(i, t):
                m = TT * i + t
                if t == 0:
                    pe.wait_ge(s_a_nm, i + 1)
                    pe.wait_ge(s_a_ql, i + 1)
                if m >= 2:
                    pe.wait_ge(s_a_p, m - 1)
                o = ps[:, 3 + m % 2, :]
                kh, kl = (q[:, i % 2, P * t:P * t + P] for q in (KTh, KTl))
                qh, ql = (q[:, i % 2].rearrange("p h q -> p (h q)") for q in (qTh, qTl))
                te.matmul(o, ones_r[0:HPK, :], nm[0:HPK, i % 2], start=True, stop=False)
                te.matmul(o, kh, qh, start=False, stop=False)
                te.matmul(o, kh, ql, start=False, stop=False)
                te.matmul(o, kl, qh, start=False, stop=True).then_inc(s_a_s, 1)

            def values(m):
                i, t = divmod(m, TT)
                pe.wait_ge(*p_rest_done(m))
                if m == 0:
                    pe.wait_ge(s_v_lo, 1)
                if t == 0 and i >= 2:
                    pe.wait_ge(s_a_o, i - 1)
                o, hd = ps[:, 5 + i % 2, :], slice(HD * (i % 2), HD * (i % 2) + HD)
                te.matmul(o, Vh[:, t, hd], p_hi[:, m % NP], start=t == 0, stop=False)
                te.matmul(o, Vh[:, t, hd], p_lo[:, m % NP], start=False, stop=False)
                mm = te.matmul(o, Vl[:, t, hd], p_hi[:, m % NP], start=False, stop=t == TT - 1)
                if t == TT - 1:
                    mm.then_inc(s_a_pv, 1)

            def row_sums(i):
                pe.wait_ge(s_a_sum, 9 * (i + 1))
                pe.wait_ge(s_a_qh, min(i + 3, 2 * LT))
                pe.wait_ge(s_a_ql, min(i + 3, 2 * LT))
                for h in range(HPK):
                    last = te.matmul(ps[:, 7, h:h + 1], psum_p[:, i % 2, P * h:P * h + P], onec, start=True, stop=True)
                last.then_inc(s_a_sm, 1)

            def over_sums(i):
                pe.wait_ge(s_a_ri, i + 1)
                for h in range(HPK):
                    last = tr(ps[:, 7, P * h:P * h + P], rinv[:, h:h + 1].broadcast_to([P, P]))
                last.then_inc(s_a_rt, 1)

            pe.wait_ge(s_kt_lo, 6)
            for j in range(2 * NH):
                h, half = divmod(j, 2)
                if j % 4 == 0:
                    wh, wl = split_of(("gate", j // 4))
                if j >= 2:
                    pe.wait_ge(s_g_ev, j - 1)
                fs, cols = slice(P * (h % 2), P * (h % 2) + P), slice(NCTX + 512 * half, NCTX + 512 * half + 512)
                for k in range(KT):
                    te.matmul(ps[:, 3 + j % 2, :], wh[:, k, fs], hi[:, k, cols], start=k == 0, stop=False)
                    te.matmul(ps[:, 3 + j % 2, :], wh[:, k, fs], lo[:, k, cols], start=False, stop=False)
                    last = te.matmul(ps[:, 3 + j % 2, :], wl[:, k, fs], hi[:, k, cols], start=False, stop=k == KT - 1)
                last.then_inc(s_g_mm, 1)
                if j == 11:
                    pe.wait_ge(s_gt_ev, 6)
                    pe.wait_ge(s_ones, 2)
                    pe.wait_ge(s_q_ok, 4 * LT)
                    q_transposes(0)
                if j >= 12:
                    max_scores(0, j - 12)
                if j == 12:
                    q_transposes(1)
            max_rows(0)
            pe.wait_ge(s_g_ev, 2 * NH)
            for m in range(TT * 2 * LT + LAG):
                i, t = divmod(m, TT)
                if m >= LAG:
                    values(m - LAG)
                if i < 2 * LT:
                    scores(i, t)
                if i < 2 * LT and i and t == 4:
                    row_sums(i - 1)
                if i < 2 * LT and i and t == 6:
                    over_sums(i - 1)
                if i + 1 < 2 * LT:
                    if t % 2 == 0 and t < 8:
                        max_scores(i + 1, t // 2)
                    if t == 8:
                        max_rows(i + 1)
                if i + 2 < 2 * LT and t == 9:
                    q_transposes(i + 2)
            row_sums(2 * LT - 1)
            over_sums(2 * LT - 1)
            for q in range(4):
                ws = split_of(("out1", q))
                for t in range(LT):
                    j = LT * q + t
                    if q == 0:
                        pe.wait_ge(s_a_ol, 2 * (t + 1))
                    if j >= 4:
                        pe.wait_ge(s_z_t, j - 3)
                    token_major_split(ws, j % 4, lambda k: (OTh[t][:, k], OTl[:, t, k]), s_z_mm)


_ROPE = (np.arange(SEQ)[:, None] // 64, np.arange(SEQ)[:, None] % 64)


def kernel(**inputs):
    import concourse.bacc as bacc
    from concourse.bass_utils import run_bass_kernel_spmd

    nc = bacc.Bacc("TRN2", target_bir_lowering=False, num_devices=1, dynamic_dma_scratch_size=64)
    arrays, args = {}, []

    def declare(name, a):
        arrays[name] = a
        args.append(nc.dram_tensor(name, a.shape, mybir.dt.from_np(a.dtype), kind="ExternalInput").ap())

    names = ["x", "c", "ctx", "c_ctx", "norm_g", "w_mod", "b_mod", "we_in", "we_out", "gm_v_g", "gm_w_s", "gm_b_s",
             "s5_lam_re", "s5_lam_im", "s5_log_dt", "s5_b_re", "s5_b_im", "s5_c_re", "s5_c_im", "s5_d",
             "s5_w_glu", "s5_b_glu", "wo_in", "wo_out", "q_norm_g", "k_norm_g", "final_g"]
    for name in names:
        declare(f"in_{name}", np.ascontiguousarray(inputs[name]))
    freqs = 10000.0 ** (-np.arange(HD // 4, dtype=np.float32) / np.float32(HD // 4))
    ang = np.concatenate([(p.astype(np.float32) * freqs).astype(np.float32) for p in _ROPE], axis=1)
    declare("identity", np.eye(P, dtype=np.float32))
    declare("rope_cos", np.cos(ang).astype(np.float32))
    declare("rope_sin", np.sin(ang).astype(np.float32))
    out = nc.dram_tensor("out", (1, SEQ, D), F32, kind="ExternalOutput").ap()
    build(nc, *args, out)
    r = run_bass_kernel_spmd(nc, [arrays], core_ids=[0])
    return r.results[0]["out"]
```
